# Optimizing a Trainium2 kernel written in Bass

```python
import math
import jax, jax.numpy as jnp
from jax import lax
import numpy as np

D_MODEL = 2048
BATCH = 1
SEQ = 256
DEPTH = 1
DEC_BATCH = 8
DEC_SEQ = 4
PAST_LEN = 2048
PAGE_SIZE = 128

N_MEM = 256
D_MIX = D_MODEL
D_A = D_MIX // 4
D_B = D_MIX // 4
D_C = D_MIX // 2
CONV_A_WIDTH = 31
S5_GROUP = 16
S5_GROUPS = D_B // S5_GROUP
S5_STATE = 64
SSD_HEAD_DIM = 64
SSD_HEADS = D_C // SSD_HEAD_DIM
SSD_GROUPS = 2
SSD_HPG = SSD_HEADS // SSD_GROUPS
SSD_STATE = 128
SSD_CONV_WIDTH = 4
SSD_CHUNK = 128
D_XBC = D_C + 2 * SSD_GROUPS * SSD_STATE
D_IN = 2 * D_A + D_B + D_C + D_XBC + SSD_HEADS
IN_SPLITS = (D_A, 2 * D_A, 2 * D_A + D_B, 2 * D_A + D_B + D_C, 2 * D_A + D_B + D_C + D_XBC)
XA_HEADS = 4
XA_HEAD_DIM = D_MODEL // XA_HEADS
D_FF = 5504
FFN_CONV_WIDTH = 3
EPS = 1e-6

kernel_name = "hymba_style_conv_s5_ssd_hybrid_step"

def _rmsnorm(x, w):
    xf = x.astype(jnp.float32)
    y = xf * lax.rsqrt(jnp.mean(xf * xf, axis=-1, keepdims=True) + EPS)
    return (y * w.astype(jnp.float32)).astype(x.dtype)

def _layernorm(x, w, b):
    xf = x.astype(jnp.float32)
    mu = jnp.mean(xf, axis=-1, keepdims=True)
    xc = xf - mu
    y = xc * lax.rsqrt(jnp.mean(xc * xc, axis=-1, keepdims=True) + EPS)
    return (y * w.astype(jnp.float32) + b.astype(jnp.float32)).astype(x.dtype)

def _causal_dwconv(x, buf, w, b):
    xp = jnp.concatenate([buf.astype(x.dtype), x], axis=1)
    y = lax.conv_general_dilated(xp, w[:, None, :].astype(x.dtype), window_strides=(1,), padding='VALID',
                                 dimension_numbers=('NWC', 'WIO', 'NWC'), feature_group_count=x.shape[-1])
    return y + b.astype(x.dtype), xp[:, -(w.shape[0] - 1):]

def _conformer_conv(v, g, buf, w, b, ln_w, ln_b):
    u = v * jax.nn.sigmoid(g)
    c, new_buf = _causal_dwconv(u, buf, w, b)
    c = _layernorm(c, ln_w, ln_b)
    return jax.nn.silu(c), new_buf

def _complex_affine_combine(c1, c2):
    a1r, a1i, b1r, b1i = c1
    a2r, a2i, b2r, b2i = c2
    return (a1r * a2r - a1i * a2i,
            a1r * a2i + a1i * a2r,
            a2r * b1r - a2i * b1i + b2r,
            a2r * b1i + a2i * b1r + b2i)

def _s5(u, s_re, s_im, lam_re, lam_im, log_dt, b_re, b_im, c_re, c_im, d, glu_w, glu_b):
    f32 = jnp.float32
    bt, L, _ = u.shape
    uf = u.astype(f32)
    ug = uf.reshape(bt, L, S5_GROUPS, S5_GROUP)
    dt = jnp.exp(log_dt.astype(f32))[:, None]
    lr, li = lam_re.astype(f32), lam_im.astype(f32)
    mag = jnp.exp(lr * dt)
    ang = li * dt
    ab_re, ab_im = mag * jnp.cos(ang), mag * jnp.sin(ang)
    den = lr * lr + li * li
    nr, ni = ab_re - 1.0, ab_im
    co_re = (nr * lr + ni * li) / den
    co_im = (ni * lr - nr * li) / den
    br, bi = b_re.astype(f32), b_im.astype(f32)
    bb_re = co_re[..., None] * br - co_im[..., None] * bi
    bb_im = co_re[..., None] * bi + co_im[..., None] * br
    bu_re = jnp.einsum('blgh,gph->blgp', ug, bb_re)
    bu_im = jnp.einsum('blgh,gph->blgp', ug, bb_im)
    sr, si = s_re.astype(f32), s_im.astype(f32)
    bu_re = bu_re.at[:, 0].add(ab_re * sr - ab_im * si)
    bu_im = bu_im.at[:, 0].add(ab_re * si + ab_im * sr)
    a_re = jnp.broadcast_to(ab_re, bu_re.shape)
    a_im = jnp.broadcast_to(ab_im, bu_im.shape)
    _, _, h_re, h_im = lax.associative_scan(_complex_affine_combine, (a_re, a_im, bu_re, bu_im), axis=1)
    y = (jnp.einsum('blgp,ghp->blgh', h_re, c_re.astype(f32))
         - jnp.einsum('blgp,ghp->blgh', h_im, c_im.astype(f32)))
    y = y.reshape(bt, L, D_B) + d.astype(f32) * uf
    y = jax.nn.gelu(y)
    y = y * jax.nn.sigmoid(y @ glu_w.astype(f32) + glu_b.astype(f32))
    return y.astype(u.dtype), h_re[:, -1], h_im[:, -1]

def _ssd_chunked(x, dt, A, Bm, Cm, s0):
    bt, L, G, R, P = x.shape
    N = Bm.shape[-1]
    Q = SSD_CHUNK if L % SSD_CHUNK == 0 else L
    nc = L // Q
    x = x.reshape(bt, nc, Q, G, R, P)
    dt = dt.reshape(bt, nc, Q, G, R)
    Bm = Bm.reshape(bt, nc, Q, G, N)
    Cm = Cm.reshape(bt, nc, Q, G, N)
    a_cs = jnp.cumsum(dt * A, axis=2)
    xdt = x * dt[..., None]
    causal = jnp.tril(jnp.ones((Q, Q), dtype=bool))[:, :, None, None]
    seg = a_cs[:, :, :, None] - a_cs[:, :, None, :]
    decay = jnp.exp(jnp.where(causal, seg, -jnp.inf))
    cb = jnp.einsum('bclgn,bcsgn->bclsg', Cm, Bm)
    y_diag = jnp.einsum('bclsg,bclsgr,bcsgrp->bclgrp', cb, decay, xdt)
    decay_states = jnp.exp(a_cs[:, :, -1:] - a_cs)
    states = jnp.einsum('bcsgn,bcsgr,bcsgrp->bcgrpn', Bm, decay_states, xdt)
    chunk_decay = jnp.exp(a_cs[:, :, -1])

    def step(s, inp):
        dec, st = inp
        return dec[..., None, None] * s + st, s

    final, prev = lax.scan(step, s0, (jnp.moveaxis(chunk_decay, 1, 0), jnp.moveaxis(states, 1, 0)))
    prev = jnp.moveaxis(prev, 0, 1)
    y_off = jnp.einsum('bclgn,bcgrpn,bclgr->bclgrp', Cm, prev, jnp.exp(a_cs))
    return (y_diag + y_off).reshape(bt, L, G, R, P), final

def _mamba2(z, xbc, dt_raw, conv_buf, ssm_state, conv_w, conv_b, dt_bias, a_log, d, norm_w):
    f32 = jnp.float32
    bt, L, _ = z.shape
    xbc_c, new_buf = _causal_dwconv(xbc, conv_buf, conv_w, conv_b)
    xbc_c = jax.nn.silu(xbc_c).astype(f32)
    xs = xbc_c[..., :D_C].reshape(bt, L, SSD_GROUPS, SSD_HPG, SSD_HEAD_DIM)
    Bm = xbc_c[..., D_C:D_C + SSD_GROUPS * SSD_STATE].reshape(bt, L, SSD_GROUPS, SSD_STATE)
    Cm = xbc_c[..., D_C + SSD_GROUPS * SSD_STATE:].reshape(bt, L, SSD_GROUPS, SSD_STATE)
    dt = jax.nn.softplus(dt_raw.astype(f32) + dt_bias.astype(f32)).reshape(bt, L, SSD_GROUPS, SSD_HPG)
    A = -jnp.exp(a_log.astype(f32)).reshape(SSD_GROUPS, SSD_HPG)
    s0 = ssm_state.astype(f32).reshape(bt, SSD_GROUPS, SSD_HPG, SSD_HEAD_DIM, SSD_STATE)
    y, final = _ssd_chunked(xs, dt, A, Bm, Cm, s0)
    y = y + d.astype(f32).reshape(SSD_GROUPS, SSD_HPG)[..., None] * xs
    y = y.reshape(bt, L, D_C) * jax.nn.silu(z.astype(f32))
    yg = y.reshape(bt, L, SSD_GROUPS, D_C // SSD_GROUPS)
    yg = yg * lax.rsqrt(jnp.mean(yg * yg, axis=-1, keepdims=True) + EPS)
    y = yg.reshape(bt, L, D_C) * norm_w.astype(f32)
    return y.astype(z.dtype), new_buf, final.reshape(bt, SSD_HEADS, SSD_HEAD_DIM, SSD_STATE)

def _cross_attention(h, mem_k, mem_v, wq, wo):
    bt, L, _ = h.shape
    q = (h @ wq).reshape(bt, L, XA_HEADS, XA_HEAD_DIM)
    s = jnp.einsum('blhd,bmhd->bhlm', q, mem_k.astype(h.dtype)).astype(jnp.float32) / math.sqrt(XA_HEAD_DIM)
    p = jax.nn.softmax(s, axis=-1).astype(h.dtype)
    o = jnp.einsum('bhlm,bmhd->blhd', p, mem_v.astype(h.dtype)).reshape(bt, L, D_MODEL)
    return o @ wo

def _conv_ffn(h, buf, w_gate, w_up, conv_w, conv_b, w_down):
    g, new_buf = _causal_dwconv(h @ w_gate, buf, conv_w, conv_b)
    return (jax.nn.silu(g) * (h @ w_up)) @ w_down, new_buf

def _layer(x, mem_k, mem_v, conv_a_buf, s5_re, s5_im, conv_c_buf, ssd_state, ffn_buf, p):
    h = _rmsnorm(x, p['norm_mix_w'])
    a_v, a_g, b_u, c_z, c_xbc, c_dt = jnp.split(h @ p['w_in'], IN_SPLITS, axis=-1)
    ya, conv_a_buf = _conformer_conv(a_v, a_g, conv_a_buf, p['conv_a_w'], p['conv_a_b'], p['ln_a_w'], p['ln_a_b'])
    yb, s5_re, s5_im = _s5(b_u, s5_re, s5_im, p['s5_lam_re'], p['s5_lam_im'], p['s5_log_dt'], p['s5_b_re'],
                           p['s5_b_im'], p['s5_c_re'], p['s5_c_im'], p['s5_d'], p['s5_glu_w'], p['s5_glu_b'])
    yc, conv_c_buf, ssd_state = _mamba2(c_z, c_xbc, c_dt, conv_c_buf, ssd_state, p['conv_c_w'], p['conv_c_b'],
                                        p['ssd_dt_bias'], p['ssd_a_log'], p['ssd_d'], p['ssd_norm_w'])
    x = x + jnp.concatenate([ya, yb, yc], axis=-1) @ p['w_out']
    x = x + _cross_attention(_rmsnorm(x, p['norm_xa_w']), mem_k, mem_v, p['xa_wq'], p['xa_wo'])
    f, ffn_buf = _conv_ffn(_rmsnorm(x, p['norm_ffn_w']), ffn_buf, p['ffn_w_gate'], p['ffn_w_up'],
                           p['ffn_conv_w'], p['ffn_conv_b'], p['ffn_w_down'])
    x = x + f
    return x, (conv_a_buf, s5_re, s5_im, conv_c_buf, ssd_state, ffn_buf)

def setup_inputs(seed: int = 0) -> dict:
    key = jax.random.key(seed)
    ks = iter(jax.random.split(key, 64))
    f32 = jnp.float32

    def nrm(shape, scale):
        return jax.random.normal(next(ks), shape, f32) * scale

    def gain(shape):
        return 1.0 + nrm(shape, 0.02)

    dt0 = jnp.exp(jax.random.uniform(next(ks), (DEPTH, SSD_HEADS), f32, math.log(1e-3), math.log(1e-1)))
    lam_im = jnp.pi * jnp.arange(S5_STATE, dtype=f32)
    return {
        'x_prompt': nrm((BATCH, SEQ, D_MODEL), 1.0),
        'x_sample': nrm((DEC_BATCH, DEC_SEQ, D_MODEL), 1.0),
        'mem_prompt': nrm((BATCH, N_MEM, D_MODEL), 1.0),
        'cache_mem_k': nrm((DEPTH, DEC_BATCH, N_MEM, XA_HEADS, XA_HEAD_DIM), 1.0),
        'cache_mem_v': nrm((DEPTH, DEC_BATCH, N_MEM, XA_HEADS, XA_HEAD_DIM), 1.0),
        'state_conv_a': nrm((DEPTH, DEC_BATCH, CONV_A_WIDTH - 1, D_A), 0.5),
        'state_s5_re': nrm((DEPTH, DEC_BATCH, S5_GROUPS, S5_STATE), 0.1),
        'state_s5_im': nrm((DEPTH, DEC_BATCH, S5_GROUPS, S5_STATE), 0.1),
        'state_conv_c': nrm((DEPTH, DEC_BATCH, SSD_CONV_WIDTH - 1, D_XBC), 1.0),
        'state_ssd': nrm((DEPTH, DEC_BATCH, SSD_HEADS, SSD_HEAD_DIM, SSD_STATE), 0.1),
        'state_ffn_conv': nrm((DEPTH, DEC_BATCH, FFN_CONV_WIDTH - 1, D_FF), 1.0),
        'norm_mix_w': gain((DEPTH, D_MODEL)),
        'w_in': nrm((DEPTH, D_MODEL, D_IN), D_MODEL ** -0.5),
        'conv_a_w': nrm((DEPTH, CONV_A_WIDTH, D_A), CONV_A_WIDTH ** -0.5),
        'conv_a_b': nrm((DEPTH, D_A), 0.02),
        'ln_a_w': gain((DEPTH, D_A)),
        'ln_a_b': nrm((DEPTH, D_A), 0.02),
        's5_lam_re': -0.5 + nrm((DEPTH, S5_GROUPS, S5_STATE), 0.02),
        's5_lam_im': lam_im + nrm((DEPTH, S5_GROUPS, S5_STATE), 0.01),
        's5_log_dt': jax.random.uniform(next(ks), (DEPTH, S5_GROUPS), f32, math.log(1e-3), math.log(1e-1)),
        's5_b_re': nrm((DEPTH, S5_GROUPS, S5_STATE, S5_GROUP), (2 * S5_GROUP) ** -0.5),
        's5_b_im': nrm((DEPTH, S5_GROUPS, S5_STATE, S5_GROUP), (2 * S5_GROUP) ** -0.5),
        's5_c_re': nrm((DEPTH, S5_GROUPS, S5_GROUP, S5_STATE), S5_STATE ** -0.5),
        's5_c_im': nrm((DEPTH, S5_GROUPS, S5_GROUP, S5_STATE), S5_STATE ** -0.5),
        's5_d': nrm((DEPTH, D_B), 1.0),
        's5_glu_w': nrm((DEPTH, D_B, D_B), D_B ** -0.5),
        's5_glu_b': nrm((DEPTH, D_B), 0.02),
        'conv_c_w': nrm((DEPTH, SSD_CONV_WIDTH, D_XBC), SSD_CONV_WIDTH ** -0.5),
        'conv_c_b': nrm((DEPTH, D_XBC), 0.02),
        'ssd_dt_bias': dt0 + jnp.log(-jnp.expm1(-dt0)),
        'ssd_a_log': jnp.log(jax.random.uniform(next(ks), (DEPTH, SSD_HEADS), f32, 1.0, 16.0)),
        'ssd_d': gain((DEPTH, SSD_HEADS)),
        'ssd_norm_w': gain((DEPTH, D_C)),
        'w_out': nrm((DEPTH, D_MIX, D_MODEL), D_MIX ** -0.5),
        'norm_xa_w': gain((DEPTH, D_MODEL)),
        'norm_mem_w': gain((DEPTH, D_MODEL)),
        'xa_wq': nrm((DEPTH, D_MODEL, D_MODEL), D_MODEL ** -0.5),
        'xa_wk': nrm((DEPTH, D_MODEL, D_MODEL), D_MODEL ** -0.5),
        'xa_wv': nrm((DEPTH, D_MODEL, D_MODEL), D_MODEL ** -0.5),
        'xa_wo': nrm((DEPTH, D_MODEL, D_MODEL), D_MODEL ** -0.5),
        'norm_ffn_w': gain((DEPTH, D_MODEL)),
        'ffn_w_gate': nrm((DEPTH, D_MODEL, D_FF), D_MODEL ** -0.5),
        'ffn_w_up': nrm((DEPTH, D_MODEL, D_FF), D_MODEL ** -0.5),
        'ffn_conv_w': nrm((DEPTH, FFN_CONV_WIDTH, D_FF), FFN_CONV_WIDTH ** -0.5),
        'ffn_conv_b': nrm((DEPTH, D_FF), 0.02),
        'ffn_w_down': nrm((DEPTH, D_FF, D_MODEL), D_FF ** -0.5),
        'final_norm_w': gain((D_MODEL,)),
    }

def reference(x_prompt, x_sample, mem_prompt, cache_mem_k, cache_mem_v, state_conv_a, state_s5_re, state_s5_im,
              state_conv_c, state_ssd, state_ffn_conv, norm_mix_w, w_in, conv_a_w, conv_a_b, ln_a_w, ln_a_b,
              s5_lam_re, s5_lam_im, s5_log_dt, s5_b_re, s5_b_im, s5_c_re, s5_c_im, s5_d, s5_glu_w, s5_glu_b,
              conv_c_w, conv_c_b, ssd_dt_bias, ssd_a_log, ssd_d, ssd_norm_w, w_out, norm_xa_w, norm_mem_w,
              xa_wq, xa_wk, xa_wv, xa_wo, norm_ffn_w, ffn_w_gate, ffn_w_up, ffn_conv_w, ffn_conv_b, ffn_w_down,
              final_norm_w):
    bp = x_prompt.shape[0]
    yp, ys = x_prompt, x_sample
    outs_p = [[] for _ in range(8)]
    outs_s = [[] for _ in range(6)]
    for l in range(DEPTH):
        p = {'norm_mix_w': norm_mix_w[l], 'w_in': w_in[l], 'conv_a_w': conv_a_w[l], 'conv_a_b': conv_a_b[l],
             'ln_a_w': ln_a_w[l], 'ln_a_b': ln_a_b[l], 's5_lam_re': s5_lam_re[l], 's5_lam_im': s5_lam_im[l],
             's5_log_dt': s5_log_dt[l], 's5_b_re': s5_b_re[l], 's5_b_im': s5_b_im[l], 's5_c_re': s5_c_re[l],
             's5_c_im': s5_c_im[l], 's5_d': s5_d[l], 's5_glu_w': s5_glu_w[l], 's5_glu_b': s5_glu_b[l],
             'conv_c_w': conv_c_w[l], 'conv_c_b': conv_c_b[l], 'ssd_dt_bias': ssd_dt_bias[l],
             'ssd_a_log': ssd_a_log[l], 'ssd_d': ssd_d[l], 'ssd_norm_w': ssd_norm_w[l], 'w_out': w_out[l],
             'norm_xa_w': norm_xa_w[l], 'xa_wq': xa_wq[l], 'xa_wo': xa_wo[l], 'norm_ffn_w': norm_ffn_w[l],
             'ffn_w_gate': ffn_w_gate[l], 'ffn_w_up': ffn_w_up[l], 'ffn_conv_w': ffn_conv_w[l],
             'ffn_conv_b': ffn_conv_b[l], 'ffn_w_down': ffn_w_down[l]}
        memn = _rmsnorm(mem_prompt, norm_mem_w[l])
        mk = (memn @ xa_wk[l]).reshape(bp, N_MEM, XA_HEADS, XA_HEAD_DIM)
        mv = (memn @ xa_wv[l]).reshape(bp, N_MEM, XA_HEADS, XA_HEAD_DIM)
        yp, st_p = _layer(yp, mk, mv,
                          jnp.zeros((bp, CONV_A_WIDTH - 1, D_A), yp.dtype),
                          jnp.zeros((bp, S5_GROUPS, S5_STATE), jnp.float32),
                          jnp.zeros((bp, S5_GROUPS, S5_STATE), jnp.float32),
                          jnp.zeros((bp, SSD_CONV_WIDTH - 1, D_XBC), yp.dtype),
                          jnp.zeros((bp, SSD_HEADS, SSD_HEAD_DIM, SSD_STATE), jnp.float32),
                          jnp.zeros((bp, FFN_CONV_WIDTH - 1, D_FF), yp.dtype), p)
        ys, st_s = _layer(ys, cache_mem_k[l], cache_mem_v[l], state_conv_a[l], state_s5_re[l], state_s5_im[l],
                          state_conv_c[l], state_ssd[l], state_ffn_conv[l], p)
        for lst, v in zip(outs_p, st_p + (mk, mv)):
            lst.append(v)
        for lst, v in zip(outs_s, st_s):
            lst.append(v)
    y_prompt = _rmsnorm(yp, final_norm_w)
    y_sample = _rmsnorm(ys, final_norm_w)
    (p_conv_a, p_s5_re, p_s5_im, p_conv_c, p_ssd, p_ffn_conv, p_mem_k, p_mem_v) = [jnp.stack(o) for o in outs_p]
    (s_conv_a, s_s5_re, s_s5_im, s_conv_c, s_ssd, s_ffn_conv) = [jnp.stack(o) for o in outs_s]
    return (y_prompt, y_sample, p_conv_a, p_s5_re, p_s5_im, p_conv_c, p_ssd, p_ffn_conv, p_mem_k, p_mem_v,
            s_conv_a, s_s5_re, s_s5_im, s_conv_c, s_ssd, s_ffn_conv)


_drawn_inputs = setup_inputs


def setup_inputs(seed=0):
    import zlib

    import numpy as np

    out = dict(_drawn_inputs(seed))
    spreads = {}
    factors = {'conv_a_b': 5.005,
     'ln_a_w': 8.0,
     'ln_a_b': 8.0,
     's5_c_re': 3.964,
     's5_c_im': 3.841,
     's5_glu_b': 53.343,
     'ssd_d': 6.63,
     'ssd_norm_w': 4.149,
     'norm_xa_w': 8.0,
     'norm_mem_w': 2.904,
     'ffn_conv_b': 20.666,
     'final_norm_w': 8.066,
     'norm_ffn_w': 2.733}
    for name, (base, spread) in spreads.items():
        noise = np.random.default_rng([zlib.crc32(name.encode()), seed]).standard_normal(out[name].shape)
        drawn = base * np.exp(spread * noise) if base else spread * noise
        out[name] = __import__('jax').numpy.asarray(drawn.astype(out[name].dtype))
    for name, factor in factors.items():
        out[name] = (out[name] * factor).astype(out[name].dtype)
    return out
```

```python
import math
from contextlib import ExitStack

import concourse.bass as bass
from concourse import mybir

F32 = mybir.dt.float32
F32R = mybir.dt.float32r
ALU = mybir.AluOpType
ACT = mybir.ActivationFunctionType
AX = mybir.AxisListType

P = 128
D = 2048
KT = D // P
NP, NB, NL = 256, 8, 4
NS = NB * NL
T = NP + NS
GW = 512
GM = GW // P
SLABS = 8
D_IN = 4112
WA = 31
HA = WA - 1
UP = HA + NP
US = HA + NL
WC, HC = 4, 3
XP = HC + NP
XS = HC + NL
SG, SP_ = 32, 64
SJ = SG * SP_ // P
NH, HP, NST = 16, 64, 128
YT = NH * HP // P
XH, XD = 4, 512
NM = 256
MT = NM // P
FF = 5504
FT = FF // P
EPS = 1e-6
TWO_PI = 2.0 * math.pi
MAGIC = 1.5 * 2.0 ** 23
PI_A = 6.28125
PI_B = 0.00193500518798828125
PI_C = TWO_PI - PI_A - PI_B
GORDER = [2, 0, 1, 5, 6, 7, 3, 4]
GROUP_DT = 8 * GW


SERIES = {
    "act_setup": (("s5_exp", 2), ("s5_sin", 2), ("dt_act", 5), ("s5_bus", 4), ("mem_sq", 2), ("mem_s", 1),
                  ("memn", 2), ("tap_a", 8), ("tap_c", 24), ("conv_c", 12), ("s5_gelu", 4), ("memT", 16),
                  ("compact", 2), ("ex_read", 10)),
    "act_mixers": (("conf_sq", 4), ("conf_s", 1), ("conf_silu", 4), ("cat_a_hi", 4), ("gate_s", 2),
                   ("cat_c_hi", 8), ("qs_hi", 4), ("ps_exp", 1), ("pTs_hi", 4), ("os_hi", 1)),
    "act_sample": (("kc_hi", 64), ("v_hi", 32)),
    "dve_sample": (("kc_lo", 64), ("v_lo", 32)),
    "dve_setup": (("s5_arg", 2), ("theta", 1), ("bc_padded", 4), ("dt_read", 1), ("dt_dve", 3),
                  ("dt_rows", 1), ("mem_v", 2), ("u_done", 8), ("conv_a", 4), ("conv_c_taps", 12)),
    "dve_mixers": (("centred", 4), ("conf_read", 1), ("conf_scaled", 4), ("cat_a", 4), ("tok_read", 3),
                   ("gate_read", 2), ("gate_scaled", 8), ("cat_c", 8), ("qs_lo", 4), ("s_kept", 8), ("ps_max", 1),
                   ("ps_norm", 1), ("pTs_lo", 4), ("o_kept", 8), ("os_lo", 1)),
    "dve_norms": (("hmix", 16), ("hxa", 16), ("hffn", 16), ("hfin", 16)),
    "pe_mixers": (("mem_t", 8), ("ex_mm", 5), ("glu_mm", 4), ("conf_mm", 2), ("tok_mm", 1), ("ps_t", 1),
                  ("os_t", 1)),
}
PLACE = {}
for series, kinds in SERIES.items():
    before = 0
    for kind, count in kinds:
        PLACE[kind] = (series, before)
        before += count


class Own:

    def __init__(self, eng, sem):
        self.eng, self.sem, self.n = eng, sem, 0

    def step(self, ins):
        ins.then_inc(self.sem, 1)
        self.n = self.n + 1

    def sync(self):
        self.eng.wait_ge(self.sem, self.n)

    def link(self, ins):
        self.step(ins)
        self.sync()


def hymba_step(nc, I, O):
    ctx = ExitStack()
    sems = {}

    def S(name):
        name = PLACE.get(name, (name, 0))[0]
        if name not in sems:
            sems[name] = ctx.enter_context(nc.semaphore(name))
        return sems[name]

    def at(name, count):
        return S(name), count + PLACE.get(name, (name, 0))[1]

    def alloc(stack, name, shape, dt=F32):
        return stack.enter_context(nc.sbuf_tensor(name, shape, dt))

    with ctx:
        def sb(name, shape, dt=F32):
            return alloc(ctx, name, shape, dt)

        ident = sb("ident", [P, P])
        ones = sb("ones", [P, P])
        negmask = sb("negmask", [P, P])
        negs = sb("negs", [NS, NS])
        bmask = sb("bmask", [P, NB])
        g4 = sb("g4", [P, 4])
        gsel = sb("gsel", [P, 2])
        gneg = sb("gneg", [P, 2])
        segmask = sb("segmask", [NH, T])
        prm = sb("prm", [P, 120 + 104 + 124])
        xT = sb("xT", [P, KT, T])
        ssq = sb("ssq", [P, T])
        sqt = sb("sqt", [P, T])
        rstd = sb("rstd", [P, T])
        hbuf = sb("hbuf", [P, 2, T])
        raw = sb("raw", [P, 4, 1024])
        msum = sb("msum", [P, 6])
        pairs = sb("pairs", [P, 2])
        gcol_b = sb("gcol_b", [P, 4])

        def col(base):
            return prm[:, base:base + 1]
        C_MIX, C_XA, C_MEM, C_FFN, C_FIN, C_CAB, C_LNW, C_LNB, C_S5D, C_GLB, C_SNW, C_CCB = \
            0, 16, 32, 48, 64, 80, 84, 88, 92, 96, 100, 108
        C_LR, C_LI, C_LDT, C_CCW, C_SSDD = 120, 136, 152, 168, 216
        C_CAW = 224

        lev = ExitStack()
        mtok = alloc(lev, "mtok", [P, MT, D])
        xbr = alloc(lev, "xbr", [P, 12, XP + NB * XS])
        th = alloc(lev, "th", [P, 4, T])
        lev.close()
        hhi = sb("hhi", [P, KT, T], F32R)
        hlo = sb("hlo", [P, KT, T], F32R)
        lev = ExitStack()
        xtok = alloc(lev, "xtok", [P, 3, D])
        lev.close()
        lev = ExitStack()
        tabC = alloc(lev, "tabC", [P, SJ, NP])
        tabS = alloc(lev, "tabS", [P, SJ, NP])
        lev.close()
        lev = ExitStack()
        glu_w = alloc(lev, "glu_w", [P, 4, 512])
        lev.close()
        lev = ExitStack()
        qs_hi = alloc(lev, "qs_hi", [P, KT, XH, NS], F32R)
        qs_lo = alloc(lev, "qs_lo", [P, KT, XH, NS], F32R)
        lev.close()
        kT = sb("kT", [P, KT, NM])
        lev = ExitStack()
        pTs_hi = alloc(lev, "pTs_hi", [P, MT, XH, XH, NS], F32R)
        pTs_lo = alloc(lev, "pTs_lo", [P, MT, XH, XH, NS], F32R)
        lev.close()
        vtok = sb("vtok", [P, MT, D])
        def fx(r):
            room = kT if r < 8 else vtok
            return room[0:18, :, :].rearrange("p a b -> p (a b)")[:, (r % 8) * 512:(r % 8 + 1) * 512]

        mixers = ExitStack()
        lev = ExitStack()
        hT = alloc(lev, "hT", [P, KT, T])
        lev.close()
        lev = ExitStack()
        memT = alloc(lev, "memT", [P, KT, NM])
        lev.close()
        alloc(mixers, "hT_room", [P, KT, T])
        uT = alloc(mixers, "uT", [P, 4, T])
        zs = alloc(mixers, "zs", [P, YT, T])
        xc = alloc(mixers, "xc", [P, 12, T])
        wdt = alloc(mixers, "wdt", [P, KT, NH])
        dtr = alloc(mixers, "dtr", [NH, 3, T])
        tokT = alloc(mixers, "tokT", [P, 9, NH])
        diag = alloc(mixers, "diag", [NH, NH])
        hcol = alloc(mixers, "hcol", [NH, 4])
        R_DT, R_CS, R_END = [dtr[:, i, :] for i in range(3)]
        R_RAW, R_EXP, R_LN, R_W, R_T = [zs[0:NH, i, :] for i in (3, 4, 5, 6, 7)]
        lev = ExitStack()
        rows = alloc(lev, "rows", [P, 3, P])
        srow = alloc(lev, "srow", [P, 2, P])
        harow = alloc(lev, "harow", [120, 2, 512])
        hcrow = alloc(lev, "hcrow", [NB * HC, 1536])
        brow = alloc(lev, "brow", [P, 2, SJ, 16])
        crow = alloc(lev, "crow", [P, 2, 4, SP_])
        bpad = alloc(lev, "bpad", [P, 2, SJ, 32])
        cpad = alloc(lev, "cpad", [P, 2, 4, 2, SP_])
        lev.close()
        lev = ExitStack()
        va = alloc(lev, "va", [P, 4, T])
        tAB = alloc(lev, "tAB", [P, 2, 2, NP])
        gri = alloc(lev, "gri", [P, 2, 2, NP])
        hAB = alloc(lev, "hAB", [P, 2, 2, NP])
        hri = alloc(lev, "hri", [P, 2, 2, NP])
        hsr = alloc(lev, "hsr", [P, 2, SJ, NS])
        s0s = alloc(lev, "s0s", [P, 2, P])
        bT = alloc(lev, "bT", [P, 2, 4, P])
        cT = alloc(lev, "cT", [P, 2, 4, P])
        up = alloc(lev, "up", [P, 4, UP + NB * US])
        sc = alloc(lev, "sc", [P, 25, SJ])
        fin = alloc(lev, "fin", [P, 2, SJ])
        new_a = hri[:, 0, 0, 0:4 * NS]
        new_c = hri[:, 1, :, :].rearrange("p a b -> p (a b)")[:, 0:12 * NB * HC]
        exa = tAB[:, :, :, :].rearrange("p i a b -> p i (a b)")
        lev.close()
        lev = ExitStack()
        xdt = alloc(lev, "xdt", [P, 3, NH * HP])
        xds = alloc(lev, "xds", [P, NH * HP])
        btok = alloc(lev, "btok", [P, 3, 2, NST])
        cb = alloc(lev, "cb", [P, 2, 2, P])
        cbs = alloc(lev, "cbs", [NS, 2, NS])
        pvT = alloc(lev, "pvT", [P, NH * HP])
        ecl = alloc(lev, "ecl", [P, NH])
        dec = alloc(lev, "dec", [P, 2, NP])
        decs = alloc(lev, "decs", [NS, 2, NS])
        eb = alloc(lev, "eb", [P, P + NS])
        yo = alloc(lev, "yo", [P, P + NS])
        s0 = alloc(lev, "s0", [P, 2, NB, NST])
        s0T = alloc(lev, "s0T", [P, NB, P])
        bm = alloc(lev, "bm", [NS, NB, NST])
        lev.close()
        mixers.close()

        whi = sb("whi", [P, 2, 1024], F32R)
        wlo = sb("wlo", [P, 2, 1024], F32R)
        lev = ExitStack()
        qT = alloc(lev, "qT", [P, KT, T])
        kv = alloc(lev, "kv", [P, 2, MT, D])
        kc_hi = alloc(lev, "kc_hi", [P, 2, 4, NM], F32R)
        kc_lo = alloc(lev, "kc_lo", [P, 2, 4, NM], F32R)
        pr = alloc(lev, "pr", [P, 2, NM])
        pT = alloc(lev, "pT", [P, 2, MT, P])
        prs = alloc(lev, "prs", [P, NM])
        osum = alloc(lev, "osum", [P, XD])
        sm = alloc(lev, "sm", [P, 9, 4])
        lev.close()
        lev = ExitStack()
        act = alloc(lev, "act", [P, FT, T])
        frow = alloc(lev, "frow", [86, 2, P])
        fprm = alloc(lev, "fprm", [P, 4, FT])
        fhrow = alloc(lev, "fhrow", [16, FF])
        lev.close()
        lev = ExitStack()
        alloc(lev, "act_room", [P, FT, T])
        alloc(lev, "frow_room", [86, 2, P])
        alloc(lev, "fprm_room", [P, 4, FT])
        fh = alloc(lev, "fh", [P, FT, NB, 2])
        gcol = alloc(lev, "gcol", [P, FT, 18])
        cg = alloc(lev, "cg", [P, 4, T])
        spad = alloc(lev, "spad", [P, 4, NB, NL + 2])
        gs = alloc(lev, "gs", [P, 4, T])
        ahi = alloc(lev, "ahi", [P, 2, T], F32R)
        alo = alloc(lev, "alo", [P, 2, T], F32R)
        lev.close()
        lev = ExitStack()
        fT = alloc(lev, "fT", [P, KT, T])
        yst = alloc(lev, "yst", [P, 6, 512])
        lev.close()

        B = [ctx.enter_context(nc.psum_tensor(f"bank{i}", [P, 512], F32)) for i in range(8)]

        def v3(ap, n):
            return ap.rearrange("p (a b) -> p a b", b=n)

        def vsplit(ap, n):
            return ap.rearrange("p (a b) -> p a b", a=n)

        def up_sample(t):
            return v3(up[:, t, UP:UP + NB * US], US)

        def xbr_sample(t):
            return v3(xbr[:, t, XP:XP + NB * XS], XS)

        NA = 8 * 8
        NKV = 8 * 8
        NS_B = NA + NKV
        G_OUT, G_Q, G_O, G_FF = 0, 4, 8, 12
        FPAIRS = FF // GW
        FTAIL = (FF - FPAIRS * GW) // P
        NG_B = G_FF + 2 * FPAIRS + 2
        NB_DOWN = NG_B * 8
        DG = 8

        w_in = I["w_in"][0]
        rows_of = lambda w: w.rearrange("(s k p) n -> s p k n", k=2, p=P)

        def slab_src(w, s, c0, width):
            return rows_of(w)[s][:, :, bass.ds(c0, width)] if not isinstance(c0, int) \
                else rows_of(w)[s][:, :, c0:c0 + width]

        def slab_dst(slot, width):
            return raw[:, slot, 0:2 * width].rearrange("p (k n) -> p k n", k=2)

        def wait_raw(eng, fill, slot):
            eng.wait_ge(*at(f"raw_loaded{slot}", 16 * (fill + 1)))

        def wait_used_A(eng, sl):
            if sl < 0:
                return
            if sl < NA:
                g, r = divmod(sl, 8)
                eng.wait_ge(*at("in_slab" if r < 7 else "in_acc", 7 * g + r + 1 if r < 7 else 4 * (g + 1)))
            else:
                g, r = divmod(sl - NA, 8)
                eng.wait_ge(*at("kv_slab" if r < 7 else "kv_acc", 7 * g + r + 1 if r < 7 else 2 * (g + 1)))

        def wait_used_B(eng, g, r):
            if r < 0:
                g, r = g - 1, r + 8
            if isinstance(g, int) and g < 0:
                return
            if r < 7:
                eng.wait_ge(*at("b_slab", 7 * g + (r + 1)))
            elif isinstance(g, int) and g >= NG_B - 2:
                eng.wait_ge(*at("b_acc", 4 * (NG_B - 2) + FTAIL * (g - NG_B + 3)))
            else:
                eng.wait_ge(*at("b_acc", 4 * g + 4))

        def loop(eng, n, body):
            body(0)
            with eng.Fori(1, n) as i:
                body(i)

        STORES = dict(st_kv=16, st_conv_a=2, st_conv_c=6, st_conv_a_old=1, st_s5=4, st_ssd_p=1,
                      st_ssd0=4, st_ssd1=4, st_ffn=4, st_y0=6, st_y1=6)

        block = ctx.enter_context(nc.Block())

        @block.sync
        def _(sp):
            for t in range(2):
                sp.dma_start(xtok[:, t, :], I["x_prompt"][0, t * P:(t + 1) * P, :]).then_inc(S("x_loaded"), 16)
            sp.dma_start(xtok[0:NS, 2, :], I["x_sample"].rearrange("b l d -> (b l) d")).then_inc(S("x_loaded"), 16)
            with nc.allow_non_contiguous_dma(reason="16 columns of w_in"):
                sp.dma_start(wdt[:, :, :], w_in.rearrange("(k p) n -> p k n", p=P)[:, :, GROUP_DT:D_IN])\
                  .then_inc(S("wdt_loaded"), 16)

            for g, cg_ in enumerate(GORDER):
                for s in range(8):
                    sl = 8 * g + s
                    wait_used_A(sp, sl - 4)
                    sp.dma_start(slab_dst(sl % 4, GW), slab_src(w_in, s, cg_ * GW, GW))\
                      .then_inc(S(f"raw_loaded{sl % 4}"), 16)
                if g == 1:
                    for t in range(MT):
                        sp.dma_start(mtok[:, t, :], I["mem_prompt"][0, t * P:(t + 1) * P, :])\
                          .then_inc(S("mem_loaded"), 16)
            for g in range(8):
                w = I["xa_wk"][0] if g < 4 else I["xa_wv"][0]
                for s in range(8):
                    sl = NA + 8 * g + s
                    wait_used_A(sp, sl - 4)
                    sp.dma_start(slab_dst(sl % 4, GW), slab_src(w, s, (g % 4) * GW, GW))\
                      .then_inc(S(f"raw_loaded{sl % 4}"), 16)

            def split_group(w, g, c0, width=GW):
                for s in range(8):
                    if isinstance(g, int) and g == 0 and s < 4:
                        wait_used_A(sp, NS_B + s - 4)
                    else:
                        sp.wait_ge(*at("w_lo", 8 * g + (s - 3)))
                    sp.dma_start(slab_dst(s % 4, width), slab_src(w, s, c0, width))\
                      .then_inc(S(f"raw_loaded{s % 4}"), 16)

            def four_groups(w, g0):
                loop(sp, 4, lambda i: split_group(w, g0 + i, i * GW))

            k_rows = I["cache_mem_k"][0].rearrange("b (t p) h d -> b p t (h d)", p=P)
            v_rows = I["cache_mem_v"][0].rearrange("b (t p) h d -> b p t (h d)", p=P)
            four_groups(I["w_out"][0], G_OUT)
            sp.wait_ge(*at("cat_c", 8))
            for i in range(2):
                sp.wait_ge(*at(f"st_ssd{i}", 16 * 4))
            for b in range(2):
                sp.dma_start(kv[:, b % 2, :, :], k_rows[b]).then_inc(S(f"kv_loaded{b % 2}"), 16)
            four_groups(I["xa_wq"][0], G_Q)
            for b in range(2, NB):
                sp.wait_ge(*at("kc_t", 8 * (b - 1)))
                sp.dma_start(kv[:, b % 2, :, :], k_rows[b]).then_inc(S(f"kv_loaded{b % 2}"), 16)
            for b in range(NB):
                if b < 2:
                    sp.wait_ge(*at("kc_t", 8 * (NB - 1 + b)))
                else:
                    sp.wait_ge(*at("v_lo", XH * (b - 1)))
                sp.dma_start(kv[:, b % 2, :, :], v_rows[b]).then_inc(S(f"kv_loaded{b % 2}"), 16)
            four_groups(I["xa_wo"][0], G_O)

            def gate_up(i):
                split_group(I["ffn_w_gate"][0], G_FF + 2 * i, i * GW)
                split_group(I["ffn_w_up"][0], G_FF + 1 + 2 * i, i * GW)
            loop(sp, FPAIRS, gate_up)
            split_group(I["ffn_w_gate"][0], G_FF + 2 * FPAIRS, FPAIRS * GW, FTAIL * P)
            split_group(I["ffn_w_up"][0], G_FF + 1 + 2 * FPAIRS, FPAIRS * GW, FTAIL * P)

            wd = I["ffn_w_down"][0].rearrange("(f p) n -> f p n", p=P)
            for half in range(2):
                c0 = half * DG * P

                def down(f, j):
                    sp.wait_ge(*at("w_lo", NB_DOWN + half * FT + f - 3))
                    slot = (NB_DOWN + half * FT + j) % 4
                    src = wd[f, :, c0:c0 + DG * P] if isinstance(f, int) \
                        else wd[bass.ds(f, 1), :, c0:c0 + DG * P].rearrange("a p n -> p (a n)")
                    sp.dma_start(raw[:, slot, :], src).then_inc(S(f"raw_loaded{slot}"), 16)

                def four(i):
                    for j in range(4):
                        down(4 * i + j, j)
                loop(sp, FT // 4, four)
                for j in range(FT % 4):
                    down(FT - FT % 4 + j, j)
            for name, n in STORES.items():
                sp.wait_ge(*at(name, 16 * n))


        @block.gpsimd
        def _(pool):
            me = Own(pool, S("pool_step"))
            me.step(pool.memset(ident[:, :], 0.0))
            me.step(pool.memset(ones[:, :], 1.0))
            me.step(pool.memset(negmask[:, :], 0.0))
            me.step(pool.memset(negs[:, :], 0.0))
            me.step(pool.memset(bmask[:, :], 1.0))
            me.step(pool.memset(g4[:, :], 1.0))
            me.step(pool.memset(segmask[:, :], 1.0))
            me.sync()
            me.step(pool.affine_select(out=ident[:, :], in_=ident[:, :], compare_op=ALU.not_equal, fill=1.0,
                                       base=0, pattern=[[-1, P]], channel_multiplier=1))
            me.step(pool.affine_select(out=negmask[:, :], in_=negmask[:, :], compare_op=ALU.is_ge, fill=-1e30,
                                       base=0, pattern=[[1, P]], channel_multiplier=-1))
            vneg = v3(negs[:, :], NL)
            me.step(pool.affine_select(out=vneg, in_=vneg, compare_op=ALU.is_ge, fill=-1e30,
                                       base=0, pattern=[[NL, NB], [1, NL]], channel_multiplier=-1))
            me.step(pool.affine_select(out=g4[:, :], in_=g4[:, :], compare_op=ALU.is_ge, fill=0.0,
                                       base=0, pattern=[[-32, 4]], channel_multiplier=1))
            me.step(pool.memset(segmask[:, 0:1], 0.0))
            me.step(pool.memset(segmask[:, P:P + 1], 0.0))
            me.step(pool.memset(segmask[:, NP:T:NL], 0.0))
            me.sync()
            me.step(pool.affine_select(out=vneg, in_=vneg, compare_op=ALU.is_ge, fill=-1e30,
                                       base=0, pattern=[[-NL, NB], [0, NL]], channel_multiplier=1))
            me.step(pool.affine_select(out=g4[:, :], in_=g4[:, :], compare_op=ALU.is_ge, fill=0.0,
                                       base=15, pattern=[[32, 4]], channel_multiplier=-1))
            pool.memset(bpad[:, :, :, :], 0.0).then_inc(S("consts"), 1)
            pool.memset(ssq[:, :], 0.0).then_inc(S("consts"), 1)
            me.sync()
            pool.wait_ge(*at("consts", 2))

            def squares(n, ready, base):
                for k in range(KT):
                    pool.wait_ge(*at(ready, base + k + 1))
                    me.link(pool.tensor_tensor(sqt[:, :], xT[:, k, :], xT[:, k, :], ALU.mult))
                    q = pool.tensor_tensor(ssq[:, :], ssq[:, :], sqt[:, :], ALU.add)
                    if k == KT - 1:
                        q.then_inc(S("ssq_done"), 1)
                    else:
                        me.link(q)

            squares(0, "s0_turned", 1)

            pool.wait_ge(*at("theta", 1))
            n = 1
            while n < NP:
                er, ei = sc[:, 16, :], sc[:, 17, :]
                step = min(n, 32)
                for o in range(0, n, step):
                    e_r = er.unsqueeze(2).to_broadcast([P, SJ, step])
                    e_i = ei.unsqueeze(2).to_broadcast([P, SJ, step])
                    c_in, s_in = tabC[:, :, o:o + step], tabS[:, :, o:o + step]
                    t1 = tAB[:, 0, :, :].rearrange("p a b -> p (a b)")[:, 0:SJ * step].rearrange(
                        "p (j t) -> p j t", j=SJ)
                    t2 = tAB[:, 1, :, :].rearrange("p a b -> p (a b)")[:, 0:SJ * step].rearrange(
                        "p (j t) -> p j t", j=SJ)
                    me.step(pool.tensor_tensor(t1, c_in, e_r, ALU.mult))
                    me.step(pool.tensor_tensor(t2, s_in, e_i, ALU.mult))
                    me.sync()
                    me.step(pool.tensor_tensor(tabC[:, :, n + o:n + o + step], t1, t2, ALU.subtract))
                    me.sync()
                    me.step(pool.tensor_tensor(t1, c_in, e_i, ALU.mult))
                    me.step(pool.tensor_tensor(t2, s_in, e_r, ALU.mult))
                    me.sync()
                    me.step(pool.tensor_tensor(tabS[:, :, n + o:n + o + step], t1, t2, ALU.add))
                    me.sync()
                n *= 2
                if n < NP:
                    a, b_, c_ = sc[:, 18, :], sc[:, 19, :], sc[:, 20, :]
                    me.step(pool.tensor_tensor(a, er, er, ALU.mult))
                    me.step(pool.tensor_tensor(b_, ei, ei, ALU.mult))
                    me.step(pool.tensor_tensor(c_, er, ei, ALU.mult))
                    me.sync()
                    me.step(pool.tensor_tensor(er, a, b_, ALU.subtract))
                    me.step(pool.tensor_tensor(ei, c_, c_, ALU.add))
                    me.sync()
            pool.wait_ge(*at("sum_mm", 1))
            pool.memset(ssq[:, :], 0.0).then_inc(S("tables"), 1)
            for h in range(XH):
                rows_h = bmask[NS * h:NS * (h + 1), :]
                me.link(pool.affine_select(out=rows_h, in_=rows_h, compare_op=ALU.is_ge, fill=0.0,
                                           base=0, pattern=[[-NL, NB]], channel_multiplier=1))
                me.link(pool.affine_select(out=rows_h, in_=rows_h, compare_op=ALU.is_ge, fill=0.0,
                                           base=NL - 1, pattern=[[NL, NB]], channel_multiplier=-1))

            for j in range(SJ):
                pool.wait_ge(*at("s5_scanned", j + 1))
                g_ = gri[:, j % 2, :, :]
                me.step(pool.tensor_tensor(hAB[:, 0, :, :], g_,
                                           tabC[:, j, :].unsqueeze(1).to_broadcast([P, 2, NP]), ALU.mult))
                me.step(pool.tensor_tensor(hAB[:, 1, :, :], g_,
                                           tabS[:, j, :].unsqueeze(1).to_broadcast([P, 2, NP]), ALU.mult))
                me.sync()
                if j >= 2:
                    pool.wait_ge(*at("s5_h_used", j - 1))
                pool.tensor_tensor(hri[:, j % 2, 0, :], hAB[:, 0, 0, :], hAB[:, 1, 1, :], ALU.subtract)\
                    .then_inc(S("s5_h"), 1)
                pool.tensor_tensor(hri[:, j % 2, 1, :], hAB[:, 0, 1, :], hAB[:, 1, 0, :], ALU.add)\
                    .then_inc(S("s5_h"), 1)
                pool.wait_ge(*at("s5_h", 2 * j + 2))
                me.link(pool.tensor_copy(fin[:, 0, j:j + 1], hri[:, j % 2, 0, NP - 1:NP]))
                me.link(pool.tensor_copy(fin[:, 1, j:j + 1], hri[:, j % 2, 1, NP - 1:NP]))
                if j == 1:
                    pool.wait_ge(*at("s5_bus", 4))
                    pool.wait_ge(*at("s0_turned", 18))
                    hr = hsr[:, 0, :, :].rearrange("p j (b l) -> p j b l", l=NL)
                    hi = hsr[:, 1, :, :].rearrange("p j (b l) -> p j b l", l=NL)
                    a_r = sc[:, 12, :].unsqueeze(2).to_broadcast([P, SJ, NB])
                    a_i = sc[:, 13, :].unsqueeze(2).to_broadcast([P, SJ, NB])
                    ta = hAB[:, 0, 0, 0:P].rearrange("p (j b) -> p j b", b=NB)
                    tb = hAB[:, 0, 1, 0:P].rearrange("p (j b) -> p j b", b=NB)
                    tc_ = hAB[:, 1, 0, 0:P].rearrange("p (j b) -> p j b", b=NB)
                    td = hAB[:, 1, 1, 0:P].rearrange("p (j b) -> p j b", b=NB)
                    for l in range(NL):
                        p_r = s0s[:, 0, :].rearrange("p (b j) -> p j b", j=SJ) if l == 0 else hr[:, :, :, l - 1]
                        p_i = s0s[:, 1, :].rearrange("p (b j) -> p j b", j=SJ) if l == 0 else hi[:, :, :, l - 1]
                        me.step(pool.tensor_tensor(ta, a_r, p_r, ALU.mult))
                        me.step(pool.tensor_tensor(tb, a_i, p_i, ALU.mult))
                        me.step(pool.tensor_tensor(tc_, a_r, p_i, ALU.mult))
                        me.step(pool.tensor_tensor(td, a_i, p_r, ALU.mult))
                        me.sync()
                        me.step(pool.tensor_tensor(ta, ta, tb, ALU.subtract))
                        me.step(pool.tensor_tensor(tc_, tc_, td, ALU.add))
                        me.sync()
                        me.step(pool.tensor_tensor(hr[:, :, :, l], hr[:, :, :, l], ta, ALU.add))
                        q = pool.tensor_tensor(hi[:, :, :, l], hi[:, :, :, l], tc_, ALU.add)
                        if l < NL - 1:
                            me.step(q)
                            me.sync()
                        else:
                            q.then_inc(S("s5_hs"), 1)
                            me.sync()
                            pool.wait_ge(*at("s5_hs", 1))
            pool.wait_ge(*at("s5_hs", 1))
            for i in range(2):
                last = hsr[:, i, :, :].rearrange("p j (b l) -> p b j l", l=NL)[:, :, :, NL - 1]
                pool.tensor_copy(s0s[:, i, :].rearrange("p (b j) -> p b j", j=SJ), last).then_inc(S("s5_fin"), 1)
            me.link(pool.memset(sqt[:, :], 0.0))

            for j in range(YT):
                g = j // 4
                for h in range(2):
                    pool.wait_ge(*at("decay", 4 * j + 2 * h + 1))
                    pool.tensor_tensor(vsplit(dec[:, h, :], 2), vsplit(dec[:, h, :], 2),
                                       cb[:, :, g, :], ALU.mult).then_inc(S("mixed"), 1)
                    pool.wait_ge(*at("decay", 4 * j + 2 * h + 2))
                    pool.tensor_tensor(decs[:, h, :], decs[:, h, :], cbs[:, g, :], ALU.mult)\
                        .then_inc(S("mixed"), 1)
                pool.wait_ge(*at("eb_ready", j + 1))
                pool.wait_ge(*at("s0_T", 2 * j + 2))
                last = eb[:, P:P + NS].rearrange("p (b l) -> p b l", l=NL)[:, :, NL - 1]
                pool.tensor_tensor(s0[:, j % 2, :, :], s0[:, j % 2, :, :],
                                   last.unsqueeze(2).to_broadcast([P, NB, NST]), ALU.mult)\
                    .then_inc(S("s0_decayed"), 1)
            for j in range(YT):
                pool.wait_ge(*at("gated", j + 1))
                dst = ssq if j < 4 else sqt
                me.link(pool.tensor_tensor(hbuf[:, 1, :], zs[:, j, :], zs[:, j, :], ALU.mult))
                q = pool.tensor_tensor(dst[:, :], dst[:, :], hbuf[:, 1, :], ALU.add)
                if j % 4 == 3:
                    q.then_inc(S("gate_sq"), 1)
                    pool.wait_ge(*at("gate_sq", j // 4 + 1))
                else:
                    me.link(q)

            for n, (ready, base, summed) in enumerate((("x_out", 0, 1), ("x_o", 0, 2), ("x_down", 0, 3))):
                if n == 0:
                    pool.wait_ge(*at("gate_mm", 2))
                else:
                    pool.wait_ge(*at("sum_mm", n + 1))
                me.link(pool.memset(ssq[:, :], 0.0))
                if n == 2:
                    def pair(i, mt=GM):
                        for m in range(mt):
                            pool.wait_ge(*at("silu", 4 * i + m + 1))
                            pool.tensor_tensor(cg[:, m, :], cg[:, m, :], rstd[:, :], ALU.mult)\
                                .then_inc(S("gate_n"), 1)
                    loop(pool, FPAIRS, pair)
                    pair(FPAIRS, FTAIL)
                squares(n + 1, ready, base)
                if n == 0:
                    pool.wait_ge(*at("scores", 8))
                    for pad in (qs_hi, qs_lo):
                        pool.memset(pad[:, :, :, :].bitcast(F32), 0.0).then_inc(S("pads"), 1)
                    pool.wait_ge(*at("pv", 8))
                    for pad in (pTs_hi, pTs_lo):
                        pool.memset(pad[:, :, :, :, :].bitcast(F32), 0.0).then_inc(S("pads"), 1)

        @block.tensor
        def _(pe):
            def mm(out, l, r, start=True, stop=True):
                return pe.matmul(out, lhsT=l, rhs=r, start=start, stop=stop)

            pe.wait_ge(*at("consts", 1))
            pe.wait_ge(*at("rows_loaded", 16 * 18))
            pe.wait_ge(*at("rows_spread", 2))
            pe.transpose(B[0][:, 0:120], rows[0:120, 0, :], ident[0:120, 0:120])
            pe.transpose(B[0][:, 120:224], rows[0:104, 1, :], ident[0:104, 0:104])
            pe.transpose(B[0][:, 224:348], rows[0:124, 2, :], ident[0:124, 0:124]).then_inc(S("s0_t"), 1)
            pe.wait_ge(*at("x_loaded", 48))
            for k in range(KT):
                bk = B[4 + k % 3]
                if k >= 3:
                    pe.wait_ge(*at("s0_turned", k - 1))
                for t in range(2):
                    pe.transpose(bk[:, t * P:(t + 1) * P], xtok[:, t, k * P:(k + 1) * P], ident[:, :])
                pe.transpose(bk[:, NP:T], xtok[0:NS, 2, k * P:(k + 1) * P], ident[0:NS, 0:NS]).then_inc(S("s0_t"), 1)
            pe.wait_ge(*at("hist_loaded", 16 * 9))
            for i in range(2):
                q = pe.transpose(B[1][:, i * P:(i + 1) * P], srow[:, i, :], ident[:, :])
            q.then_inc(S("s0_t"), 1)
            for c in range(2):
                for t in range(4):
                    q = pe.transpose(B[2 + c][:, t * 120:(t + 1) * 120], harow[:, c, t * P:(t + 1) * P],
                                     ident[0:120, 0:120])
                q.then_inc(S("s0_t"), 1)
            pe.wait_ge(*at("s0_turned", 17))
            for t in range(12):
                q = pe.transpose(B[4][:, t * 24:(t + 1) * 24], hcrow[:, t * P:(t + 1) * P], ident[0:24, 0:24])
            q.then_inc(S("s0_t"), 1)
            pe.wait_ge(*at("ssq_done", 1))
            mm(B[7][:, 0:T], ones[:, :], ssq[:, :]).then_inc(S("sum_mm"), 1)
            pe.wait_ge(*at("wdt_loaded", 16))
            pe.wait_ge(*at("norm_v", 1))
            for k in range(KT):
                pe.wait_ge(*at("hmix", k + 1))
                q = mm(B[7][0:NH, 0:T], wdt[:, k, :], hT[:, k, :], k == 0, k == KT - 1)
            q.then_inc(S("dt_mm"), 1)
            pe.wait_ge(*at("s0_turned", 21))

            def in_group(g, hook):
                for s in range(8):
                    sl = 8 * g + s
                    wait_raw(pe, sl // 4, sl % 4)
                    w = slab_dst(sl % 4, GW)
                    for m in range(GM):
                        if s == 0 and g > 0:
                            pe.wait_ge(*at("in_read", 4 * (g - 1) + m + 1))
                        for kk in range(2):
                            q = mm(B[m][:, 0:T], w[:, kk, m * P:(m + 1) * P], hT[:, 2 * s + kk, :],
                                   s == 0 and kk == 0, s == 7 and kk == 1)
                        if s == 7:
                            q.then_inc(S("in_acc"), 1)
                    if s < 7:
                        q.then_inc(S("in_slab"), 1)
                    hook(8 * g + s)

            def s5_lhs(i, j):
                r = 32 * (j % 4)
                return bT[r:r + 32, i, j // 4, :], r

            def s5_in(j):
                if j >= 2:
                    pe.wait_ge(*at("s5_turned", 2 * (j - 1)))
                else:
                    pe.wait_ge(*at("s5_bus", 4))
                for i in range(2):
                    l, r = s5_lhs(i, j)
                    q = pe.matmul(B[4 + j % 2][:, i * NP:(i + 1) * NP], lhsT=l, rhs=uT[r:r + 32, j // 4, 0:NP],
                                  start=True, stop=True, tile_position=(r, 0))
                q.then_inc(S("s5_in"), 1)

            def s5_out(j):
                jt, r = j // 4, 32 * (j % 4)
                bk = B[6 + jt % 2]
                if j % 4 == 0 and jt >= 2:
                    pe.wait_ge(*at("s5_yd", jt - 1))
                if j == 0:
                    pe.wait_ge(*at("s5_bus", 4))
                    pe.wait_ge(*at("s5_hs", 1))
                for i in range(2):
                    pe.wait_ge(*at("s5_h", 2 * j + i + 1))
                    q = pe.matmul(bk[r:r + 32, 0:NP], lhsT=cT[:, i, jt, r:r + 32], rhs=hri[:, j % 2, i, :],
                                  start=i == 0, stop=i == 1, tile_position=(0, r))
                q.then_inc(S("s5_h_used"), 1)
                for i in range(2):
                    q = pe.matmul(bk[r:r + 32, NP:T], lhsT=cT[:, i, jt, r:r + 32], rhs=hsr[:, i, j, :],
                                  start=i == 0, stop=i == 1, tile_position=(0, r))
                if j % 4 == 3:
                    q.then_inc(S("s5_y"), 1)

            def conf_sum(name, src, bk):
                for t in range(4):
                    pe.wait_ge(*at(name, t + 1))
                    q = mm(B[bk][:, 0:T], ones[:, :], src[:, t, :], t == 0, t == 3)
                q.then_inc(S("conf_mm"), 1)

            def hook_in(x):
                if x == 5:
                    pe.wait_ge(*at("bc_padded", 4))
                    pe.wait_ge(*at("dt_read", 1))
                    for i in range(4):
                        for t in range(4):
                            src = bpad[:, i, 4 * t:4 * t + 4, :].rearrange("p a b -> p (a b)") if i < 2 \
                                else cpad[:, i - 2, t, :, :].rearrange("p a b -> p (a b)")
                            q = pe.transpose(B[4 + i][:, t * P:(t + 1) * P], src, ident[:, :])
                        q.then_inc(S("s0_t"), 1)
                if x == 9:
                    pe.wait_ge(*at("s0_turned", 25))
                    pe.wait_ge(*at("in_read", 4))
                    for r in range(4):
                        for i in range(2):
                            for jt in range(4):
                                l, row = s5_lhs(i, 4 * jt + r)
                                c0 = (4 * i + jt) * NS
                                q = pe.matmul(B[4 + r][:, c0:c0 + NS], lhsT=l, rhs=uT[row:row + 32, jt, NP:T],
                                              start=True, stop=True, tile_position=(row, 0))
                        q.then_inc(S("s5_bus_mm"), 1)
                if 16 <= x < 16 + SJ:
                    s5_in(x - 16)
                if 20 <= x < 20 + SJ:
                    s5_out(x - 20)

            for g in range(8):
                in_group(g, hook_in)

            for k in range(KT):
                bk = B[6 + (k // 2) % 2]
                if k % 2 == 0 and k >= 4:
                    pe.wait_ge(*at("memT", k - 2))
                if k == 0:
                    pe.wait_ge(*at("memn", 2))
                    pe.wait_ge(*at("s5_yd", 4))
                for t in range(MT):
                    q = pe.transpose(bk[:, (k % 2) * NM + t * P:(k % 2) * NM + (t + 1) * P],
                                     mtok[:, t, k * P:(k + 1) * P], ident[:, :])
                if k % 2:
                    q.then_inc(S("mem_t"), 1)

            pe.wait_ge(*at("compact", 2))
            for t in range(4):
                pe.transpose(B[4][0:HA, t * P:(t + 1) * P], up[:, t, UP - HA:UP], ident[:, :])
            for t in range(4):
                q = pe.transpose(B[5][0:NS, t * P:(t + 1) * P], new_a[:, t * NS:(t + 1) * NS], ident[:, :])
            q.then_inc(S("ex_mm"), 1)
            for r in range(3):
                pe.wait_ge(*at("ex_read", 2 * r + 2))
                for t in range(4):
                    pe.transpose(B[4][0:HC, t * P:(t + 1) * P], xbr[:, 4 * r + t, XP - HC:XP], ident[:, :])
                for t in range(4):
                    q = pe.transpose(B[5][0:NB * HC, t * P:(t + 1) * P],
                                     new_c[:, (4 * r + t) * 24:(4 * r + t + 1) * 24], ident[:, :])
                q.then_inc(S("ex_mm"), 1)
            pe.wait_ge(*at("ex_read", 8))
            pe.wait_ge(*at("s5_fin", 2))
            for i in range(2):
                pe.transpose(B[4][0:SJ, i * P:(i + 1) * P], fin[:, i, :], ident[:, :])
            for i in range(2):
                q = pe.transpose(B[5][:, i * P:(i + 1) * P], s0s[:, i, :], ident[:, :])
            q.then_inc(S("ex_mm"), 1)

            for m in range(4):
                if m == 0:
                    pe.wait_ge(*at("glu_loaded", 16))
                    pe.wait_ge(*at("ex_read", 10))
                bk = B[4 + m % 2]
                if m >= 2:
                    pe.wait_ge(*at("s5_gate", m - 1))
                for k in range(4):
                    if m == 0:
                        pe.wait_ge(*at("s5_gelu", k + 1))
                    q = mm(bk[:, 0:T], glu_w[:, k, m * P:(m + 1) * P], uT[:, k, :], k == 0, k == 3)
                q.then_inc(S("glu_mm"), 1)

            pe.wait_ge(*at("memT", KT))
            conf_sum("conv_a", va, 6)
            conf_sum("conf_sq", th, 7)

            pe.wait_ge(*at("dt_rows", 1))
            pe.wait_ge(*at("s5_gate", 4))
            for q3 in range(3):
                for c in range(3):
                    w = P if c < 2 else NS
                    q = pe.transpose(B[4][0:w, (q3 * 3 + c) * NH:(q3 * 3 + c + 1) * NH],
                                     dtr[:, q3, c * P:c * P + w], ident[0:NH, 0:NH])
            q = mm(B[4][:, 256:256 + NH], ones[0:NH, :], diag[:, :])
            q.then_inc(S("tok_mm"), 1)
            for c in range(3):
                w = P if c < 2 else NS
                pe.wait_ge(*at("conv_c", 12))
                for hf in range(2):
                    bk = B[2 + hf]
                    if c == 0:
                        pe.wait_ge(*at("in_read", 32))
                    else:
                        pe.wait_ge(*at("xdt", 2 * (c - 1) + hf + 1))
                    for t in range(4):
                        q = pe.transpose(bk[0:w, t * P:(t + 1) * P], xc[:, 4 * hf + t, c * P:c * P + w], ident[:, :])
                    q.then_inc(S("x_t"), 1)
                bk = B[5]
                if c > 0:
                    pe.wait_ge(*at("btok", c))
                for g in range(2):
                    q = pe.transpose(bk[0:w, g * P:(g + 1) * P], xc[:, 8 + g, c * P:c * P + w], ident[:, :])
                q.then_inc(S("b_t"), 1)
            pe.wait_ge(*at("conf_read", 1))
            for c in range(2):
                for g in range(2):
                    mm(B[6][:, (2 * c + g) * P:(2 * c + g + 1) * P], xc[:, 8 + g, c * P:(c + 1) * P],
                       xc[:, 10 + g, c * P:(c + 1) * P])
            for g in range(2):
                q = mm(B[7][0:NS, g * NS:(g + 1) * NS], xc[:, 8 + g, NP:T], xc[:, 10 + g, NP:T])
            q.then_inc(S("cb_mm"), 1)
            for c in range(2):
                pe.wait_ge(*at("xds", c + 1))
                pe.wait_ge(*at("btok", 3))
                if c == 0:
                    pe.wait_ge(*at("xdt", 6))
                else:
                    pe.wait_ge(*at("st_read", 2))
                for g in range(2):
                    q = mm(B[2 + g][:, :], btok[:, c, g, :], xds[:, g * 512:(g + 1) * 512])
                q.then_inc(S("st_mm"), 1)
            pe.wait_ge(*at("st_read", 4))
            for j in range(YT):
                q = pe.transpose(B[2 + j // 4][:, (j % 4) * P:(j % 4 + 1) * P], xds[:, j * P:(j + 1) * P], ident[:, :])
            q.then_inc(S("st_mm"), 1)

            def kv_group(g):
                for s in range(8):
                    sl = NA + 8 * g + s
                    wait_raw(pe, sl // 4, sl % 4)
                    w = slab_dst(sl % 4, GW)
                    for t in range(MT):
                        if s == 0 and g > 0:
                            pe.wait_ge(*at("kv_read", 2 * (g - 1) + t + 1))
                        if s == 0 and g == 0:
                            pe.wait_ge(*at("in_read", 32))
                        for kk in range(2):
                            if g == 0 and t == 0:
                                pe.wait_ge(*at("memT", 2 * s + kk + 1))
                            q = mm(B[t][:, :], memT[:, 2 * s + kk, t * P:(t + 1) * P], w[:, kk, :],
                                   s == 0 and kk == 0, s == 7 and kk == 1)
                        if s == 7:
                            q.then_inc(S("kv_acc"), 1)
                    if s < 7:
                        q.then_inc(S("kv_slab"), 1)

            def k_turn(g):
                for i in range(2):
                    pe.wait_ge(*at("kv_read", 2 * g + 2))
                    if i == 0:
                        pe.wait_ge(*at("upd_read", 2 * g + 2))
                    for d in range(2):
                        for t in range(MT):
                            c0 = g * GW + (2 * i + d) * P
                            q = pe.transpose(B[6 + i][:, d * NM + t * P:d * NM + (t + 1) * P],
                                             vtok[:, t, c0:c0 + P], ident[:, :])
                    q.then_inc(S("k_t"), 1)

            def head_bcast(h, n=P):
                return ident[0:NH, h:h + 1].to_broadcast([NH, n])

            def ssd_a(j):
                for h in range(2):
                    if j > 0:
                        pe.wait_ge(*at("seg", 6 * (j - 1) + 3 * h + 3))
                    elif h == 0:
                        pe.wait_ge(*at("st_out", 1))
                    mm(B[2 + h][:, 0:T], head_bcast(2 * j + h), R_CS).then_inc(S("abc"), 1)
                if j > 0:
                    pe.wait_ge(*at("yo_read", j))
                else:
                    pe.wait_ge(*at("tok_read", 3))
                for h in range(2):
                    q = pe.matmul(B[4][HP * h:HP * (h + 1), 0:P + NS], lhsT=head_bcast(2 * j + h, HP),
                                  rhs=R_CS[:, P:T], start=True, stop=True, tile_position=(0, HP * h))
                q.then_inc(S("ebc"), 1)
                pe.wait_ge(*at(f"s0_loaded{j % 2}", 16 * (j // 2 + 1)))
                if j > 0:
                    pe.wait_ge(*at("kT_read" if j <= 4 else "upd_read", 2 * j))
                else:
                    pe.wait_ge(*at("cb_read", 2))
                for b in range(NB):
                    q = pe.transpose(B[6 + b // 4][:, (b % 4) * P:(b % 4 + 1) * P], s0[:, j % 2, b, :], ident[:, :])
                    if b % 4 == 3:
                        q.then_inc(S("s0_t_mm"), 1)

            def ssd_b(j):
                g = j // 4
                if j > 0:
                    pe.wait_ge(*at("gated", j))
                else:
                    pe.wait_ge(*at("btok", 3))
                for h in range(2):
                    hd = 2 * j + h
                    r = HP * h
                    pe.wait_ge(*at("mixed", 4 * j + 2 * h + 2))
                    for c in range(2):
                        pe.matmul(B[5][r:r + HP, c * P:(c + 1) * P], lhsT=xdt[:, c, hd * HP:(hd + 1) * HP],
                                  rhs=dec[:, h, c * P:(c + 1) * P], start=True, stop=True, tile_position=(0, r))
                    q = pe.matmul(B[5][r:r + HP, NP:T], lhsT=xdt[0:NS, 2, hd * HP:(hd + 1) * HP],
                                  rhs=decs[:, h, :], start=True, stop=True, tile_position=(0, r))
                    q.then_inc(S("y_mm"), 1)
                pe.wait_ge(*at("eb_ready", j + 1))
                pe.wait_ge(*at("s0_T", 2 * j + 2))
                mm(B[4][:, 256:256 + P], pvT[:, j * P:(j + 1) * P], xc[:, 10 + g, P:NP])
                for b in range(NB):
                    q = mm(B[4][:, 384 + NL * b:384 + NL * (b + 1)], s0T[:, b, :],
                           xc[:, 10 + g, NP + NL * b:NP + NL * (b + 1)])
                q.then_inc(S("yo_mm"), 1)
                pe.wait_ge(*at("masked_b", g + 1))
                for i in range(2):
                    q = mm(B[6 + i][:, :], xds[0:NS, j * P:(j + 1) * P],
                           bm[:, 4 * i:4 * i + 4, :].rearrange("p b n -> p (b n)"))
                q.then_inc(S("upd_mm"), 1)

            pe.wait_ge(*at("xds", 3))
            for j in range(8):
                ssd_a(j)
                kv_group(j)
                ssd_b(j)
                if j < 4:
                    k_turn(j)

            for g in range(2):
                pe.wait_ge(*at("gate_sq", g + 1))
                if g == 0:
                    pe.wait_ge(*at("seg", 48))
                mm(B[2 + g][:, 0:T], ones[:, :], (ssq if g == 0 else sqt)[:, :]).then_inc(S("gate_mm"), 1)

            def split_mm(out, wslot, wo, xh, xl, first, last):
                pe.matmul(out, lhsT=whi[:, wslot, wo:wo + P], rhs=xh, start=first, stop=False)
                pe.matmul(out, lhsT=whi[:, wslot, wo:wo + P], rhs=xl, start=False, stop=False)
                return pe.matmul(out, lhsT=wlo[:, wslot, wo:wo + P], rhs=xh, start=False, stop=last)

            def split_group(g, bank0, bank_free, ready, width=GW, between=None):
                for s in range(8):
                    pe.wait_ge(*at("w_lo", 8 * g + (s + 1)))
                    for m in range(width // P):
                        if s == 0:
                            bank_free(m)
                        for kk in range(2):
                            if m == 0:
                                ready(2 * s + kk)
                            k = 2 * s + kk
                            q = split_mm(B[bank0 + m][:, 0:T], s % 2, kk * width + m * P, hhi[:, k, :], hlo[:, k, :],
                                         s == 0 and kk == 0, s == 7 and kk == 1)
                        if s == 7:
                            q.then_inc(S("b_acc"), 1)
                    if s < 7:
                        q.then_inc(S("b_slab"), 1)
                    if between:
                        between(s)

            def never(_):
                pass

            def four_groups(g0, before, read, ready, between=None):
                split_group(g0, 0, before, ready, between=between)
                with pe.Fori(1, 3) as i:
                    split_group(g0 + i, 0, lambda m: pe.wait_ge(*at(read, 4 * i + (m - 3))), never)
                split_group(g0 + 3, 4, never, never)

            def mean_square(n):
                def after(s):
                    if s == 4:
                        pe.wait_ge(*at("ssq_done", n + 1))
                        mm(B[4][:, 0:T], ones[:, :], ssq[:, :]).then_inc(S("sum_mm"), 1)
                return after

            def ready_cat(k):
                name, n = ("cat_a", k + 1) if k < 4 else ("cat_b", k - 3) if k < 8 else ("cat_c", k - 7)
                pe.wait_ge(*at(name, n))

            def before_out(m):
                pe.wait_ge(*at("kv_read", 16))
                pe.wait_ge(*at("gate_read", 2))
            four_groups(G_OUT, before_out, "x_out", ready_cat)
            four_groups(G_Q, lambda m: pe.wait_ge(*at("x_out", 9 + m)), "q_read",
                        lambda k: pe.wait_ge(*at("hxa", k + 1)), mean_square(1))

            pe.wait_ge(*at("q_read", 16))
            def scores(n):
                h, l = divmod(n, 2)
                if n >= 2:
                    pe.wait_ge(*at("p_exp", n - 1))
                for d in range(4):
                    q = mm(B[n % 2][:, 0:NM], qT[:, 4 * h + d, l * P:(l + 1) * P], kT[:, 4 * h + d, :],
                           d == 0, d == 3)
                q.then_inc(S("scores"), 1)

            def p_turn(n):
                pe.wait_ge(*at("p_norm", n + 1))
                if n >= 2:
                    pe.wait_ge(*at("pT", n - 1))
                for t in range(MT):
                    q = pe.transpose(B[2 + n % 2][:, t * P:(t + 1) * P], pr[:, n % 2, t * P:(t + 1) * P], ident[:, :])
                q.then_inc(S("p_t"), 1)

            def p_values(n):
                h, l = divmod(n, 2)
                pe.wait_ge(*at("pT", n + 1))
                if n >= 2:
                    pe.wait_ge(*at("o_lo", n - 1))
                for d in range(4):
                    for t in range(MT):
                        c0 = (4 * h + d) * P
                        q = mm(B[4 + n % 2][:, d * P:(d + 1) * P], vtok[:, t, c0:c0 + P], pT[:, n % 2, t, :],
                               t == 0, t == MT - 1)
                q.then_inc(S("pv"), 1)

            def turn_k(u):
                b, h = divmod(u, XH)
                if h == 0:
                    pe.wait_ge(*at(f"kv_loaded{b % 2}", 16 * (b // 2 + 1)))
                if u >= 2:
                    pe.wait_ge(*at("kc_lo", 2 * (u - 1)))
                for i in range(2):
                    for d in range(2):
                        for t in range(MT):
                            c0 = (4 * h + 2 * i + d) * P
                            q = pe.transpose(B[4 + 2 * (u % 2) + i][:, d * NM + t * P:d * NM + (t + 1) * P],
                                             kv[:, b % 2, t, c0:c0 + P], ident[:, :])
                    q.then_inc(S("kc_t"), 1)

            def sample_scores(u):
                b, h = divmod(u, XH)
                pe.wait_ge(*at("kc_lo", 2 * u + 2))
                if h == 0 and b >= 2:
                    pe.wait_ge(*at("s_kept", b - 1))
                for d in range(4):
                    k = 4 * h + d
                    q = padded_mm(B[b % 2][:, 0:NM], (qs_hi[:, k, :, :], qs_lo[:, k, :, :]),
                                  (kc_hi[:, u % 2, d, :], kc_lo[:, u % 2, d, :]), k == 0, k == KT - 1)
                q.then_inc(S("s_scores"), 1)

            def padded_mm(out, left, right, first, last):
                left = [x.rearrange("p h t -> p (h t)") for x in left]
                pe.matmul(out, lhsT=left[0], rhs=right[0], start=first, stop=False)
                pe.matmul(out, lhsT=left[0], rhs=right[1], start=False, stop=False)
                return pe.matmul(out, lhsT=left[1], rhs=right[0], start=False, stop=last)

            scores(0)
            for n in range(8):
                if n < 7:
                    scores(n + 1)
                p_turn(n)
                p_values(n)
            pe.wait_ge(*at("p_exp", 8))
            pe.wait_ge(*at("o_lo", 8))
            pe.wait_ge(*at("qs_lo", 4))
            for u in range(NB * XH + 1):
                if u < NB * XH:
                    turn_k(u)
                if u > 0:
                    sample_scores(u - 1)
            pe.wait_ge(*at("ps_norm", 1))
            pe.wait_ge(*at("pT", 8))
            for t in range(MT):
                q = pe.transpose(B[4][:, t * P:(t + 1) * P], prs[:, t * P:(t + 1) * P], ident[:, :])
            q.then_inc(S("ps_t"), 1)
            pe.wait_ge(*at("pTs_lo", 4))
            for b in range(NB):
                for h in range(XH):
                    n = XH * b + h
                    pe.wait_ge(*at("v_lo", n + 1))
                    if h == 0 and b >= 2:
                        pe.wait_ge(*at("o_kept", b - 1))
                    for t in range(MT):
                        c0 = t * XD
                        q = padded_mm(B[2 + b % 2][:, 0:XD], (pTs_hi[:, t, h, :, :], pTs_lo[:, t, h, :, :]),
                                      (whi[:, n % 2, c0:c0 + XD], wlo[:, n % 2, c0:c0 + XD]),
                                      h == 0 and t == 0, h == XH - 1 and t == MT - 1)
                    q.then_inc(S("pv_sample"), 1)
            pe.wait_ge(*at("o_kept", NB))
            for d in range(4):
                q = pe.transpose(B[4][:, d * P:(d + 1) * P], osum[:, d * P:(d + 1) * P], ident[:, :])
            q.then_inc(S("os_t"), 1)

            def ready_o(k):
                pe.wait_ge(*at("os_lo", 1))
            def ff_columns(s):
                if s != 4:
                    return
                pe.wait_ge(*at("ff_rows", 16 * 4))
                for i in range(2):
                    q = pe.transpose(B[5][:, i * 86:(i + 1) * 86], frow[:, i, :], ident[0:86, 0:86])
                q.then_inc(S("ff_t"), 1)
                for r in range(2):
                    lo, hi_ = (0, 32) if r == 0 else (32, FT)
                    for t in range(lo, hi_):
                        q = pe.transpose(B[6 + r][:, (t - lo) * 16:(t - lo + 1) * 16], fhrow[:, t * P:(t + 1) * P],
                                         ident[0:16, 0:16])
                    q.then_inc(S("ff_t"), 1)
            four_groups(G_O, never, "x_o", lambda k: ready_o(k) if k == 0 else None, ff_columns)

            def before_up(m):
                pe.wait_ge(*at("ff_cols", 3))
                pe.wait_ge(*at("norm_v", 3))
            split_group(G_FF, 0, lambda m: pe.wait_ge(*at("x_o", 9 + m)), lambda k: pe.wait_ge(*at("hffn", k + 1)),
                        between=mean_square(2))
            split_group(G_FF + 1, 4, before_up, never)
            with pe.Fori(1, FPAIRS) as i:
                split_group(G_FF + 2 * i, 0, lambda m: pe.wait_ge(*at("g_read", 4 * i + (m - 3))), never)
                split_group(G_FF + 1 + 2 * i, 4, lambda m: pe.wait_ge(*at("act", 4 * i + (m - 3))), never)
            split_group(G_FF + 2 * FPAIRS, 0, lambda m: pe.wait_ge(*at("g_read", 4 * FPAIRS + m - 3)), never, FTAIL * P)
            split_group(G_FF + 1 + 2 * FPAIRS, 4, lambda m: pe.wait_ge(*at("act", 4 * FPAIRS + m - 3)), never, FTAIL * P)

            pe.wait_ge(*at("act", FT))
            for r in range(11):
                if r >= 8:
                    pe.wait_ge(*at("fx_read", r - 7))
                for t in range(4 * r, min(4 * r + 4, FT)):
                    q = pe.transpose(B[r % 8][0:18, (t % 4) * P:(t % 4 + 1) * P], gcol[:, t, :], ident[:, :])
                q.then_inc(S("fx_t"), 1)

            pe.wait_ge(*at("fx_read", 11))
            for half in range(2):
                base = half * FT

                def down(f, j, first, last):
                    pe.wait_ge(*at("w_lo", NB_DOWN + base + f + 1))
                    pe.wait_ge(*at("a_lo", base + f + 1))
                    slot = (NB_DOWN + base + j) % 2
                    for m in range(DG):
                        if first and half == 1:
                            pe.wait_ge(*at("x_down", m + 1))
                        q = split_mm(B[m][:, 0:T], slot, m * P, ahi[:, slot, :], alo[:, slot, :], first, last)
                    q.then_inc(S("d_slab"), 1)

                for j in range(4):
                    down(j, j, j == 0, False)
                with pe.Fori(1, FT // 4) as i:
                    for j in range(4):
                        down(4 * i + j, j, False, False)
                for j in range(FT % 4):
                    f = FT - FT % 4 + j
                    down(f, j, False, f == FT - 1)

            pe.wait_ge(*at("ssq_done", 4))
            mm(B[0][:, 0:T], ones[:, :], ssq[:, :]).then_inc(S("sum_mm"), 1)
            pe.wait_ge(*at("x_down", 16))
            pe.wait_ge(*at("norm_v", 4))
            for k in range(KT):
                pe.wait_ge(*at("hfin", k + 1))
                set_ = (k // 4) % 2
                if k % 4 == 0 and k >= 8:
                    pe.wait_ge(*at("y_read", 3 * (k // 4 - 1)))
                for t in range(3):
                    w = P if t < 2 else NS
                    q = pe.transpose(B[1 + 3 * set_ + t][0:w, (k % 4) * P:(k % 4 + 1) * P],
                                     fT[:, k, t * P:t * P + w], ident[:, :])
                    if k % 4 == 3 and t == 2:
                        q.then_inc(S("y_t"), 1)



        @block.scalar
        def _(sc_):
            a = sc_.activation
            me = Own(sc_, S("act_step"))

            def row_load(dst, src):
                sc_.dma_start(dst, src).then_inc(S("rows_loaded"), 16)

            def tiles(ap):
                return ap.rearrange("(k p) -> k p", p=P)
            for i, name in enumerate(("norm_mix_w", "norm_xa_w", "norm_mem_w", "norm_ffn_w")):
                row_load(rows[16 * i:16 * i + 16, 0, :], tiles(I[name][0]))
            row_load(rows[64:80, 0, :], tiles(I["final_norm_w"]))
            for i, name in enumerate(("conv_a_b", "ln_a_w", "ln_a_b", "s5_d", "s5_glu_b")):
                row_load(rows[80 + 4 * i:84 + 4 * i, 0, :], tiles(I[name][0]))
            row_load(rows[100:108, 0, :], tiles(I["ssd_norm_w"][0]))
            row_load(rows[108:120, 0, :], tiles(I["conv_c_b"][0]))
            row_load(rows[0:16, 1, :], I["s5_lam_re"][0].rearrange("(j a) p -> j (a p)", a=2))
            row_load(rows[16:32, 1, :], I["s5_lam_im"][0].rearrange("(j a) p -> j (a p)", a=2))
            row_load(pairs[32:48, :], I["s5_log_dt"][0].rearrange("(j a) -> j a", a=2))
            row_load(rows[48:96, 1, :], I["conv_c_w"][0].rearrange("w (t p) -> (w t) p", p=P))
            row_load(pairs[96:104, :], I["ssd_d"][0].rearrange("(j a) -> j a", a=2))
            row_load(rows[0:124, 2, :], I["conv_a_w"][0].rearrange("w (t p) -> (w t) p", p=P))
            sc_.dma_start(hcol[:, 0:1], I["ssd_a_log"][0].unsqueeze(1)).then_inc(S("hcol_loaded"), 16)
            sc_.dma_start(hcol[:, 1:2], I["ssd_dt_bias"][0].unsqueeze(1)).then_inc(S("hcol_loaded"), 16)

            def hist_load(dst, src):
                sc_.dma_start(dst, src).then_inc(S("hist_loaded"), 16)
            for i, name in enumerate(("state_s5_re", "state_s5_im")):
                hist_load(srow[:, i, :], I[name][0].rearrange("b (j a) p -> (b j) (a p)", a=2))
            conv_a_rows = I["state_conv_a"][0].rearrange("b r c -> (b r) c")
            for c in range(2):
                hist_load(harow[:, c, :], conv_a_rows[c * 120:(c + 1) * 120, :])
            hist_load(hcrow[:, :], I["state_conv_c"][0].rearrange("b r c -> (b r) c"))
            for i, name in enumerate(("s5_b_re", "s5_b_im")):
                hist_load(brow[:, i, :, :], I[name][0].rearrange("(j a) p h -> (a p) j h", a=2))
            for i, name in enumerate(("s5_c_re", "s5_c_im")):
                hist_load(crow[:, i, :, :], I[name][0].rearrange("g h p -> (g h) p").rearrange("(t q) p -> q t p", q=P))
            sc_.dma_start(O["s_conv_a"][0][:, 0:HA - NL, :], I["state_conv_a"][0][:, NL:HA, :])\
               .then_inc(S("st_conv_a_old"), 16)

            def root(n):
                sc_.wait_ge(*at("norm_v", n + 1))
                a(rstd[:, :], rstd[:, :], ACT.Sqrt).then_inc(S("norm_s"), 1)
            root(0)
            sc_.wait_ge(*at("s0_turned", 1))
            a(sc[:, 0, :], prm[:, C_LDT:C_LDT + SJ], ACT.Exp).then_inc(S("s5_exp"), 1)
            sc_.wait_ge(*at("s5_arg", 1))
            a(sc[:, 14, :], sc[:, 1, :], ACT.Exp).then_inc(S("s5_exp"), 1)
            sc_.wait_ge(*at("s5_arg", 2))
            a(sc[:, 6, :], sc[:, 4, :], ACT.Sin, scale=0.5).then_inc(S("s5_sin"), 1)
            a(sc[:, 7, :], sc[:, 5, :], ACT.Sin).then_inc(S("s5_sin"), 1)
            sc_.wait_ge(*at("hcol_loaded", 32))
            a(hcol[:, 2:3], hcol[:, 0:1], ACT.Exp).then_inc(S("dt_act"), 1)
            sc_.wait_ge(*at("dt_dve", 1))
            a(R_EXP, R_EXP, ACT.Exp).then_inc(S("dt_act"), 1)
            sc_.wait_ge(*at("dt_dve", 2))
            a(R_LN, R_W, ACT.Ln).then_inc(S("dt_act"), 1)
            sc_.wait_ge(*at("dt_dve", 3))
            a(R_END, R_END, ACT.Exp).then_inc(S("dt_act"), 1)
            a(hcol[:, 3:4], R_CS[:, NP - 1:NP], ACT.Exp).then_inc(S("dt_act"), 1)

            def in_evac(g):
                for m in range(GM):
                    sc_.wait_ge(*at("in_acc", 4 * g + m + 1))
                    bk = B[m]
                    bs = vsplit(bk[:, NP:T], NB)
                    if g == 0:
                        q = a(uT[:, m, :], bk[:, 0:T], ACT.Copy)
                    elif g == 1:
                        q = a(va[:, m, :], bk[:, 0:T], ACT.Copy, scale=0.5)
                    elif g == 2:
                        q = a(th[:, m, :], bk[:, 0:T], ACT.Tanh, scale=0.5)
                    elif g < 6:
                        t = 4 * (g - 3) + m
                        a(xbr[:, t, HC:XP], bk[:, 0:NP], ACT.Copy)
                        q = a(xbr_sample(t)[:, :, HC:XS], bs, ACT.Copy)
                    else:
                        q = a(zs[:, 4 * (g - 6) + m, :], bk[:, 0:T], ACT.Silu)
                    q.then_inc(S("in_read"), 1)

            in_evac(0)
            for r in range(4):
                sc_.wait_ge(*at("s5_bus_mm", r + 1))
                a(hsr[:, :, :, :].rearrange("p i (a r) n -> p i a r n", r=4)[:, :, :, r, :],
                  B[4 + r][:, 0:8 * NS].rearrange("p (i a n) -> p i a n", i=2, a=4), ACT.Copy)\
                    .then_inc(S("s5_bus"), 1)
            sc_.wait_ge(*at("mem_loaded", 32))
            for t in range(MT):
                a(zs[:, :, :].rearrange("p a b -> p (a b)")[:, 0:D], mtok[:, t, :], ACT.Square,
                  accum_out=msum[:, t:t + 1]).then_inc(S("mem_sq"), 1)
                sc_.wait_ge(*at("mem_sq", t + 1))
            sc_.wait_ge(*at("mem_v", 1))
            a(msum[:, 2:4], msum[:, 2:4], ACT.Sqrt).then_inc(S("mem_s"), 1)
            sc_.wait_ge(*at("mem_v", 2))
            for t in range(MT):
                a(mtok[:, t, :], mtok[:, t, :], ACT.Copy, scale=msum[:, 4 + t:5 + t]).then_inc(S("memn"), 1)
            in_evac(1)
            in_evac(2)
            in_evac(3)

            def first_tap(dst, dst_s, src, src_s, w, b, name):
                a(dst, src, ACT.Identity, scale=w, bias=b).then_inc(S(name), 1)
                a(dst_s, src_s, ACT.Identity, scale=w, bias=b).then_inc(S(name), 1)

            for t in range(4):
                sc_.wait_ge(*at("u_done", 2 * t + 2))
                first_tap(va[:, t, 0:NP], vsplit(va[:, t, NP:T], NB), up[:, t, 0:NP], up_sample(t)[:, :, 0:NL],
                          col(C_CAW + t), col(C_CAB + t), "tap_a")
            in_evac(4)
            in_evac(5)
            for t in range(12):
                sc_.wait_ge(*at("in_read", 12 + t + 1))
                sc_.wait_ge(*at("s0_turned", 21))
                first_tap(xc[:, t, 0:NP], vsplit(xc[:, t, NP:T], NB), xbr[:, t, 0:NP], xbr_sample(t)[:, :, 0:NL],
                          col(C_CCW + t), col(C_CCB + t), "tap_c")
            in_evac(6)
            in_evac(7)
            for t in range(12):
                sc_.wait_ge(*at("conv_c_taps", t + 1))
                a(xc[:, t, :], xc[:, t, :], ACT.Silu).then_inc(S("conv_c"), 1)
            for t in range(4):
                sc_.wait_ge(*at("s5_yd", t + 1))
                a(uT[:, t, :], uT[:, t, :], ACT.Gelu_apprx_tanh).then_inc(S("s5_gelu"), 1)
            sc_.wait_ge(*at("s5_h", 2 * SJ))
            sc_.dma_start(glu_w[:, :, :], I["s5_glu_w"][0].rearrange("(k p) n -> p k n", p=P))\
               .then_inc(S("glu_loaded"), 16)
            for k in range(KT):
                sc_.wait_ge(*at("mem_t", k // 2 + 1))
                a(memT[:, k, :], B[6 + (k // 2) % 2][:, (k % 2) * NM:(k % 2 + 1) * NM], ACT.Copy,
                  scale=col(C_MEM + k)).then_inc(S("memT"), 1)
            sc_.wait_ge(*at("s5_h_used", SJ))
            sc_.wait_ge(*at("s5_fin", 2))
            sc_.wait_ge(*at("u_done", 8))
            a(new_a.rearrange("p (t b l) -> p t b l", t=4, b=NB),
              up[:, :, UP:UP + NB * US].rearrange("p t (b w) -> p t b w", w=US)[:, :, :, HA:US], ACT.Copy)\
                .then_inc(S("compact"), 1)
            a(new_c.rearrange("p (t b l) -> p t b l", t=12, b=NB),
              xbr[:, :, XP:XP + NB * XS].rearrange("p t (b w) -> p t b w", w=XS)[:, :, :, XS - HC:XS], ACT.Copy)\
                .then_inc(S("compact"), 1)
            for r in range(4):
                sc_.wait_ge(*at("ex_mm", r + 1))
                if r:
                    sc_.wait_ge(*at("st_conv_a" if r == 1 else "st_conv_c", 32 if r == 1 else 32 * (r - 1)))
                n_p, n_s = (HA, NS) if r == 0 else (HC, NB * HC)
                a(exa[0:n_p, 0, :], B[4][0:n_p, :], ACT.Copy).then_inc(S("ex_read"), 1)
                a(exa[0:n_s, 1, :], B[5][0:n_s, :], ACT.Copy).then_inc(S("ex_read"), 1)
                sc_.wait_ge(*at("ex_read", 2 * r + 2))
                if r == 0:
                    dst_p, dst_s, name = O["p_conv_a"][0, 0], O["s_conv_a"][0][:, HA - NL:HA, :], "st_conv_a"
                else:
                    cs = slice((r - 1) * 512, r * 512)
                    dst_p, dst_s, name = O["p_conv_c"][0, 0][:, cs], O["s_conv_c"][0][:, :, cs], "st_conv_c"
                sc_.dma_start(dst_p, exa[0:n_p, 0, :]).then_inc(S(name), 16)
                sc_.dma_start(dst_s, exa[0:n_s, 1, :]).then_inc(S(name), 16)
            sc_.wait_ge(*at("ex_mm", 5))
            sc_.wait_ge(*at("st_conv_c", 96))
            a(exa[0:SJ, 0, 0:256], B[4][0:SJ, 0:256], ACT.Copy).then_inc(S("ex_read"), 1)
            a(exa[:, 1, 0:256], B[5][:, 0:256], ACT.Copy).then_inc(S("ex_read"), 1)
            sc_.wait_ge(*at("ex_read", 10))
            for i, n_ in enumerate(("re", "im")):
                sc_.dma_start(O[f"p_s5_{n_}"][0, 0].rearrange("(j a) p -> j (a p)", a=2),
                              exa[0:SJ, 0, i * P:(i + 1) * P]).then_inc(S("st_s5"), 16)
                sc_.dma_start(O[f"s_s5_{n_}"][0].rearrange("b (j a) p -> (b j) (a p)", a=2),
                              exa[:, 1, i * P:(i + 1) * P]).then_inc(S("st_s5"), 16)

            for m in range(4):
                sc_.wait_ge(*at("glu_mm", m + 1))
                if m >= 2:
                    sc_.wait_ge(*at("cat_b", m - 1))
                a(hbuf[:, m % 2, :], B[4 + m % 2][:, 0:T], ACT.Tanh, scale=0.5, bias=gcol_b[:, m:m + 1])\
                    .then_inc(S("s5_gate"), 1)
                if m >= 1:
                    sc_.wait_ge(*at("gated_b", m))
                    a(hhi[:, 3 + m, :], hbuf[:, (m - 1) % 2, :], ACT.Copy, scale=0.5).then_inc(S("cat_b_hi"), 1)
            sc_.wait_ge(*at("gated_b", 4))
            a(hhi[:, 7, :], hbuf[:, 1, :], ACT.Copy, scale=0.5).then_inc(S("cat_b_hi"), 1)
            for t in range(4):
                sc_.wait_ge(*at("centred", t + 1))
                a(th[:, t, :], va[:, t, :], ACT.Square).then_inc(S("conf_sq"), 1)
            sc_.wait_ge(*at("conf_read", 1))
            a(rstd[:, :], rstd[:, :], ACT.Sqrt).then_inc(S("conf_s"), 1)
            for t in range(4):
                sc_.wait_ge(*at("conf_scaled", t + 1))
                a(va[:, t, :], va[:, t, :], ACT.Silu, bias=col(C_LNB + t)).then_inc(S("conf_silu"), 1)
            for t in range(4):
                sc_.wait_ge(*at("conf_silu", t + 1))
                a(hhi[:, t, :], va[:, t, :], ACT.Copy).then_inc(S("cat_a_hi"), 1)

            s0_src = I["state_ssd"][0].rearrange("b (j r) p n -> j (r p) b n", r=2)
            s0_dst = O["s_ssd"][0].rearrange("b (j r) p n -> j (r p) b n", r=2)
            sc_.wait_ge(*at("cat_a", 4))
            sc_.wait_ge(*at("cat_b", 4))
            sc_.wait_ge(*at("st_s5", 64))
            for j in range(2):
                sc_.dma_start(s0[:, j, :, :], s0_src[j]).then_inc(S(f"s0_loaded{j}"), 16)
            sc_.wait_ge(*at("st_out", 1))
            sc_.dma_start(O["p_ssd"][0, 0].rearrange("(j r) p n -> (r p) j n", r=2), s0T[:, :, :])\
               .then_inc(S("st_ssd_p"), 16)
            sc_.wait_ge(*at("st_ssd_p", 16))

            for j in range(8):
                for h in range(2):
                    sc_.wait_ge(*at("seg", 6 * j + 3 * h + 2))
                    a(dec[:, h, :], dec[:, h, :], ACT.Exp).then_inc(S("decay"), 1)
                    sc_.wait_ge(*at("seg", 6 * j + 3 * h + 3))
                    a(decs[:, h, :], decs[:, h, :], ACT.Exp).then_inc(S("decay"), 1)
                sc_.wait_ge(*at("ebc", j + 1))
                if j > 0:
                    sc_.wait_ge(*at("yo_read", j))
                    sc_.wait_ge(*at("s0_decayed", j))
                a(eb[:, :], B[4][:, 0:P + NS], ACT.Exp).then_inc(S("eb_ready"), 1)
                for i in range(2):
                    sc_.wait_ge(*at("s0_t_mm", 2 * j + i + 1))
                    if j > 0:
                        sc_.wait_ge(*at("yo_mm", j))
                    a(s0T[:, 4 * i:4 * i + 4, :], v3(B[6 + i][:, :], P), ACT.Copy).then_inc(S("s0_T"), 1)
                g = j
                if g == 4:
                    sc_.wait_ge(*at("st_kv", 16 * 8))
                if g >= 4:
                    sc_.wait_ge(*at("k_t", 2 * (g - 4) + 2))
                if g == 0:
                    sc_.wait_ge(*at("s5_h", 2 * SJ))
                for t in range(MT):
                    sc_.wait_ge(*at("kv_acc", 2 * g + t + 1))
                    part = vtok[:, t, (g % 4) * GW:(g % 4 + 1) * GW]
                    a(part, B[t][:, :], ACT.Copy).then_inc(S("kv_read"), 1)
                for t in range(MT):
                    sc_.wait_ge(*at("kv_read", 2 * g + t + 1))
                    part = vtok[:, t, (g % 4) * GW:(g % 4 + 1) * GW]
                    sc_.dma_start((O["p_mem_k"] if g < 4 else O["p_mem_v"])[0, 0][t * P:(t + 1) * P, g % 4, :], part)\
                       .then_inc(S("st_kv"), 16)
                sc_.wait_ge(*at("upd_read", 2 * j + 2))
                sc_.dma_start(s0_dst[j], s0[:, j % 2, :, :]).then_inc(S(f"st_ssd{j % 2}"), 16)
                if j + 2 < YT:
                    sc_.wait_ge(*at(f"st_ssd{j % 2}", 16 * (j // 2 + 1)))
                    sc_.dma_start(s0[:, j % 2, :, :], s0_src[j + 2]).then_inc(S(f"s0_loaded{j % 2}"), 16)
                if g < 4:
                    for i in range(2):
                        sc_.wait_ge(*at("k_t", 2 * g + i + 1))
                        a(kT[:, 4 * g + 2 * i:4 * g + 2 * i + 2, :], v3(B[6 + i][:, :], NM), ACT.Copy)\
                            .then_inc(S("kT_read"), 1)

            def split(g, s, width=GW):
                slot = s % 2
                wait_raw(sc_, NS_B // 4 + 2 * g + s // 4, s % 4)
                wait_used_B(sc_, g, s - 2)
                a(whi[:, slot, 0:2 * width], raw[:, s % 4, 0:2 * width], ACT.Copy).then_inc(S("w_hi"), 1)

            def root(n):
                sc_.wait_ge(*at("norm_v", n + 1))
                a(rstd[:, :], rstd[:, :], ACT.Sqrt).then_inc(S("norm_s"), 1)

            def groups_1_to_3(g0, after_slab):
                with sc_.Fori(1, 3) as i:
                    for s in range(8):
                        split(g0 + i, s)
                for s in range(8):
                    split(g0 + 3, s)
                    after_slab(s)

            def h_hi(w_col, x_name, k):
                sc_.wait_ge(*at(x_name, k + 1))
                a(hhi[:, k, :], xT[:, k, :], ACT.Copy, scale=col(w_col + k)).then_inc(S("h_hi"), 1)

            def h_hi_early(w_col, x_name):
                def after_slab(s):
                    if s >= 2:
                        for k in (2 * s - 4, 2 * s - 3):
                            h_hi(w_col, x_name, k)
                return after_slab

            def first_group_after_norm(n, g, w_col, x_name):
                split(g, 0)
                split(g, 1)
                for k in range(12, KT):
                    h_hi(w_col, x_name, k)
                for s in range(2, 8):
                    split(g, s)
                root(n)

            split(G_OUT, 0)
            split(G_OUT, 1)
            for g in range(2):
                sc_.wait_ge(*at("gate_read", g + 1))
                buf = rstd[:, :] if g == 0 else hbuf[:, 0, :]
                a(buf, buf, ACT.Sqrt).then_inc(S("gate_s"), 1)
            split(G_OUT, 2)
            split(G_OUT, 3)
            for j in range(YT):
                sc_.wait_ge(*at("gate_scaled", j + 1))
                a(hhi[:, 8 + j, :], zs[:, j, :], ACT.Copy).then_inc(S("cat_c_hi"), 1)
            for i in range(2):
                sc_.wait_ge(*at(f"st_ssd{i}", 16 * 4))
            for s in range(4, 8):
                split(G_OUT, s)
            groups_1_to_3(G_OUT, h_hi_early(C_XA, "x_out"))
            first_group_after_norm(1, G_Q, C_XA, "x_out")
            groups_1_to_3(G_Q, lambda s: None)
            SCALE = 1.0 / math.sqrt(XD)
            for n in range(8 + 1):
                if n < 8:
                    sc_.wait_ge(*at("p_max", n + 1))
                    if n >= 2:
                        sc_.wait_ge(*at("p_t", n - 1))
                    a(pr[:, n % 2, :], B[n % 2][:, 0:NM], ACT.Exp, scale=SCALE, bias=sm[:, n, 1:2],
                      accum_out=sm[:, n, 2:3]).then_inc(S("p_exp"), 1)
                if n >= 1:
                    o = n - 1
                    h, l = divmod(o, 2)
                    sc_.wait_ge(*at("p_t", o + 1))
                    if o >= 2:
                        sc_.wait_ge(*at("pv", o - 1))
                    a(pT[:, o % 2, :, :], v3(B[2 + o % 2][:, 0:NM], P), ACT.Copy).then_inc(S("pT"), 1)
                    sc_.wait_ge(*at("pv", o + 1))
                    a(hhi[:, 4 * h:4 * h + 4, l * P:(l + 1) * P], v3(B[4 + o % 2][:, :], P), ACT.Copy)\
                        .then_inc(S("o_hi"), 1)
            sc_.wait_ge(*at("pads", 2))
            for h in range(XH):
                a(qs_hi[:, 4 * h:4 * h + 4, h, :], qT[:, 4 * h:4 * h + 4, NP:T], ACT.Copy).then_inc(S("qs_hi"), 1)
            for u in range(NB * XH):
                for i in range(2):
                    sc_.wait_ge(*at("kc_t", 2 * u + i + 1))
                    if u >= 2:
                        sc_.wait_ge(*at("s_scores", u - 1))
                    a(kc_hi[:, u % 2, 2 * i:2 * i + 2, :], v3(B[4 + 2 * (u % 2) + i][:, :], NM), ACT.Copy)\
                        .then_inc(S("kc_hi"), 1)
            sc_.wait_ge(*at("ps_max", 1))
            a(prs[:, :], prs[:, :], ACT.Exp, scale=SCALE, bias=sm[:, 8, 1:2],
              accum_out=sm[:, 8, 2:3]).then_inc(S("ps_exp"), 1)
            sc_.wait_ge(*at("ps_t", 1))
            sc_.wait_ge(*at("pads", 4))
            for h in range(XH):
                a(pTs_hi[:, :, h, h, :], v3(B[4][:, 0:NM], P)[:, :, NS * h:NS * (h + 1)], ACT.Copy)\
                    .then_inc(S("pTs_hi"), 1)
            for b in range(NB):
                sc_.wait_ge(*at(f"kv_loaded{b % 2}", 16 * ((NB + b) // 2 + 1)))
                for h in range(XH):
                    n = XH * b + h
                    if n >= 2:
                        sc_.wait_ge(*at("pv_sample", n - 1))
                    a(v3(whi[:, n % 2, :], XD), kv[:, b % 2, :, h * XD:(h + 1) * XD], ACT.Copy)\
                        .then_inc(S("v_hi"), 1)
            sc_.wait_ge(*at("pv_sample", NB * XH))
            split(G_O, 0)
            sc_.wait_ge(*at("os_t", 1))
            a(hhi[:, :, NP:T].rearrange("p (h d) t -> p h d t", d=4),
              B[4][:, :].rearrange("p (d h t) -> p h d t", d=4, h=XH), ACT.Copy).then_inc(S("os_hi"), 1)

            sc_.wait_ge(*at("os_lo", 1))
            cw = I["ffn_conv_w"][0].rearrange("w (t p) -> (w t) p", p=P)
            sc_.dma_start(frow[:, 0, :], cw[0:86, :]).then_inc(S("ff_rows"), 16)
            sc_.dma_start(frow[0:3 * FT - 86, 1, :], cw[86:3 * FT, :]).then_inc(S("ff_rows"), 16)
            sc_.dma_start(frow[3 * FT - 86:86, 1, :], tiles(I["ffn_conv_b"][0])).then_inc(S("ff_rows"), 16)
            sc_.dma_start(fhrow[:, :], I["state_ffn_conv"][0].rearrange("b r c -> (b r) c"))\
               .then_inc(S("ff_rows"), 16)
            for s in range(1, 8):
                split(G_O, s)
            groups_1_to_3(G_O, h_hi_early(C_FFN, "x_o"))

            def one(t, i):
                return t[:, i, :] if isinstance(i, int) else t[:, bass.ds(i, 1), :].rearrange("p a b -> p (a b)")

            def pcol(r, f):
                return fprm[:, r, f:f + 1] if isinstance(f, int) else fprm[:, r, bass.ds(f, 1)]

            def affine(i, m):
                f = 4 * i + m
                sc_.wait_ge(*at("g_read", f + 1))
                if not (isinstance(i, int) and i == 0):
                    sc_.wait_ge(*at("act", f - 3))
                a(cg[:, m, :], gs[:, m, :], ACT.Identity, scale=pcol(2, f), bias=pcol(3, f)).then_inc(S("aff"), 1)
                a(spad[:, m, :, 2:2 + NL], vsplit(gs[:, m, NP:T], NB), ACT.Copy).then_inc(S("aff"), 1)

            def silu(i, m):
                sc_.wait_ge(*at("taps", 4 * i + m + 1))
                a(cg[:, m, :], cg[:, m, :], ACT.Silu).then_inc(S("silu"), 1)

            def pair(i, mt=GM, width=GW):
                g = G_FF + 2 * i
                if isinstance(i, int) and i == 0:
                    first_group_after_norm(2, g, C_FFN, "x_o")
                    sc_.wait_ge(*at("ff_cols", 3))
                else:
                    for s in range(8):
                        split(g, s, width)
                split(g + 1, 0, width)
                split(g + 1, 1, width)
                for m in range(4):
                    if m < mt:
                        affine(i, m)
                    if 0 < m:
                        silu(i, m - 1) if m - 1 < mt else None
                    split(g + 1, 2 + m, width)
                if mt == 4:
                    silu(i, 3)
                split(g + 1, 6, width)
                split(g + 1, 7, width)
            loop(sc_, FPAIRS, pair)
            pair(FPAIRS, FTAIL, FTAIL * P)

            for r in range(11):
                w = P * (min(4 * r + 4, FT) - 4 * r)
                sc_.wait_ge(*at("fx_t", r + 1))
                a(fx(r)[:, 0:w], B[r % 8][0:18, 0:w], ACT.Copy).then_inc(S("fx_read"), 1)
            sc_.wait_ge(*at("fx_read", 11))
            for room, f0, nf in ((kT, 0, 4096), (vtok, 4096, FF - 4096)):
                rows_ = room[:, :, :].rearrange("p a b -> p (a b)")
                sc_.dma_start(O["p_ffn_conv"][0, 0][:, f0:f0 + nf], rows_[0:2, 0:nf]).then_inc(S("st_ffn"), 16)
                sc_.dma_start(O["s_ffn_conv"][0].rearrange("b r n -> (b r) n")[:, f0:f0 + nf],
                              rows_[2:18, 0:nf]).then_inc(S("st_ffn"), 16)

            for half in range(2):
                base = half * FT

                def down(f, j, turn):
                    n = NB_DOWN + base + j
                    slot = n % 2
                    wait_raw(sc_, (NS_B + n) // 4 + turn, n % 4)
                    if half == 0 and isinstance(f, int) and f < 2:
                        wait_used_B(sc_, NG_B - 1, 6 + f)
                    else:
                        sc_.wait_ge(*at("d_slab", base + f - 1))
                    a(whi[:, slot, :], raw[:, n % 4, :], ACT.Copy).then_inc(S("w_hi"), 1)
                    a(ahi[:, slot, :], one(act, f), ACT.Copy).then_inc(S("a_hi"), 1)

                for j in range(4):
                    down(j, j, 0)
                with sc_.Fori(1, FT // 4) as i:
                    for j in range(4):
                        down(4 * i + j, j, i)
                for j in range(FT % 4):
                    down(FT - FT % 4 + j, j, FT // 4)

            root(3)
            for n in range(4):
                for t in range(3):
                    w = P if t < 2 else NS
                    slot = 3 * (n % 2) + t
                    sc_.wait_ge(*at("y_t", n + 1))
                    if n >= 2:
                        sc_.wait_ge(*at(f"st_y{n % 2}", 16 * 3))
                    a(yst[0:w, slot, :], B[1 + slot][0:w, :], ACT.Copy).then_inc(S("y_read"), 1)
                for t in range(3):
                    w = P if t < 2 else NS
                    slot = 3 * (n % 2) + t
                    sc_.wait_ge(*at("y_read", 3 * n + t + 1))
                    dst = O["y_prompt"][0, t * P:(t + 1) * P, n * 512:(n + 1) * 512] if t < 2 \
                        else O["y_sample"].rearrange("b l d -> (b l) d")[:, n * 512:(n + 1) * 512]
                    sc_.dma_start(dst, yst[0:w, slot, :]).then_inc(S(f"st_y{n % 2}"), 16)

        @block.vector
        def _(v):
            me = Own(v, S("dve_step"))

            def turned(n, *copies):
                v.wait_ge(*at("s0_t", n + 1))
                for i, (dst, src) in enumerate(copies):
                    q = v.tensor_copy(dst, src)
                q.then_inc(S("s0_turned"), 1)

            v.wait_ge(*at("rows_loaded", 16 * 18))
            for r in (slice(32, 48), slice(96, 104)):
                v.tensor_copy(rows[r, 1, :].rearrange("j (a p) -> j a p", a=2),
                              pairs[r, :].unsqueeze(2).to_broadcast([r.stop - r.start, 2, 64]))\
                    .then_inc(S("rows_spread"), 1)
            turned(0, (prm[:, :], B[0][:, 0:348]))
            for k in range(KT):
                turned(1 + k, (xT[:, k, :], B[4 + k % 3][:, 0:T]))
            v.wait_ge(*at("hist_loaded", 16 * 9))
            turned(17, (s0s[:, :, :], v3(B[1][:, 0:256], P)))
            me.step(v.memset(up[:, :, 0:HA], 0.0))
            me.step(v.memset(xbr[:, :, 0:HC], 0.0))
            for c in range(2):
                dsts = []
                for t in range(4):
                    dsts.append((up_sample(t)[:, 4 * c:4 * c + 4, 0:HA],
                                 v3(B[2 + c][:, t * 120:(t + 1) * 120], HA)))
                turned(18 + c, *dsts)
            turned(20, *[(xbr_sample(t)[:, :, 0:HC], v3(B[4][:, t * 24:(t + 1) * 24], HC)) for t in range(12)])

            def norm(n, bank, w_col, out, name, lo):
                v.wait_ge(*at("sum_mm", n + 1))
                v.tensor_scalar(rstd[:, :], B[bank][:, 0:T], 1.0 / D, EPS, ALU.mult, ALU.add)\
                    .then_inc(S("norm_v"), 1)
                v.wait_ge(*at("norm_s", n + 1))
                me.link(v.reciprocal(rstd[:, :], rstd[:, :]))
                for k in range(KT):
                    if lo and k >= 2:
                        v.wait_ge(*at(name, k - 1))
                    v.scalar_tensor_tensor(out=out(k), in0=xT[:, k, :], scalar=col(w_col + k), in1=rstd[:, :],
                                           op0=ALU.mult, op1=ALU.mult).then_inc(S("h32" if lo else name), 1)
                    if lo and k >= 1:
                        lo(k - 1)
                if lo:
                    lo(KT - 1)
            norm(0, 7, C_MIX, lambda k: hT[:, k, :], "hmix", None)

            lr, li = prm[:, C_LR:C_LR + SJ], prm[:, C_LI:C_LI + SJ]
            c = lambda i: sc[:, i, :]
            tt, ts, stt = v.tensor_tensor, v.tensor_scalar, v.scalar_tensor_tensor
            v.wait_ge(*at("s5_exp", 1))
            tt(c(1), lr, c(0), ALU.mult).then_inc(S("s5_arg"), 1)
            me.link(tt(c(2), li, c(0), ALU.mult))
            me.link(ts(c(3), c(2), 1.0 / TWO_PI, MAGIC, ALU.mult, ALU.add))
            me.link(ts(c(3), c(3), MAGIC, None, ALU.subtract))
            me.link(stt(c(4), c(3), -PI_A, c(2), ALU.mult, ALU.add))
            me.link(stt(c(4), c(3), -PI_B, c(4), ALU.mult, ALU.add))
            me.link(stt(c(4), c(3), -PI_C, c(4), ALU.mult, ALU.add))
            me.link(stt(c(5), c(4), -1.0, c(4), ALU.mult, ALU.max))
            ts(c(5), c(5), -0.5, math.pi / 2, ALU.mult, ALU.add).then_inc(S("s5_arg"), 1)
            v.wait_ge(*at("s5_sin", 2))
            me.step(tt(c(8), c(6), c(6), ALU.mult))
            me.step(stt(c(9), c(6), 2.0, c(7), ALU.mult, ALU.mult))
            me.sync()
            me.link(ts(c(8), c(8), -2.0, 1.0, ALU.mult, ALU.add))
            me.step(v.tensor_copy(c(16), c(8)))
            me.step(v.tensor_copy(c(17), c(9)))
            me.step(v.memset(tabC[:, :, 0:1], 1.0))
            v.memset(tabS[:, :, 0:1], 0.0).then_inc(S("theta"), 1)
            v.wait_ge(*at("s5_exp", 2))
            me.step(tt(c(12), c(14), c(8), ALU.mult))
            me.step(tt(c(13), c(14), c(9), ALU.mult))
            me.step(tt(c(10), lr, lr, ALU.mult))
            me.step(tt(c(11), li, li, ALU.mult))
            me.sync()
            me.step(tt(c(10), c(10), c(11), ALU.add))
            me.step(ts(c(15), c(12), -1.0, None, ALU.add))
            me.sync()
            me.step(v.reciprocal(c(10), c(10)))
            me.step(tt(c(21), c(15), lr, ALU.mult))
            me.step(tt(c(22), c(13), li, ALU.mult))
            me.step(tt(c(23), c(13), lr, ALU.mult))
            me.step(tt(c(24), c(15), li, ALU.mult))
            me.sync()
            me.step(tt(c(21), c(21), c(22), ALU.add))
            me.step(tt(c(23), c(23), c(24), ALU.subtract))
            me.sync()
            me.step(tt(c(21), c(21), c(10), ALU.mult))
            me.step(tt(c(22), c(23), c(10), ALU.mult))
            me.sync()
            co_r = c(21).unsqueeze(2).to_broadcast([P, SJ, 16])
            co_i = c(22).unsqueeze(2).to_broadcast([P, SJ, 16])
            tmp = [v3(zs[:, i, 0:SJ * 16], 16) for i in range(4)]
            me.step(tt(tmp[0], brow[:, 0, :, :], co_r, ALU.mult))
            me.step(tt(tmp[1], brow[:, 1, :, :], co_i, ALU.mult))
            me.step(tt(tmp[2], brow[:, 1, :, :], co_r, ALU.mult))
            me.step(tt(tmp[3], brow[:, 0, :, :], co_i, ALU.mult))
            me.sync()
            v.wait_ge(*at("consts", 1))
            for i, (x, y, op) in enumerate(((0, 1, ALU.subtract), (2, 3, ALU.add))):
                for g in range(2):
                    r = slice(64 * g, 64 * g + 64)
                    q = tt(bpad[r, i, :, 16 * g:16 * g + 16], tmp[x][r], tmp[y][r], op)
                    if g == 0:
                        me.step(q)
                q.then_inc(S("bc_padded"), 1)
            me.link(v.reduce_sum(gsel[:, 0:1], g4[:, :], axis=AX.X))
            me.link(ts(gsel[:, 1:2], gsel[:, 0:1], -1.0, 1.0, ALU.mult, ALU.add))
            me.link(ts(gneg[:, :], gsel[:, :], -1.0, None, ALU.mult))
            for i in range(2):
                m_ = gsel if i == 0 else gneg
                for g in range(2):
                    q = ts(cpad[:, i, :, g, :], crow[:, i, :, :], m_[:, g:g + 1], None, ALU.mult)
                    if g == 0:
                        me.step(q)
                q.then_inc(S("bc_padded"), 1)
            me.step(ts(gcol_b[:, :], prm[:, C_GLB:C_GLB + 4], 0.5, None, ALU.mult))

            v.wait_ge(*at("dt_mm", 1))
            v.wait_ge(*at("dt_act", 1))
            ts(R_RAW, B[7][0:NH, 0:T], hcol[:, 1:2], None, ALU.add).then_inc(S("dt_read"), 1)
            v.wait_ge(*at("dt_read", 1))
            me.link(ts(R_DT, R_RAW, 0.0, None, ALU.max))
            stt(R_EXP, R_DT, -2.0, R_RAW, ALU.mult, ALU.add).then_inc(S("dt_dve"), 1)
            v.wait_ge(*at("dt_act", 2))
            ts(R_W, R_EXP, 1.0, None, ALU.add).then_inc(S("dt_dve"), 1)
            v.wait_ge(*at("dt_dve", 2))
            me.link(ts(R_T, R_W, -1.0, None, ALU.add))
            v.wait_ge(*at("dt_act", 3))
            me.link(ts(R_W, R_T, 0.0, None, ALU.is_equal))
            me.link(ts(R_T, R_T, 1e-30, None, ALU.max))
            me.link(v.reciprocal(R_T, R_T))
            v.wait_ge(*at("dt_act", 3))
            me.link(tt(R_T, R_T, R_LN, ALU.mult))
            me.link(tt(R_T, R_T, R_W, ALU.add))
            me.link(tt(R_T, R_T, R_EXP, ALU.mult))
            me.link(tt(R_DT, R_DT, R_T, ALU.add))
            me.link(ts(R_LN, R_DT, hcol[:, 2:3], -1.0, ALU.mult, ALU.mult))
            me.link(v.tensor_tensor_scan(R_CS, segmask[:, :], R_LN, 0.0, ALU.mult, ALU.add))
            for c0, n, w in ((0, 2, P), (NP, NB, NL)):
                seg_ = R_CS[:, c0:c0 + n * w].rearrange("p (a b) -> p a b", b=w)
                q = tt(R_END[:, c0:c0 + n * w].rearrange("p (a b) -> p a b", b=w),
                       seg_[:, :, w - 1:w].to_broadcast([NH, n, w]), seg_, ALU.subtract)
                if n == 2:
                    me.step(q)
            q.then_inc(S("dt_dve"), 1)
            v.wait_ge(*at("dt_act", 5))
            v.tensor_scalar(diag[:, :], ident[0:NH, 0:NH], hcol[:, 3:4], None, ALU.mult).then_inc(S("dt_rows"), 1)

            for i in range(4):
                turned(21 + i, ((bT if i < 2 else cT)[:, i % 2, :, :], v3(B[4 + i][:, :], P)))
            v.wait_ge(*at("mem_sq", 2))
            ts(msum[:, 2:4], msum[:, 0:2], 1.0 / D, EPS, ALU.mult, ALU.add).then_inc(S("mem_v"), 1)
            v.wait_ge(*at("mem_s", 1))
            v.reciprocal(msum[:, 4:6], msum[:, 2:4]).then_inc(S("mem_v"), 1)

            def s5_y(jt):
                v.wait_ge(*at("s5_y", jt + 1))
                stt(uT[:, jt, :], uT[:, jt, :], col(C_S5D + jt), B[6 + jt % 2][:, 0:T], ALU.mult, ALU.add)\
                    .then_inc(S("s5_yd"), 1)

            v.wait_ge(*at("tables", 1))
            for j in range(SJ):
                v.wait_ge(*at("s5_in", j + 1))
                ps = v3(B[4 + j % 2][:, :], NP)
                if j >= 2:
                    v.wait_ge(*at("s5_h", 2 * (j - 1)))
                tt(tAB[:, 0, :, :], ps, tabC[:, j, :].unsqueeze(1).to_broadcast([P, 2, NP]), ALU.mult)\
                    .then_inc(S("s5_turned"), 1)
                tt(tAB[:, 1, :, :], ps, tabS[:, j, :].unsqueeze(1).to_broadcast([P, 2, NP]), ALU.mult)\
                    .then_inc(S("s5_turned"), 1)
                v.wait_ge(*at("s5_turned", 2 * j + 2))
                g_ = gri[:, j % 2, :, :]
                me.step(tt(g_[:, 0, :], tAB[:, 0, 0, :], tAB[:, 1, 1, :], ALU.add))
                me.step(tt(g_[:, 1, :], tAB[:, 0, 1, :], tAB[:, 1, 0, :], ALU.subtract))
                me.sync()
                mag = sc[:, 14, j:j + 1].to_broadcast([P, NP])
                me.step(v.tensor_tensor_scan(g_[:, 0, :], mag, g_[:, 0, :], 0.0, ALU.mult, ALU.add))
                v.tensor_tensor_scan(g_[:, 1, :], mag, g_[:, 1, :], 0.0, ALU.mult, ALU.add)\
                    .then_inc(S("s5_scanned"), 1)
                if j == 8:
                    s5_y(0)
                if j == 12:
                    s5_y(1)
            for t in range(4):
                v.wait_ge(*at("in_read", 8 + t + 1))
                stt(up[:, t, HA:UP], th[:, t, 0:NP], 1.0, va[:, t, 0:NP], ALU.add, ALU.mult)\
                    .then_inc(S("u_done"), 1)
                stt(up_sample(t)[:, :, HA:US], vsplit(th[:, t, NP:T], NB), 1.0, vsplit(va[:, t, NP:T], NB),
                    ALU.add, ALU.mult).then_inc(S("u_done"), 1)
            for t in range(4):
                v.wait_ge(*at("tap_a", 2 * t + 2))
                for w in range(1, WA):
                    wc = col(C_CAW + 4 * w + t)
                    me.step(stt(va[:, t, 0:NP], up[:, t, w:w + NP], wc, va[:, t, 0:NP], ALU.mult, ALU.add))
                    vs = vsplit(va[:, t, NP:T], NB)
                    q = stt(vs, up_sample(t)[:, :, w:w + NL], wc, vs, ALU.mult, ALU.add)
                    if w < WA - 1:
                        me.link(q)
                    else:
                        q.then_inc(S("conv_a"), 1)
                if t == 0:
                    s5_y(2)
                    s5_y(3)
            for t in range(12):
                v.wait_ge(*at("tap_c", 2 * t + 2))
                for w in range(1, WC):
                    wc = col(C_CCW + 12 * w + t)
                    me.step(stt(xc[:, t, 0:NP], xbr[:, t, w:w + NP], wc, xc[:, t, 0:NP], ALU.mult, ALU.add))
                    vs = vsplit(xc[:, t, NP:T], NB)
                    q = stt(vs, xbr_sample(t)[:, :, w:w + NL], wc, vs, ALU.mult, ALU.add)
                    if w < WC - 1:
                        me.link(q)
                    else:
                        q.then_inc(S("conv_c_taps"), 1)

            v.wait_ge(*at("ex_mm", 5))
            v.wait_ge(*at("mem_t", 8))
            def gate_lo(m):
                v.wait_ge(*at("cat_b_hi", m + 1))
                stt(hlo[:, 4 + m, :], hbuf[:, m % 2, :], 0.5, hhi[:, 4 + m, :].bitcast(F32), ALU.mult, ALU.subtract)\
                    .then_inc(S("cat_b"), 1)
            for m in range(4):
                v.wait_ge(*at("s5_gate", m + 1))
                stt(hbuf[:, m % 2, :], hbuf[:, m % 2, :], 1.0, uT[:, m, :], ALU.add, ALU.mult)\
                    .then_inc(S("gated_b"), 1)
                if m >= 1:
                    gate_lo(m - 1)
            gate_lo(3)
            v.wait_ge(*at("conf_mm", 1))
            for t in range(4):
                stt(va[:, t, :], B[6][:, 0:T], -1.0 / 512, va[:, t, :], ALU.mult, ALU.add).then_inc(S("centred"), 1)
            v.wait_ge(*at("centred", 4))
            v.wait_ge(*at("conf_mm", 2))
            ts(rstd[:, :], B[7][:, 0:T], 1.0 / 512, EPS, ALU.mult, ALU.add).then_inc(S("conf_read"), 1)
            v.wait_ge(*at("conf_s", 1))
            me.link(v.reciprocal(rstd[:, :], rstd[:, :]))
            for t in range(4):
                stt(va[:, t, :], va[:, t, :], col(C_LNW + t), rstd[:, :], ALU.mult, ALU.mult)\
                    .then_inc(S("conf_scaled"), 1)
            for t in range(4):
                v.wait_ge(*at("cat_a_hi", t + 1))
                tt(hlo[:, t, :], va[:, t, :], hhi[:, t, :].bitcast(F32), ALU.subtract).then_inc(S("cat_a"), 1)
            v.wait_ge(*at("cat_a", 4))

            v.wait_ge(*at("st_s5", 64))
            v.wait_ge(*at("tok_mm", 1))
            src = B[4][:, 0:9 * NH].rearrange("p (q c h) -> p q c h", q=3, c=3)
            dst = tokT[:, :, :].rearrange("p (q c) h -> p q c h", q=3)
            v.tensor_copy(dst[:, :, 0:2, :], src[:, :, 0:2, :]).then_inc(S("tok_read"), 1)
            v.tensor_copy(dst[0:NS, :, 2, :], src[0:NS, :, 2, :]).then_inc(S("tok_read"), 1)
            v.tensor_copy(ecl[:, :], B[4][:, 256:256 + NH]).then_inc(S("tok_read"), 1)
            v.wait_ge(*at("tok_read", 3))

            def per_head(q, c, w, h0=0, n=NH):
                return tokT[0:w, 3 * q + c, h0:h0 + n].unsqueeze(2).to_broadcast([w, n, HP])
            for c in range(3):
                w = P if c < 2 else NS
                for hf in range(2):
                    v.wait_ge(*at("x_t", 2 * c + hf + 1))
                    tt(v3(xdt[0:w, c, hf * 512:(hf + 1) * 512], HP), v3(B[2 + hf][0:w, :], HP),
                       per_head(0, c, w, 8 * hf, 8), ALU.mult).then_inc(S("xdt"), 1)
                v.wait_ge(*at("b_t", c + 1))
                v.tensor_copy(btok[0:w, c, :, :], v3(B[5][0:w, 0:2 * P], P)).then_inc(S("btok"), 1)
            v.wait_ge(*at("cb_mm", 1))
            v.tensor_copy(cb[:, :, :, :], B[6][:, :].rearrange("p (c g n) -> p c g n", c=2, g=2))\
                .then_inc(S("cb_read"), 1)
            v.tensor_copy(cbs[:, :, :], v3(B[7][0:NS, 0:2 * NS], NS)).then_inc(S("cb_read"), 1)
            v.wait_ge(*at("xdt", 6))
            tt(v3(xds[:, :], HP), v3(xdt[:, 0, :], HP), per_head(2, 0, P), ALU.mult).then_inc(S("xds"), 1)
            v.wait_ge(*at("st_mm", 1))
            for g in range(2):
                v.tensor_copy(pvT[:, g * 512:(g + 1) * 512], B[2 + g][:, :]).then_inc(S("st_read"), 1)
            tt(v3(xds[:, :], HP), v3(xdt[:, 1, :], HP), per_head(2, 1, P), ALU.mult).then_inc(S("xds"), 1)
            v.wait_ge(*at("st_mm", 2))
            v.wait_ge(*at("st_read", 2))
            me.link(tt(v3(xds[:, :], HP), v3(pvT[:, :], HP), ecl[:, :].unsqueeze(2).to_broadcast([P, NH, HP]),
                       ALU.mult))
            for g in range(2):
                part = xds[:, g * 512:(g + 1) * 512]
                tt(part, B[2 + g][:, :], part, ALU.add).then_inc(S("st_read"), 1)
            v.wait_ge(*at("st_mm", 3))
            me.step(v.tensor_copy(s0T[:, 0:4, :], v3(B[2][:, :], P)))
            v.tensor_copy(s0T[:, 4:8, :], v3(B[3][:, :], P)).then_inc(S("st_out"), 1)
            v.wait_ge(*at("btok", 3))

            def masked_b(g):
                tt(bm[:, :, :], btok[0:NS, 2, g, :].unsqueeze(1).to_broadcast([NS, NB, NST]),
                   bmask[0:NS, :].unsqueeze(2).to_broadcast([NS, NB, NST]), ALU.mult).then_inc(S("masked_b"), 1)
            masked_b(0)
            tt(v3(xds[0:NS, :], HP), v3(xdt[0:NS, 2, :], HP), per_head(2, 2, NS), ALU.mult).then_inc(S("xds"), 1)

            for j in range(YT):
                for h in range(2):
                    hd = 2 * j + h
                    v.wait_ge(*at("abc", hd + 1))
                    if j > 0:
                        v.wait_ge(*at("y_mm", 2 * (j - 1) + h + 1))
                    for c in range(2):
                        stt(dec[:, h, c * P:(c + 1) * P], B[2 + h][:, c * P:(c + 1) * P],
                            tokT[:, 3 + c, hd:hd + 1], negmask[:, :], ALU.subtract, ALU.add).then_inc(S("seg"), 1)
                    stt(decs[:, h, :], B[2 + h][0:NS, NP:T], tokT[0:NS, 5, hd:hd + 1], negs[:, :],
                        ALU.subtract, ALU.add).then_inc(S("seg"), 1)
                v.wait_ge(*at("yo_mm", j + 1))
                tt(yo[:, :], B[4][:, 256:256 + P + NS], eb[:, :], ALU.mult).then_inc(S("yo_read"), 1)
                me.link(stt(hbuf[:, 0, :], xc[:, j, :], col(C_SSDD + j), B[5][:, 0:T], ALU.mult, ALU.add))
                v.wait_ge(*at("yo_read", j + 1))
                me.link(tt(hbuf[:, 0, P:T], hbuf[:, 0, P:T], yo[:, :], ALU.add))
                tt(zs[:, j, :], zs[:, j, :], hbuf[:, 0, :], ALU.mult).then_inc(S("gated"), 1)
                v.wait_ge(*at("upd_mm", j + 1))
                v.wait_ge(*at("s0_decayed", j + 1))
                for i in range(2):
                    part = s0[:, j % 2, 4 * i:4 * i + 4, :]
                    tt(part, v3(B[6 + i][:, :], NST), part, ALU.add).then_inc(S("upd_read"), 1)
                if j == 3:
                    masked_b(1)
            def split(g, s, width=GW):
                v.wait_ge(*at("w_hi", 8 * g + (s + 1)))
                wsl = slice(0, 2 * width)
                tt(wlo[:, s % 2, wsl], raw[:, s % 4, wsl], whi[:, s % 2, wsl].bitcast(F32), ALU.subtract)\
                    .then_inc(S("w_lo"), 1)

            def one(t, i):
                return t[:, i, :] if isinstance(i, int) else t[:, bass.ds(i, 1), :].rearrange("p a b -> p (a b)")

            def bank_of(i, m):
                return B[m] if not isinstance(i, int) or i < 3 else B[4 + m]

            def x_add(g0, name, i, m):
                v.wait_ge(*at("b_acc", 4 * (g0 + i) + (m + 1)))
                x_ = one(xT, 4 * i + m)
                tt(x_, bank_of(i, m)[:, 0:T], x_, ALU.add).then_inc(S(name), 1)

            def q_scale(i, m):
                v.wait_ge(*at("b_acc", 4 * (G_Q + i) + (m + 1)))
                tt(one(qT, 4 * i + m), bank_of(i, m)[:, 0:T], rstd[:, :], ALU.mult).then_inc(S("q_read"), 1)

            def h_lo(n, w_col, name, k):
                v.wait_ge(*at("h_hi", KT * (n - 1) + k + 1))
                stt(hlo[:, k, :], xT[:, k, :], col(w_col + k), hhi[:, k, :].bitcast(F32), ALU.mult, ALU.subtract)\
                    .then_inc(S(name), 1)

            def groups_1_to_3(g0, evac, after_slab):
                with v.Fori(1, 3) as i:
                    split(g0 + i, 0)
                    for m in range(GM):
                        evac(i - 1, m)
                    for s in range(1, 8):
                        split(g0 + i, s)
                split(g0 + 3, 0)
                for m in range(GM):
                    evac(2, m)
                for s in range(1, 8):
                    split(g0 + 3, s)
                    after_slab(s)

            def h_lo_early(n, w_col, name):
                def after_slab(s):
                    if s >= 2:
                        for k in (2 * s - 4, 2 * s - 3):
                            h_lo(n, w_col, name, k)
                return after_slab

            def first_group_after_norm(n, g, w_col, name, evac, meanwhile=None):
                split(g, 0)
                split(g, 1)
                for m in range(GM):
                    evac(3, m)
                    h_lo(n, w_col, name, 12 + m)
                for s in range(2, 7):
                    split(g, s)
                v.wait_ge(*at("sum_mm", n + 1))
                v.tensor_scalar(rstd[:, :], B[4][:, 0:T], 1.0 / D, EPS, ALU.mult, ALU.add)\
                    .then_inc(S("norm_v"), 1)
                split(g, 7)
                v.wait_ge(*at("norm_s", n + 1))
                me.link(v.reciprocal(rstd[:, :], rstd[:, :]))

            split(G_OUT, 0)
            split(G_OUT, 1)
            for g in range(2):
                v.wait_ge(*at("gate_mm", g + 1))
                if g == 0:
                    v.wait_ge(*at("gated", YT))
                ts(rstd[:, :] if g == 0 else hbuf[:, 0, :], B[2 + g][:, 0:T], 1.0 / 512, EPS, ALU.mult, ALU.add)\
                    .then_inc(S("gate_read"), 1)
            for g in range(2):
                v.wait_ge(*at("gate_s", g + 1))
                buf = rstd[:, :] if g == 0 else hbuf[:, 0, :]
                me.link(v.reciprocal(buf, buf))
            split(G_OUT, 2)
            for j in range(YT):
                stt(zs[:, j, :], zs[:, j, :], col(C_SNW + j), rstd[:, :] if j < 4 else hbuf[:, 0, :],
                    ALU.mult, ALU.mult).then_inc(S("gate_scaled"), 1)
            split(G_OUT, 3)
            for j in range(YT):
                v.wait_ge(*at("cat_c_hi", j + 1))
                q = tt(hlo[:, 8 + j, :], zs[:, j, :], hhi[:, 8 + j, :].bitcast(F32), ALU.subtract)
                q.then_inc(S("cat_c"), 1)
            v.wait_ge(*at("cat_c", 8))
            for s in range(4, 8):
                split(G_OUT, s)

            add_out = lambda i, m: x_add(G_OUT, "x_out", i, m)
            groups_1_to_3(G_OUT, add_out, h_lo_early(1, C_XA, "hxa"))
            first_group_after_norm(1, G_Q, C_XA, "hxa", add_out)
            groups_1_to_3(G_Q, q_scale, lambda s: None)
            for m in range(GM):
                q_scale(3, m)
            SCALE = 1.0 / math.sqrt(XD)

            def row_max(src, n, name):
                me.link(v.reduce_max(sm[:, n, 0:1], src, axis=AX.X))
                ts(sm[:, n, 1:2], sm[:, n, 0:1], -SCALE, None, ALU.mult).then_inc(S(name), 1)

            def normalise(buf, n, name):
                me.link(v.reciprocal(sm[:, n, 3:4], sm[:, n, 2:3]))
                ts(buf, buf, sm[:, n, 3:4], None, ALU.mult).then_inc(S(name), 1)
            for n in range(8 + 1):
                if n < 8:
                    v.wait_ge(*at("scores", n + 1))
                    row_max(B[n % 2][:, 0:NM], n, "p_max")
                    v.wait_ge(*at("p_exp", n + 1))
                    normalise(pr[:, n % 2, :], n, "p_norm")
                if n >= 1:
                    o = n - 1
                    h, l = divmod(o, 2)
                    v.wait_ge(*at("o_hi", o + 1))
                    tt(hlo[:, 4 * h:4 * h + 4, l * P:(l + 1) * P], v3(B[4 + o % 2][:, :], P),
                       hhi[:, 4 * h:4 * h + 4, l * P:(l + 1) * P].bitcast(F32), ALU.subtract).then_inc(S("o_lo"), 1)
            for h in range(XH):
                v.wait_ge(*at("qs_hi", h + 1))
                tt(qs_lo[:, 4 * h:4 * h + 4, h, :], qT[:, 4 * h:4 * h + 4, NP:T],
                   qs_hi[:, 4 * h:4 * h + 4, h, :].bitcast(F32), ALU.subtract).then_inc(S("qs_lo"), 1)

            def keep(b, name, acc, bank, n):
                if b == 0:
                    q = ts(acc, bank[:, 0:n], bmask[:, 0:1], None, ALU.mult)
                else:
                    v.wait_ge(*at(name, b))
                    q = stt(acc, bank[:, 0:n], bmask[:, b:b + 1], acc, ALU.mult, ALU.add)
                q.then_inc(S(name), 1)

            def keep_scores(b):
                v.wait_ge(*at("s_scores", XH * (b + 1)))
                keep(b, "s_kept", prs[:, :], B[b % 2], NM)

            def keep_values(b):
                v.wait_ge(*at("pv_sample", XH * (b + 1)))
                keep(b, "o_kept", osum[:, :], B[2 + b % 2], XD)

            for u in range(NB * XH):
                for i in range(2):
                    v.wait_ge(*at("kc_hi", 2 * u + i + 1))
                    half = slice(2 * i, 2 * i + 2)
                    tt(kc_lo[:, u % 2, half, :], v3(B[4 + 2 * (u % 2) + i][:, :], NM),
                       kc_hi[:, u % 2, half, :].bitcast(F32), ALU.subtract).then_inc(S("kc_lo"), 1)
                if u % XH == 1 and u > 1:
                    keep_scores(u // XH - 1)
            keep_scores(NB - 1)
            v.wait_ge(*at("s_kept", NB))
            row_max(prs[:, :], 8, "ps_max")
            v.wait_ge(*at("ps_exp", 1))
            normalise(prs[:, :], 8, "ps_norm")
            for h in range(XH):
                v.wait_ge(*at("pTs_hi", 4))
                tt(pTs_lo[:, :, h, h, :], v3(B[4][:, 0:NM], P)[:, :, NS * h:NS * (h + 1)],
                   pTs_hi[:, :, h, h, :].bitcast(F32), ALU.subtract).then_inc(S("pTs_lo"), 1)
            for n in range(NB * XH):
                b, h = divmod(n, XH)
                v.wait_ge(*at("v_hi", n + 1))
                tt(v3(wlo[:, n % 2, :], XD), kv[:, b % 2, :, h * XD:(h + 1) * XD],
                   v3(whi[:, n % 2, :], XD).bitcast(F32), ALU.subtract).then_inc(S("v_lo"), 1)
                if h == 1 and b > 0:
                    keep_values(b - 1)
            keep_values(NB - 1)
            split(G_O, 0)
            v.wait_ge(*at("os_hi", 1))
            tt(hlo[:, :, NP:T].rearrange("p (h d) t -> p h d t", d=4),
               B[4][:, :].rearrange("p (d h t) -> p h d t", d=4, h=XH),
               hhi[:, :, NP:T].bitcast(F32).rearrange("p (h d) t -> p h d t", d=4), ALU.subtract)\
                .then_inc(S("os_lo"), 1)
            for s in range(1, 7):
                split(G_O, s)

            def ffn_columns():
                v.wait_ge(*at("ff_t", 1))
                v.tensor_copy(fprm[:, :, :], v3(B[5][:, 0:4 * FT], FT)).then_inc(S("ff_cols"), 1)
                for r in range(2):
                    lo_, hi_ = (0, 32) if r == 0 else (32, FT)
                    v.wait_ge(*at("ff_t", r + 2))
                    v.tensor_copy(fh[:, lo_:hi_, :, :],
                                  B[6 + r][:, 0:16 * (hi_ - lo_)].rearrange("p (t b r) -> p t b r", b=NB, r=2))\
                        .then_inc(S("ff_cols"), 1)
                v.wait_ge(*at("ff_cols", 3))
            ffn_columns()
            split(G_O, 7)
            add_o = lambda i, m: x_add(G_O, "x_o", i, m)
            groups_1_to_3(G_O, add_o, h_lo_early(2, C_FFN, "hffn"))

            def gate_scale(i, m):
                f = 4 * i + m
                v.wait_ge(*at("b_acc", 4 * G_FF + 8 * i + m + 1))
                tt(gs[:, m, :], B[m][:, 0:T], rstd[:, :], ALU.mult).then_inc(S("g_read"), 1)

            def taps(i, m):
                f = 4 * i + m
                w0, w1 = [fprm[:, r, f:f + 1] if isinstance(f, int) else fprm[:, r, bass.ds(f, 1)] for r in range(2)]
                v.wait_ge(*at("aff", 2 * f + 2))
                hist = fh[:, f, :, :] if isinstance(f, int) \
                    else fh[:, bass.ds(f, 1), :, :].rearrange("p a b r -> p (a b) r")
                v.tensor_copy(spad[:, m, :, 0:2], hist).then_inc(S("tap_step"), 1)
                stt(cg[:, m, 1:NP], gs[:, m, 0:NP - 1], w1, cg[:, m, 1:NP], ALU.mult, ALU.add)\
                    .then_inc(S("tap_step"), 1)
                v.wait_ge(*at("tap_step", 4 * f + 1))
                cs = vsplit(cg[:, m, NP:T], NB)
                stt(cs, spad[:, m, :, 1:1 + NL], w1, cs, ALU.mult, ALU.add).then_inc(S("tap_step"), 1)
                v.wait_ge(*at("tap_step", 4 * f + 2))
                stt(cg[:, m, 2:NP], gs[:, m, 0:NP - 2], w0, cg[:, m, 2:NP], ALU.mult, ALU.add)\
                    .then_inc(S("tap_step"), 1)
                v.wait_ge(*at("tap_step", 4 * f + 3))
                stt(cs, spad[:, m, :, 0:NL], w0, cs, ALU.mult, ALU.add)
                gc = one(gcol, f)
                v.tensor_copy(gc[:, 0:2], gs[:, m, NP - 2:NP])
                v.tensor_copy(v3(gc[:, 2:18], 2), spad[:, m, :, NL:NL + 2]).then_inc(S("taps"), 1)

            def times_up(i, m, tail=False):
                f = 4 * i + m
                v.wait_ge(*at("gate_n", f + 1))
                v.wait_ge(S("b_acc"), 4 * (G_FF + 2 * FPAIRS) + FTAIL + m + 1 if tail
                          else 4 * (G_FF + 1) + 8 * i + (m + 1))
                tt(one(act, f), B[4 + m][:, 0:T], cg[:, m, :], ALU.mult).then_inc(S("act"), 1)

            def pair(i, mt=GM, width=GW):
                g = G_FF + 2 * i
                if isinstance(i, int) and i == 0:
                    first_group_after_norm(2, g, C_FFN, "hffn", add_o)
                else:
                    split(g, 0, width)
                    for m in range(GM):
                        times_up(i - 1, m)
                    for s in range(1, 8):
                        split(g, s, width)
                split(g + 1, 0, width)
                gate_scale(i, 0)
                gate_scale(i, 1)
                split(g + 1, 1, width)
                for m in range(2, mt):
                    gate_scale(i, m)
                for m in range(4):
                    if m < mt:
                        taps(i, m)
                    split(g + 1, 2 + m, width)
                split(g + 1, 6, width)
                split(g + 1, 7, width)
            loop(v, FPAIRS, pair)
            pair(FPAIRS, FTAIL, FTAIL * P)
            for m in range(FTAIL):
                times_up(FPAIRS, m, True)

            def add_half(hf):
                v.wait_ge(*at("d_slab", (hf + 1) * FT))
                for m in range(DG):
                    x_ = xT[:, DG * hf + m, :]
                    tt(x_, B[m][:, 0:T], x_, ALU.add).then_inc(S("x_down"), 1)

            for half in range(2):
                base = half * FT

                def down(f, j):
                    slot = (NB_DOWN + base + j) % 2
                    v.wait_ge(*at("w_hi", NB_DOWN + base + f + 1))
                    tt(wlo[:, slot, :], raw[:, (NB_DOWN + base + j) % 4, :], whi[:, slot, :].bitcast(F32),
                       ALU.subtract).then_inc(S("w_lo"), 1)
                    v.wait_ge(*at("a_hi", base + f + 1))
                    tt(alo[:, slot, :], one(act, f), ahi[:, slot, :].bitcast(F32), ALU.subtract)\
                        .then_inc(S("a_lo"), 1)

                down(0, 0)
                if half == 1:
                    add_half(0)
                for j in range(1, 4):
                    down(j, j)
                with v.Fori(1, FT // 4) as i:
                    for j in range(4):
                        down(4 * i + j, j)
                for j in range(FT % 4):
                    down(FT - FT % 4 + j, j)

            add_half(1)
            norm(3, 0, C_FIN, lambda k: fT[:, k, :], "hfin", None)


OUTPUTS = [
    ("y_prompt", (1, NP, D)), ("y_sample", (NB, NL, D)),
    ("p_conv_a", (1, 1, HA, 512)), ("p_s5_re", (1, 1, SG, SP_)), ("p_s5_im", (1, 1, SG, SP_)),
    ("p_conv_c", (1, 1, HC, 1536)), ("p_ssd", (1, 1, NH, HP, NST)), ("p_ffn_conv", (1, 1, 2, FF)),
    ("p_mem_k", (1, 1, NM, XH, XD)), ("p_mem_v", (1, 1, NM, XH, XD)),
    ("s_conv_a", (1, NB, HA, 512)), ("s_s5_re", (1, NB, SG, SP_)), ("s_s5_im", (1, NB, SG, SP_)),
    ("s_conv_c", (1, NB, HC, 1536)), ("s_ssd", (1, NB, NH, HP, NST)), ("s_ffn_conv", (1, NB, 2, FF)),
]


def kernel(**inputs):
    import numpy as np
    import concourse.bacc as bacc
    from concourse.bass_utils import run_bass_kernel_spmd as run

    nc = bacc.Bacc("TRN2", target_bir_lowering=False, num_devices=1)
    arrays, ins, outs = {}, {}, {}
    for name, value in inputs.items():
        value = np.ascontiguousarray(value)
        arrays[f"in_{name}"] = value
        ins[name] = nc.dram_tensor(f"in_{name}", value.shape, mybir.dt.from_np(value.dtype),
                                   kind="ExternalInput").ap()
    for name, shape in OUTPUTS:
        outs[name] = nc.dram_tensor(f"out_{name}", shape, F32, kind="ExternalOutput").ap()
    hymba_step(nc, ins, outs)
    r = run(nc, [arrays], core_ids=[0]).results[0]
    return tuple(r[f"out_{name}"] for name, _ in OUTPUTS)
```

```python
import math
from contextlib import ExitStack

import concourse.bass as bass
from concourse import mybir

F32 = mybir.dt.float32
F32R = mybir.dt.float32r
ALU = mybir.AluOpType
ACT = mybir.ActivationFunctionType
AX = mybir.AxisListType

P = 128
D = 2048
KT = D // P
NP, NB, NL = 256, 8, 4
NS = NB * NL
T = NP + NS
GW = 512
GM = GW // P
SLABS = 8
D_IN = 4112
WA = 31
HA = WA - 1
UP = HA + NP
US = HA + NL
WC, HC = 4, 3
XP = HC + NP
XS = HC + NL
SG, SP_ = 32, 64
SJ = SG * SP_ // P
NH, HP, NST = 16, 64, 128
YT = NH * HP // P
XH, XD = 4, 512
NM = 256
MT = NM // P
FF = 5504
FT = FF // P
EPS = 1e-6
TWO_PI = 2.0 * math.pi
MAGIC = 1.5 * 2.0 ** 23
PI_A = 6.28125
PI_B = 0.00193500518798828125
PI_C = TWO_PI - PI_A - PI_B
GORDER = [2, 0, 1, 5, 6, 7, 3, 4]
GROUP_DT = 8 * GW


SERIES = {
    "act_setup": (("s5_exp", 2), ("s5_sin", 2), ("dt_act", 5), ("s5_bus", 4), ("tap_a", 8), ("s5_gelu", 4),
                  ("mem_sq", 2), ("mem_s", 1), ("memn", 2), ("tap_c", 24), ("compact", 3), ("ex_read", 10),
                  ("memT", 16), ("conv_c", 12)),
    "act_mixers": (("conf_sq", 4), ("conf_s", 1), ("conf_silu", 4), ("cat_a_hi", 4), ("gate_s", 2),
                   ("cat_c_hi", 8), ("qs_hi", 4), ("ps_exp", 1), ("pTs_hi", 4), ("os_hi", 1)),
    "act_sample": (("kc_hi", 64), ("v_hi", 32)),
    "dve_sample": (("kc_lo", 64), ("v_lo", 32)),
    "dve_setup": (("s5_arg", 2), ("theta", 1), ("bc_padded", 4), ("dt_read", 1), ("dt_dve", 3),
                  ("dt_rows", 1), ("u_done", 8), ("conv_a", 4), ("conv_c_taps", 12)),
    "dve_mixers": (("centred", 4), ("conf_read", 1), ("conf_scaled", 4), ("cat_a", 4), ("tok_read", 3),
                   ("gate_read", 2), ("gate_scaled", 8), ("cat_c", 8), ("qs_lo", 4), ("s_kept", 8), ("ps_max", 1),
                   ("ps_norm", 1), ("pTs_lo", 4), ("o_kept", 8), ("os_lo", 1)),
    "dve_norms": (("hmix", 16), ("hxa", 16), ("hffn", 16), ("hfin", 8)),
    "pe_mixers": (("glu_mm", 4), ("ex_mm", 5), ("conf_mm", 2), ("mem_t", 8), ("tok_mm", 1), ("ps_t", 1),
                  ("os_t", 1)),
}
PLACE = {}
for series, kinds in SERIES.items():
    before = 0
    for kind, count in kinds:
        PLACE[kind] = (series, before)
        before += count


class Own:

    def __init__(self, eng, sem):
        self.eng, self.sem, self.n = eng, sem, 0

    def step(self, ins):
        ins.then_inc(self.sem, 1)
        self.n = self.n + 1

    def sync(self):
        self.eng.wait_ge(self.sem, self.n)

    def link(self, ins):
        self.step(ins)
        self.sync()


def hymba_step(nc, I, O):
    ctx = ExitStack()
    sems = {}

    def S(name):
        name = PLACE.get(name, (name, 0))[0]
        if name not in sems:
            sems[name] = ctx.enter_context(nc.semaphore(name))
        return sems[name]

    def at(name, count):
        return S(name), count + PLACE.get(name, (name, 0))[1]

    def alloc(stack, name, shape, dt=F32):
        return stack.enter_context(nc.sbuf_tensor(name, shape, dt))

    with ctx:
        def sb(name, shape, dt=F32):
            return alloc(ctx, name, shape, dt)

        ident = sb("ident", [P, P])
        ones = sb("ones", [P, P])
        negmask = sb("negmask", [P, P])
        negs = sb("negs", [NS, NS])
        bmask = sb("bmask", [P, NB])
        g4 = sb("g4", [P, 4])
        gsel = sb("gsel", [P, 2])
        gneg = sb("gneg", [P, 2])
        segmask = sb("segmask", [NH, T])
        prm = sb("prm", [P, 120 + 104 + 124])
        xT = sb("xT", [P, KT, T])
        ssq = sb("ssq", [P, T])
        sqt = sb("sqt", [P, T])
        rstd = sb("rstd", [P, T])
        hbuf = sb("hbuf", [P, 2, T])
        raw = sb("raw", [P, 4, 1024])
        msum = sb("msum", [P, 6])
        xsum = sb("xsum", [P, 2, 3])
        pairs = sb("pairs", [P, 2])
        gcol_b = sb("gcol_b", [P, 4])

        def col(base):
            return prm[:, base:base + 1]
        C_MIX, C_XA, C_MEM, C_FFN, C_FIN, C_CAB, C_LNW, C_LNB, C_S5D, C_GLB, C_SNW, C_CCB = \
            0, 16, 32, 48, 64, 80, 84, 88, 92, 96, 100, 108
        C_LR, C_LI, C_LDT, C_CCW, C_SSDD = 120, 136, 152, 168, 216
        C_CAW = 224

        lev = ExitStack()
        th = alloc(lev, "th", [P, 4, T])
        alloc(lev, "cat_hi_room", [P, 4, T])
        xbr_a = alloc(lev, "xbr_a", [P, 7, XP + NB * XS])
        alloc(lev, "cat_lo_room", [P, 24 * T - 8 * T - 7 * (XP + NB * XS)])
        xbr_b = alloc(lev, "xbr_b", [P, 5, XP + NB * XS])
        lev.close()
        hhi = sb("hhi", [P, KT, T], F32R)
        hlo = sb("hlo", [P, KT, T], F32R)
        lev = ExitStack()
        xtok = alloc(lev, "xtok", [P, 3, D])
        lev.close()
        lev = ExitStack()
        tabC = alloc(lev, "tabC", [P, SJ, NP])
        tabS = alloc(lev, "tabS", [P, SJ, NP])
        lev.close()
        lev = ExitStack()
        mtok = alloc(lev, "mtok", [P, MT, D])
        glu_w = alloc(lev, "glu_w", [P, 4, 512])
        lev.close()
        lev = ExitStack()
        qs_hi = alloc(lev, "qs_hi", [P, KT, XH, NS], F32R)
        qs_lo = alloc(lev, "qs_lo", [P, KT, XH, NS], F32R)
        lev.close()
        kT = sb("kT", [P, KT, NM])
        lev = ExitStack()
        pTs_hi = alloc(lev, "pTs_hi", [P, MT, XH, XH, NS], F32R)
        pTs_lo = alloc(lev, "pTs_lo", [P, MT, XH, XH, NS], F32R)
        lev.close()
        vtok = sb("vtok", [P, MT, D])
        def fx(r):
            room = kT if r < 8 else vtok
            return room[0:18, :, :].rearrange("p a b -> p (a b)")[:, (r % 8) * 512:(r % 8 + 1) * 512]

        mixers = ExitStack()
        lev = ExitStack()
        hT = alloc(lev, "hT", [P, KT, T])
        lev.close()
        lev = ExitStack()
        memT = alloc(lev, "memT", [P, KT, NM])
        lev.close()
        alloc(mixers, "hT_room", [P, KT, T])
        uT = alloc(mixers, "uT", [P, 4, T])
        zs = alloc(mixers, "zs", [P, YT, T])
        xc = alloc(mixers, "xc", [P, 12, T])
        wdt = alloc(mixers, "wdt", [P, KT, NH])
        dtr = alloc(mixers, "dtr", [NH, 3, T])
        tokT = alloc(mixers, "tokT", [P, 9, NH])
        diag = alloc(mixers, "diag", [NH, NH])
        hcol = alloc(mixers, "hcol", [NH, 4])
        R_DT, R_CS, R_END = [dtr[:, i, :] for i in range(3)]
        R_RAW, R_EXP, R_LN, R_W, R_T = [zs[0:NH, i, :] for i in (3, 4, 5, 6, 7)]
        lev = ExitStack()
        rows = alloc(lev, "rows", [P, 3, P])
        srow = alloc(lev, "srow", [P, 2, P])
        harow = alloc(lev, "harow", [120, 2, 512])
        hcrow = alloc(lev, "hcrow", [NB * HC, 1536])
        brow = alloc(lev, "brow", [P, 2, SJ, 16])
        crow = alloc(lev, "crow", [P, 2, 4, SP_])
        bpad = alloc(lev, "bpad", [P, 2, SJ, 32])
        cpad = alloc(lev, "cpad", [P, 2, 4, 2, SP_])
        lev.close()
        lev = ExitStack()
        va = alloc(lev, "va", [P, 4, T])
        tAB = alloc(lev, "tAB", [P, 2, 2, NP])
        gri = alloc(lev, "gri", [P, 2, 2, NP])
        hAB = alloc(lev, "hAB", [P, 2, 2, NP])
        hri = alloc(lev, "hri", [P, 2, 2, NP])
        hsr = alloc(lev, "hsr", [P, 2, SJ, NS])
        s0s = alloc(lev, "s0s", [P, 2, P])
        bT = alloc(lev, "bT", [P, 2, 4, P])
        cT = alloc(lev, "cT", [P, 2, 4, P])
        up = alloc(lev, "up", [P, 4, UP + NB * US])
        sc = alloc(lev, "sc", [P, 25, SJ])
        fin = alloc(lev, "fin", [P, 2, SJ])
        new_a = hri[:, 0, 0, 0:4 * NS]
        new_c = hri[:, 1, :, :].rearrange("p a b -> p (a b)")[:, 0:12 * NB * HC]
        def exa(r):
            return (tAB, gri, hAB, tAB, hsr)[r][:, :, :, :].rearrange("p i a b -> p i (a b)")
        lev.close()
        lev = ExitStack()
        xdt = alloc(lev, "xdt", [P, 3, NH * HP])
        xds = alloc(lev, "xds", [P, NH * HP])
        btok = alloc(lev, "btok", [P, 3, 2, NST])
        cb = alloc(lev, "cb", [P, 2, 2, P])
        cbs = alloc(lev, "cbs", [NS, 2, NS])
        pvT = alloc(lev, "pvT", [P, NH * HP])
        ecl = alloc(lev, "ecl", [P, NH])
        dec = alloc(lev, "dec", [P, 2, NP])
        decs = alloc(lev, "decs", [NS, 2, NS])
        eb = alloc(lev, "eb", [P, P + NS])
        yo = alloc(lev, "yo", [P, P + NS])
        s0 = alloc(lev, "s0", [P, 2, NB, NST])
        s0T = alloc(lev, "s0T", [P, NB, P])
        bm = alloc(lev, "bm", [NS, NB, NST])
        lev.close()
        mixers.close()

        whi = sb("whi", [P, 2, 1024], F32R)
        wlo = sb("wlo", [P, 2, 1024], F32R)
        lev = ExitStack()
        qT = alloc(lev, "qT", [P, KT, T])
        kv = alloc(lev, "kv", [P, 2, MT, D])
        kc_hi = alloc(lev, "kc_hi", [P, 2, 4, NM], F32R)
        kc_lo = alloc(lev, "kc_lo", [P, 2, 4, NM], F32R)
        pr = alloc(lev, "pr", [P, 2, NM])
        pT = alloc(lev, "pT", [P, 2, MT, P])
        prs = alloc(lev, "prs", [P, NM])
        osum = alloc(lev, "osum", [P, XD])
        sm = alloc(lev, "sm", [P, 9, 4])
        lev.close()
        lev = ExitStack()
        act = alloc(lev, "act", [P, FT, T])
        frow = alloc(lev, "frow", [86, 2, P])
        fprm = alloc(lev, "fprm", [P, 4, FT])
        fhrow = alloc(lev, "fhrow", [16, FF])
        lev.close()
        lev = ExitStack()
        alloc(lev, "act_room", [P, FT, T])
        alloc(lev, "frow_room", [86, 2, P])
        alloc(lev, "fprm_room", [P, 4, FT])
        fh = alloc(lev, "fh", [P, FT, NB, 2])
        gcol = alloc(lev, "gcol", [P, FT, 18])
        cg = alloc(lev, "cg", [P, 4, T])
        spad = alloc(lev, "spad", [P, 4, NB, NL + 2])
        gs = alloc(lev, "gs", [P, 4, T])
        ahi = alloc(lev, "ahi", [P, 2, T], F32R)
        alo = alloc(lev, "alo", [P, 2, T], F32R)
        lev.close()
        lev = ExitStack()
        fT = alloc(lev, "fT", [P, KT, T])
        yst = alloc(lev, "yst", [P, 6, 512])
        lev.close()

        def v_slot(n):
            if n % 4 < 2:
                return [x[:, n % 4, :].rearrange("p (t d) -> p t d", t=MT) for x in (whi, wlo)]
            return [x[:, n % 4 - 2, :, :].rearrange("p (t a) m -> p t (a m)", t=MT) for x in (kc_hi, kc_lo)]

        B = [ctx.enter_context(nc.psum_tensor(f"bank{i}", [P, 512], F32)) for i in range(8)]

        def v3(ap, n):
            return ap.rearrange("p (a b) -> p a b", b=n)

        def vsplit(ap, n):
            return ap.rearrange("p (a b) -> p a b", a=n)

        def up_sample(t):
            return v3(up[:, t, UP:UP + NB * US], US)

        def xb(t):
            return xbr_a[:, t, :] if t < 7 else xbr_b[:, t - 7, :]

        def xbr_sample(t):
            return v3(xb(t)[:, XP:XP + NB * XS], XS)

        NA = 8 * 8
        NKV = 8 * 8
        NS_B = NA + NKV
        G_OUT, G_Q, G_O, G_FF = 0, 4, 8, 12
        FPAIRS = FF // GW
        FTAIL = (FF - FPAIRS * GW) // P
        NG_B = G_FF + 2 * FPAIRS + 2
        NB_DOWN = NG_B * 8
        DG = 8
        SQ_AT = FT - DG

        S5_AT = 15

        GLU_AT, EXPORT_AT, CONF_AT = 50, 56, 61

        TOKENS_AT, STATES_AT, CB_AT, SSD_AT, SSD_HALF, SSD_STEP, GATE_AT = 1, 6, 9, 12, 3, 6, 60
        K_TURN_AT = (10, 17, 29, 35)

        def ssd_at(y, first):
            j, r = divmod(y - first, SSD_STEP)
            return j if r == 0 and 0 <= j < YT else None

        w_in = I["w_in"][0]
        rows_of = lambda w: w.rearrange("(s k p) n -> s p k n", k=2, p=P)

        def slab_src(w, s, c0, width):
            return rows_of(w)[s][:, :, bass.ds(c0, width)] if not isinstance(c0, int) \
                else rows_of(w)[s][:, :, c0:c0 + width]

        def slab_dst(slot, width):
            return raw[:, slot, 0:2 * width].rearrange("p (k n) -> p k n", k=2)

        def wait_raw(eng, fill, slot):
            eng.wait_ge(*at(f"raw_loaded{slot}", 16 * (fill + 1)))

        def wait_used_A(eng, sl):
            if sl < 0:
                return
            if sl < NA:
                g, r = divmod(sl, 8)
                eng.wait_ge(*at("in_slab" if r < 7 else "in_acc", 7 * g + r + 1 if r < 7 else 4 * (g + 1)))
            else:
                g, r = divmod(sl - NA, 8)
                eng.wait_ge(*at("kv_slab" if r < 7 else "kv_acc", 7 * g + r + 1 if r < 7 else 2 * (g + 1)))

        def wait_used_B(eng, g, r):
            if r < 0:
                g, r = g - 1, r + 8
            if isinstance(g, int) and g < 0:
                return
            if r < 7:
                eng.wait_ge(*at("b_slab", 7 * g + (r + 1)))
            elif isinstance(g, int) and g >= NG_B - 2:
                eng.wait_ge(*at("b_acc", 4 * (NG_B - 2) + FTAIL * (g - NG_B + 3)))
            else:
                eng.wait_ge(*at("b_acc", 4 * g + 4))

        def loop(eng, n, body):
            body(0)
            with eng.Fori(1, n) as i:
                body(i)

        STORES = dict(st_kv=16, st_conv_a=2, st_conv_c=6, st_conv_a_old=1, st_s5=4, st_ssd_p=1,
                      st_ssd0=4, st_ssd1=4, st_ffn=4, st_y0=6, st_y1=6)

        block = ctx.enter_context(nc.Block())

        @block.sync
        def _(sp):
            for t in range(2):
                sp.dma_start(xtok[:, t, :], I["x_prompt"][0, t * P:(t + 1) * P, :]).then_inc(S("x_loaded"), 16)
            sp.dma_start(xtok[0:NS, 2, :], I["x_sample"].rearrange("b l d -> (b l) d")).then_inc(S("x_loaded"), 16)
            def first_states():
                with nc.allow_non_contiguous_dma(reason="16 columns of w_in"):
                    sp.dma_start(wdt[:, :, :], w_in.rearrange("(k p) n -> p k n", p=P)[:, :, GROUP_DT:D_IN])\
                      .then_inc(S("wdt_loaded"), 16)
                def hist_load(dst, src):
                    sp.dma_start(dst, src).then_inc(S("hist_loaded"), 16)
                for i, name in enumerate(("state_s5_re", "state_s5_im")):
                    hist_load(srow[:, i, :], I[name][0].rearrange("b (j a) p -> (b j) (a p)", a=2))
                conv_a_rows = I["state_conv_a"][0].rearrange("b r c -> (b r) c")
                for c in range(2):
                    hist_load(harow[:, c, :], conv_a_rows[c * 120:(c + 1) * 120, :])
                hist_load(hcrow[:, :], I["state_conv_c"][0].rearrange("b r c -> (b r) c"))
                for i, name in enumerate(("s5_b_re", "s5_b_im")):
                    hist_load(brow[:, i, :, :], I[name][0].rearrange("(j a) p h -> (a p) j h", a=2))
                for i, name in enumerate(("s5_c_re", "s5_c_im")):
                    hist_load(crow[:, i, :, :], I[name][0].rearrange("g h p -> (g h) p").rearrange("(t q) p -> q t p", q=P))
                sp.dma_start(O["s_conv_a"][0][:, 0:HA - NL, :], I["state_conv_a"][0][:, NL:HA, :])\
                   .then_inc(S("st_conv_a_old"), 16)

            for g, cg_ in enumerate(GORDER):
                for s in range(8):
                    sl = 8 * g + s
                    wait_used_A(sp, sl - 4)
                    sp.dma_start(slab_dst(sl % 4, GW), slab_src(w_in, s, cg_ * GW, GW))\
                      .then_inc(S(f"raw_loaded{sl % 4}"), 16)
                    if sl == 3:
                        first_states()
                    if sl == 42:
                        sp.wait_ge(*at("s5_prod", 2 * SJ))
                        sp.dma_start(glu_w[:, :, :], I["s5_glu_w"][0].rearrange("(k p) n -> p k n", p=P))\
                          .then_inc(S("glu_loaded"), 16)
                    if sl in (44, 46):
                        t = (sl - 44) // 2
                        sp.dma_start(mtok[:, t, :], I["mem_prompt"][0, t * P:(t + 1) * P, :])\
                          .then_inc(S("mem_loaded"), 16)
            for g in range(8):
                w = I["xa_wk"][0] if g < 4 else I["xa_wv"][0]
                for s in range(8):
                    sl = NA + 8 * g + s
                    wait_used_A(sp, sl - 4)
                    sp.dma_start(slab_dst(sl % 4, GW), slab_src(w, s, (g % 4) * GW, GW))\
                      .then_inc(S(f"raw_loaded{sl % 4}"), 16)

            def split_group(w, g, c0, width=GW, between=None):
                for s in range(8):
                    if between:
                        between(s)
                    if isinstance(g, int) and g == 0 and s < 4:
                        wait_used_A(sp, NS_B + s - 4)
                    else:
                        sp.wait_ge(*at("w_lo", 8 * g + (s - 3)))
                    sp.dma_start(slab_dst(s % 4, width), slab_src(w, s, c0, width))\
                      .then_inc(S(f"raw_loaded{s % 4}"), 16)

            def four_groups(w, g0):
                loop(sp, 4, lambda i: split_group(w, g0 + i, i * GW))

            k_rows = I["cache_mem_k"][0].rearrange("b (t p) h d -> b p t (h d)", p=P)
            v_rows = I["cache_mem_v"][0].rearrange("b (t p) h d -> b p t (h d)", p=P)
            four_groups(I["w_out"][0], G_OUT)

            def load_cache(rows_, b, t):
                sp.dma_start(kv[:, b % 2, t, :], rows_[b][:, t, :]).then_inc(S(f"kv_loaded{b % 2}"), 16)

            def early_cache(s):
                if s == 0:
                    sp.wait_ge(*at("cat_c", 8))
                    for i in range(2):
                        sp.wait_ge(*at(f"st_ssd{i}", 16 * 4))
                if s % 2:
                    load_cache(k_rows, s // 4, (s // 2) % 2)
            split_group(I["xa_wq"][0], G_Q, 0, between=early_cache)
            with sp.Fori(1, 4) as i:
                split_group(I["xa_wq"][0], G_Q + i, i * GW)
            for b in range(2, NB):
                sp.wait_ge(*at("kc_t", 8 * (b - 1)))
                for t in range(MT):
                    load_cache(k_rows, b, t)
            for b in range(NB):
                if b < 2:
                    sp.wait_ge(*at("kc_t", 8 * (NB - 1 + b)))
                else:
                    sp.wait_ge(*at("v_lo", XH * (b - 1)))
                for t in range(MT):
                    load_cache(v_rows, b, t)
            four_groups(I["xa_wo"][0], G_O)

            def gate_up(i):
                split_group(I["ffn_w_gate"][0], G_FF + 2 * i, i * GW)
                split_group(I["ffn_w_up"][0], G_FF + 1 + 2 * i, i * GW)
            loop(sp, FPAIRS, gate_up)
            split_group(I["ffn_w_gate"][0], G_FF + 2 * FPAIRS, FPAIRS * GW, FTAIL * P)
            split_group(I["ffn_w_up"][0], G_FF + 1 + 2 * FPAIRS, FPAIRS * GW, FTAIL * P)

            wd = I["ffn_w_down"][0].rearrange("(f p) n -> f p n", p=P)
            for half in range(2):
                c0 = half * DG * P

                def down(f, j):
                    sp.wait_ge(*at("w_lo", NB_DOWN + half * FT + f - 3))
                    slot = (NB_DOWN + half * FT + j) % 4
                    src = wd[f, :, c0:c0 + DG * P] if isinstance(f, int) \
                        else wd[bass.ds(f, 1), :, c0:c0 + DG * P].rearrange("a p n -> p (a n)")
                    sp.dma_start(raw[:, slot, :], src).then_inc(S(f"raw_loaded{slot}"), 16)

                def four(i):
                    for j in range(4):
                        down(4 * i + j, j)
                loop(sp, FT // 4, four)
                for j in range(FT % 4):
                    down(FT - FT % 4 + j, j)
            for n in range(4):
                for t in range(3):
                    w = P if t < 2 else NS
                    if t == 1:
                        sp.wait_ge(*at("y_read_d", n + 1))
                    else:
                        sp.wait_ge(*at("y_read_a", 2 * n + 1 + t // 2))
                    dst = O["y_prompt"][0, t * P:(t + 1) * P, n * 512:(n + 1) * 512] if t < 2 \
                        else O["y_sample"].rearrange("b l d -> (b l) d")[:, n * 512:(n + 1) * 512]
                    sp.dma_start(dst, yst[0:w, 3 * (n % 2) + t, :]).then_inc(S(f"st_y{n % 2}"), 16)
            for name, n in STORES.items():
                sp.wait_ge(*at(name, 16 * n))


        @block.gpsimd
        def _(pool):
            me = Own(pool, S("pool_step"))
            me.step(pool.memset(ident[:, :], 0.0))
            me.step(pool.memset(ones[:, :], 1.0))
            me.step(pool.memset(negmask[:, :], 0.0))
            me.step(pool.memset(negs[:, :], 0.0))
            me.step(pool.memset(bmask[:, :], 1.0))
            me.step(pool.memset(g4[:, :], 1.0))
            me.step(pool.memset(segmask[:, :], 1.0))
            me.sync()
            me.step(pool.affine_select(out=ident[:, :], in_=ident[:, :], compare_op=ALU.not_equal, fill=1.0,
                                       base=0, pattern=[[-1, P]], channel_multiplier=1))
            me.step(pool.affine_select(out=negmask[:, :], in_=negmask[:, :], compare_op=ALU.is_ge, fill=-1e30,
                                       base=0, pattern=[[1, P]], channel_multiplier=-1))
            vneg = v3(negs[:, :], NL)
            me.step(pool.affine_select(out=vneg, in_=vneg, compare_op=ALU.is_ge, fill=-1e30,
                                       base=0, pattern=[[NL, NB], [1, NL]], channel_multiplier=-1))
            me.step(pool.affine_select(out=g4[:, :], in_=g4[:, :], compare_op=ALU.is_ge, fill=0.0,
                                       base=0, pattern=[[-32, 4]], channel_multiplier=1))
            me.step(pool.memset(segmask[:, 0:1], 0.0))
            me.step(pool.memset(segmask[:, P:P + 1], 0.0))
            me.step(pool.memset(segmask[:, NP:T:NL], 0.0))
            me.sync()
            me.step(pool.affine_select(out=vneg, in_=vneg, compare_op=ALU.is_ge, fill=-1e30,
                                       base=0, pattern=[[-NL, NB], [0, NL]], channel_multiplier=1))
            me.step(pool.affine_select(out=g4[:, :], in_=g4[:, :], compare_op=ALU.is_ge, fill=0.0,
                                       base=15, pattern=[[32, 4]], channel_multiplier=-1))
            pool.memset(bpad[:, :, :, :], 0.0).then_inc(S("consts"), 1)
            pool.memset(ssq[:, :], 0.0).then_inc(S("consts"), 1)
            me.sync()
            pool.wait_ge(*at("consts", 2))

            def squares(ready, tiles=KT):
                for k in range(tiles):
                    pool.wait_ge(*at(ready, k + 1))
                    me.link(pool.tensor_tensor(sqt[:, :], xT[:, k, :], xT[:, k, :], ALU.mult))
                    q = pool.tensor_tensor(ssq[:, :], ssq[:, :], sqt[:, :], ALU.add)
                    if k == tiles - 1:
                        q.then_inc(S("ssq_done"), 1)
                    else:
                        me.link(q)

            for h in range(XH):
                rows_h = bmask[NS * h:NS * (h + 1), :]
                me.link(pool.affine_select(out=rows_h, in_=rows_h, compare_op=ALU.is_ge, fill=0.0,
                                           base=0, pattern=[[-NL, NB]], channel_multiplier=1))
                me.link(pool.affine_select(out=rows_h, in_=rows_h, compare_op=ALU.is_ge, fill=0.0,
                                           base=NL - 1, pattern=[[NL, NB]], channel_multiplier=-1))

            for j in range(SJ):
                pool.wait_ge(*at("s5_scanned", j + 1))
                g_ = gri[:, j % 2, :, :]
                if j >= 1:
                    pool.wait_ge(*at("s5_h", 2 * j))
                pool.tensor_tensor(hAB[:, 0, :, :], g_, tabC[:, j, :].unsqueeze(1).to_broadcast([P, 2, NP]),
                                   ALU.mult).then_inc(S("s5_prod"), 1)
                pool.tensor_tensor(hAB[:, 1, :, :], g_, tabS[:, j, :].unsqueeze(1).to_broadcast([P, 2, NP]),
                                   ALU.mult).then_inc(S("s5_prod"), 1)
            pool.wait_ge(*at("s5_hs", 1))
            for i in range(2):
                last = hsr[:, i, :, :].rearrange("p j (b l) -> p b j l", l=NL)[:, :, :, NL - 1]
                pool.tensor_copy(s0s[:, i, :].rearrange("p (b j) -> p b j", j=SJ), last).then_inc(S("s5_fin"), 1)
            me.link(pool.memset(sqt[:, :], 0.0))

            for j in range(YT):
                g = j // 4
                for h in range(2):
                    pool.wait_ge(*at("decay", 4 * j + 2 * h + 1))
                    pool.tensor_tensor(vsplit(dec[:, h, :], 2), vsplit(dec[:, h, :], 2),
                                       cb[:, :, g, :], ALU.mult).then_inc(S("mixed"), 1)
                    pool.wait_ge(*at("decay", 4 * j + 2 * h + 2))
                    pool.tensor_tensor(decs[:, h, :], decs[:, h, :], cbs[:, g, :], ALU.mult)\
                        .then_inc(S("mixed"), 1)
                pool.wait_ge(*at("eb_ready", j + 1))
                pool.wait_ge(*at("s0_T", 2 * j + 2))
                last = eb[:, P:P + NS].rearrange("p (b l) -> p b l", l=NL)[:, :, NL - 1]
                pool.tensor_tensor(s0[:, j % 2, :, :], s0[:, j % 2, :, :],
                                   last.unsqueeze(2).to_broadcast([P, NB, NST]), ALU.mult)\
                    .then_inc(S("s0_decayed"), 1)
            for j in range(YT):
                pool.wait_ge(*at("gated", j + 1))
                dst = ssq if j < 4 else sqt
                me.link(pool.tensor_tensor(hbuf[:, 1, :], zs[:, j, :], zs[:, j, :], ALU.mult))
                q = pool.tensor_tensor(dst[:, :], dst[:, :], hbuf[:, 1, :], ALU.add)
                if j % 4 == 3:
                    q.then_inc(S("gate_sq"), 1)
                    pool.wait_ge(*at("gate_sq", j // 4 + 1))
                else:
                    me.link(q)

            for n, ready in enumerate(("x_out", "x_o", "x_down")):
                if n == 0:
                    pool.wait_ge(*at("gate_mm", 2))
                else:
                    pool.wait_ge(*at("sum_mm", n + 1))
                me.link(pool.memset(ssq[:, :], 0.0))
                if n == 2:
                    def pair(i, mt=GM):
                        for m in range(mt):
                            pool.wait_ge(*at("silu", 4 * i + m + 1))
                            pool.tensor_tensor(cg[:, m, :], cg[:, m, :], rstd[:, :], ALU.mult)\
                                .then_inc(S("gate_n"), 1)
                    loop(pool, FPAIRS, pair)
                    pair(FPAIRS, FTAIL)
                squares(ready, KT if n < 2 else DG)
                if n == 0:
                    pool.wait_ge(*at("scores", 8))
                    for pad in (qs_hi, qs_lo):
                        pool.memset(pad[:, :, :, :].bitcast(F32), 0.0).then_inc(S("pads"), 1)
                    pool.wait_ge(*at("pv", 8))
                    pool.wait_ge(*at("st_kv", 16 * STORES["st_kv"]))
                    for pad in (pTs_hi, pTs_lo):
                        pool.memset(pad[:, :, :, :, :].bitcast(F32), 0.0).then_inc(S("pads"), 1)

            pool.wait_ge(*at("ssq_done", 3))
            for k in range(DG):
                pool.tensor_scalar(xT[:, k, :], xT[:, k, :], col(C_FIN + k), None, ALU.mult).then_inc(S("xw"), 1)

        @block.tensor
        def _(pe):
            def mm(out, l, r, start=True, stop=True):
                return pe.matmul(out, lhsT=l, rhs=r, start=start, stop=stop)

            pe.wait_ge(*at("consts", 1))
            pe.wait_ge(*at("x_loaded", 48))
            for k in range(KT):
                bk = B[4 + k % 3]
                if k >= 3:
                    pe.wait_ge(*at("s0_turned", k - 2))
                for t in range(2):
                    pe.transpose(bk[:, t * P:(t + 1) * P], xtok[:, t, k * P:(k + 1) * P], ident[:, :])
                if k == KT - 1:
                    pe.wait_ge(*at("mix_loaded", 16))
                    pe.transpose(B[0][:, 0:KT], rows[0:KT, 0, :], ident[0:KT, 0:KT])
                pe.transpose(bk[:, NP:T], xtok[0:NS, 2, k * P:(k + 1) * P], ident[0:NS, 0:NS]).then_inc(S("s0_t"), 1)
            pe.wait_ge(*at("norm_r", 2))
            for t in range(3):
                w = P if t < 2 else NS
                q = mm(B[7][:, t * P:t * P + w], xsum[0:w, 1, t:t + 1].to_broadcast([w, P]), ident[0:w, 0:w])
            q.then_inc(S("sum_mm"), 1)

            def in_group(g, hook):
                for s in range(8):
                    sl = 8 * g + s
                    wait_raw(pe, sl // 4, sl % 4)
                    w = slab_dst(sl % 4, GW)
                    for m in range(GM):
                        if s == 0 and g > 0:
                            pe.wait_ge(*at("in_read", 4 * (g - 1) + m + 1))
                        for kk in range(2):
                            if g == 0 and m == 0:
                                pe.wait_ge(*at("hmix", 2 * s + kk + 1))
                            q = mm(B[m][:, 0:T], w[:, kk, m * P:(m + 1) * P], hT[:, 2 * s + kk, :],
                                   s == 0 and kk == 0, s == 7 and kk == 1)
                        if s == 7:
                            q.then_inc(S("in_acc"), 1)
                    if s < 7:
                        q.then_inc(S("in_slab"), 1)
                    hook(8 * g + s)

            def s5_lhs(i, j):
                r = 32 * (j % 4)
                return bT[r:r + 32, i, j // 4, :], r

            def s5_in(j):
                if j >= 2:
                    pe.wait_ge(*at("s5_turned", 2 * (j - 1)))
                else:
                    pe.wait_ge(*at("s5_bus", 4))
                for i in range(2):
                    l, r = s5_lhs(i, j)
                    q = pe.matmul(B[4 + j % 2][:, i * NP:(i + 1) * NP], lhsT=l, rhs=uT[r:r + 32, j // 4, 0:NP],
                                  start=True, stop=True, tile_position=(r, 0))
                q.then_inc(S("s5_in"), 1)

            def s5_out(j):
                jt, r = j // 4, 32 * (j % 4)
                bk = B[6 + jt % 2]
                if j % 4 == 0 and jt >= 2:
                    pe.wait_ge(*at("s5_yd", jt - 1))
                if j == 0:
                    pe.wait_ge(*at("s5_bus", 4))
                    pe.wait_ge(*at("s5_hs", 1))
                for i in range(2):
                    pe.wait_ge(*at("s5_h", 2 * j + i + 1))
                    q = pe.matmul(bk[r:r + 32, 0:NP], lhsT=cT[:, i, jt, r:r + 32], rhs=hri[:, j % 2, i, :],
                                  start=i == 0, stop=i == 1, tile_position=(0, r))
                q.then_inc(S("s5_h_used"), 1)
                for i in range(2):
                    q = pe.matmul(bk[r:r + 32, NP:T], lhsT=cT[:, i, jt, r:r + 32], rhs=hsr[:, i, j, :],
                                  start=i == 0, stop=i == 1, tile_position=(0, r))
                if j % 4 == 3:
                    q.then_inc(S("s5_y"), 1)

            def conf_sum(name, src, bk):
                for t in range(4):
                    pe.wait_ge(*at(name, t + 1))
                    q = mm(B[bk][:, 0:T], ones[:, :], src[:, t, :], t == 0, t == 3)
                q.then_inc(S("conf_mm"), 1)

            def export(r):
                if r == 0:
                    pe.wait_ge(*at("compact", 3))
                    pe.wait_ge(*at("s5_gate", 4))
                else:
                    pe.wait_ge(*at("ex_read", 2 * r))
                if r == 4:
                    pe.wait_ge(*at("s5_fin", 2))
                    for i in range(2):
                        pe.transpose(B[4][0:SJ, i * P:(i + 1) * P], fin[:, i, :], ident[:, :])
                    for i in range(2):
                        q = pe.transpose(B[5][:, i * P:(i + 1) * P], s0s[:, i, :], ident[:, :])
                else:
                    for t in range(4):
                        if r == 0:
                            pe.transpose(B[4][0:HA, t * P:(t + 1) * P], up[:, t, UP - HA:UP], ident[:, :])
                        else:
                            pe.transpose(B[4][0:HC, t * P:(t + 1) * P], xb(4 * (r - 1) + t)[:, XP - HC:XP],
                                         ident[:, :])
                    for t in range(4):
                        if r == 0:
                            q = pe.transpose(B[5][0:NS, t * P:(t + 1) * P], new_a[:, t * NS:(t + 1) * NS],
                                             ident[:, :])
                        else:
                            c0 = (4 * (r - 1) + t) * NB * HC
                            q = pe.transpose(B[5][0:NB * HC, t * P:(t + 1) * P], new_c[:, c0:c0 + NB * HC],
                                             ident[:, :])
                q.then_inc(S("ex_mm"), 1)

            def glu(m):
                if m == 0:
                    pe.wait_ge(*at("glu_loaded", 16))
                bk = B[4 + m % 2]
                if m >= 2:
                    pe.wait_ge(*at("s5_gate", m - 1))
                for k in range(4):
                    if m == 0:
                        pe.wait_ge(*at("s5_gelu", k + 1))
                    q = mm(bk[:, 0:T], glu_w[:, k, m * P:(m + 1) * P], uT[:, k, :], k == 0, k == 3)
                q.then_inc(S("glu_mm"), 1)

            def hook_in(x):
                if x == 1:
                    pe.wait_ge(*at("rows_loaded", 16 * 17))
                    pe.wait_ge(*at("rows_spread", 2))
                    pe.transpose(B[6][:, 0:120], rows[0:120, 0, :], ident[0:120, 0:120])
                    pe.transpose(B[6][:, 120:224], rows[0:104, 1, :], ident[0:104, 0:104])
                    pe.transpose(B[6][:, 224:348], rows[0:124, 2, :], ident[0:124, 0:124]).then_inc(S("s0_t"), 1)
                    pe.wait_ge(*at("wdt_loaded", 16))
                    for k in range(KT):
                        pe.wait_ge(*at("hmix", k + 1))
                        q = mm(B[7][0:NH, 0:T], wdt[:, k, :], hT[:, k, :], k == 0, k == KT - 1)
                    q.then_inc(S("dt_mm"), 1)
                if x == 2:
                    pe.wait_ge(*at("s0_turned", 17))
                    pe.wait_ge(*at("hist_loaded", 16 * 9))
                    for i in range(2):
                        q = pe.transpose(B[4][:, i * P:(i + 1) * P], srow[:, i, :], ident[:, :])
                    q.then_inc(S("s0_t"), 1)
                    for c in range(2):
                        for t in range(4):
                            q = pe.transpose(B[5 + c][:, t * 120:(t + 1) * 120], harow[:, c, t * P:(t + 1) * P],
                                             ident[0:120, 0:120])
                        q.then_inc(S("s0_t"), 1)
                if x == 4:
                    pe.wait_ge(*at("s0_turned", 18))
                    for t in range(12):
                        q = pe.transpose(B[4][:, t * 24:(t + 1) * 24], hcrow[:, t * P:(t + 1) * P],
                                         ident[0:24, 0:24])
                    q.then_inc(S("s0_t"), 1)
                if x == 7:
                    pe.wait_ge(*at("bc_padded", 4))
                    pe.wait_ge(*at("dt_read", 1))
                    pe.wait_ge(*at("s0_turned", 21))
                    for i in range(4):
                        for t in range(4):
                            src = bpad[:, i, 4 * t:4 * t + 4, :].rearrange("p a b -> p (a b)") if i < 2 \
                                else cpad[:, i - 2, t, :, :].rearrange("p a b -> p (a b)")
                            q = pe.transpose(B[4 + i][:, t * P:(t + 1) * P], src, ident[:, :])
                        q.then_inc(S("s0_t"), 1)
                if x == 10:
                    pe.wait_ge(*at("s0_turned", 25))
                    pe.wait_ge(*at("in_read", 4))
                    for r in range(4):
                        for i in range(2):
                            for jt in range(4):
                                l, row = s5_lhs(i, 4 * jt + r)
                                c0 = (4 * i + jt) * NS
                                q = pe.matmul(B[4 + r][:, c0:c0 + NS], lhsT=l, rhs=uT[row:row + 32, jt, NP:T],
                                              start=True, stop=True, tile_position=(row, 0))
                        q.then_inc(S("s5_bus_mm"), 1)
                for j in range(SJ):
                    if x == S5_AT + 5 * j // 4:
                        s5_in(j)
                    if x == S5_AT + 4 + 5 * j // 4:
                        s5_out(j)
                if x in (GLU_AT, GLU_AT + 1):
                    glu(2 * (x - GLU_AT))
                    glu(2 * (x - GLU_AT) + 1)
                if 0 <= x - EXPORT_AT < 5:
                    export(x - EXPORT_AT)
                if x == CONF_AT:
                    conf_sum("conv_a", va, 6)
                if x == CONF_AT + 2:
                    conf_sum("conf_sq", th, 7)

            for g in range(8):
                in_group(g, hook_in)

            for k in range(KT):
                pair = k // 2
                bk = B[(6, 7, 2, 3)[pair % 4]]
                if k == 0:
                    pe.wait_ge(*at("memn", 2))
                    pe.wait_ge(*at("conf_read", 1))
                if k == 4:
                    pe.wait_ge(*at("in_read", 32))
                if k % 2 == 0 and k >= 8:
                    pe.wait_ge(*at("memT", k - 6))
                for t in range(MT):
                    q = pe.transpose(bk[:, (k % 2) * NM + t * P:(k % 2) * NM + (t + 1) * P],
                                     mtok[:, t, k * P:(k + 1) * P], ident[:, :])
                if k % 2:
                    q.then_inc(S("mem_t"), 1)

            def token_columns():
                pe.wait_ge(*at("dt_rows", 1))
                pe.wait_ge(*at("ex_read", 10))
                for q3 in range(3):
                    for c in range(3):
                        w = P if c < 2 else NS
                        q = pe.transpose(B[4][0:w, (q3 * 3 + c) * NH:(q3 * 3 + c + 1) * NH],
                                         dtr[:, q3, c * P:c * P + w], ident[0:NH, 0:NH])
                q = mm(B[4][:, 256:256 + NH], ones[0:NH, :], diag[:, :])
                q.then_inc(S("tok_mm"), 1)

            def token_rows(c):
                w = P if c < 2 else NS
                pe.wait_ge(*at("conv_c", 12))
                for hf in range(2):
                    bk = B[2 + hf]
                    if c == 0:
                        pe.wait_ge(*at("memT", KT))
                    else:
                        pe.wait_ge(*at("xdt", 2 * (c - 1) + hf + 1))
                    for t in range(4):
                        q = pe.transpose(bk[0:w, t * P:(t + 1) * P], xc[:, 4 * hf + t, c * P:c * P + w], ident[:, :])
                    q.then_inc(S("x_t"), 1)
                bk = B[5]
                if c > 0:
                    pe.wait_ge(*at("btok", c))
                for g in range(2):
                    q = pe.transpose(bk[0:w, g * P:(g + 1) * P], xc[:, 8 + g, c * P:c * P + w], ident[:, :])
                q.then_inc(S("b_t"), 1)

            def c_b():
                for c in range(2):
                    for g in range(2):
                        mm(B[6][:, (2 * c + g) * P:(2 * c + g + 1) * P], xc[:, 8 + g, c * P:(c + 1) * P],
                           xc[:, 10 + g, c * P:(c + 1) * P])
                for g in range(2):
                    q = mm(B[7][0:NS, g * NS:(g + 1) * NS], xc[:, 8 + g, NP:T], xc[:, 10 + g, NP:T])
                q.then_inc(S("cb_mm"), 1)

            def chunk_state(c):
                pe.wait_ge(*at("xds", c + 1))
                pe.wait_ge(*at("btok", 3))
                if c == 0:
                    pe.wait_ge(*at("xdt", 6))
                else:
                    pe.wait_ge(*at("st_read", 2))
                for g in range(2):
                    q = mm(B[2 + g][:, :], btok[:, c, g, :], xds[:, g * 512:(g + 1) * 512])
                q.then_inc(S("st_mm"), 1)

            def final_state():
                pe.wait_ge(*at("st_read", 4))
                for j in range(YT):
                    q = pe.transpose(B[2 + j // 4][:, (j % 4) * P:(j % 4 + 1) * P], xds[:, j * P:(j + 1) * P], ident[:, :])
                q.then_inc(S("st_mm"), 1)

            def kv_group(g, hook):
                for s in range(8):
                    sl = NA + 8 * g + s
                    wait_raw(pe, sl // 4, sl % 4)
                    w = slab_dst(sl % 4, GW)
                    for t in range(MT):
                        if s == 0 and g > 0:
                            pe.wait_ge(*at("kv_read", 2 * (g - 1) + t + 1))
                        if s == 0 and g == 0:
                            pe.wait_ge(*at("in_read", 28 + t + 1))
                        for kk in range(2):
                            if g == 0 and t == 0:
                                pe.wait_ge(*at("memT", 2 * s + kk + 1))
                            q = mm(B[t][:, :], memT[:, 2 * s + kk, t * P:(t + 1) * P], w[:, kk, :],
                                   s == 0 and kk == 0, s == 7 and kk == 1)
                        if s == 7:
                            q.then_inc(S("kv_acc"), 1)
                    if s < 7:
                        q.then_inc(S("kv_slab"), 1)
                    hook(8 * g + s)

            def k_turn(g):
                for i in range(2):
                    pe.wait_ge(*at("kv_read", 2 * g + 2))
                    if i == 0:
                        pe.wait_ge(*at("cb_read", 2) if g == 0 else at("upd_read", (2, 6, 8)[g - 1]))
                    for d in range(2):
                        for t in range(MT):
                            c0 = g * GW + (2 * i + d) * P
                            q = pe.transpose(B[6 + i][:, d * NM + t * P:d * NM + (t + 1) * P],
                                             vtok[:, t, c0:c0 + P], ident[:, :])
                    q.then_inc(S("k_t"), 1)

            def head_bcast(h, n=P):
                return ident[0:NH, h:h + 1].to_broadcast([NH, n])

            def ssd_a(j):
                for h in range(2):
                    if j > 0:
                        pe.wait_ge(*at("seg", 6 * (j - 1) + 3 * h + 3))
                    elif h == 0:
                        pe.wait_ge(*at("st_out", 1))
                    mm(B[2 + h][:, 0:T], head_bcast(2 * j + h), R_CS).then_inc(S("abc"), 1)
                if j > 0:
                    pe.wait_ge(*at("yo_read", j))
                else:
                    pe.wait_ge(*at("tok_read", 3))
                for h in range(2):
                    q = pe.matmul(B[4][HP * h:HP * (h + 1), 0:P + NS], lhsT=head_bcast(2 * j + h, HP),
                                  rhs=R_CS[:, P:T], start=True, stop=True, tile_position=(0, HP * h))
                q.then_inc(S("ebc"), 1)
                pe.wait_ge(*at(f"s0_loaded{j % 2}", 16 * (j // 2 + 1)))
                pe.wait_ge(*at("kT_read", (2, 4, 0, 6, 8)[j]) if j < 5 and j != 2 else at("upd_read", 2 * j))
                for b in range(NB):
                    q = pe.transpose(B[6 + b // 4][:, (b % 4) * P:(b % 4 + 1) * P], s0[:, j % 2, b, :], ident[:, :])
                    if b % 4 == 3:
                        q.then_inc(S("s0_t_mm"), 1)

            def ssd_b(j):
                g = j // 4
                if j > 0:
                    pe.wait_ge(*at("gated", j))
                else:
                    pe.wait_ge(*at("btok", 3))
                for h in range(2):
                    hd = 2 * j + h
                    r = HP * h
                    pe.wait_ge(*at("mixed", 4 * j + 2 * h + 2))
                    for c in range(2):
                        pe.matmul(B[5][r:r + HP, c * P:(c + 1) * P], lhsT=xdt[:, c, hd * HP:(hd + 1) * HP],
                                  rhs=dec[:, h, c * P:(c + 1) * P], start=True, stop=True, tile_position=(0, r))
                    q = pe.matmul(B[5][r:r + HP, NP:T], lhsT=xdt[0:NS, 2, hd * HP:(hd + 1) * HP],
                                  rhs=decs[:, h, :], start=True, stop=True, tile_position=(0, r))
                    q.then_inc(S("y_mm"), 1)
                pe.wait_ge(*at("eb_ready", j + 1))
                pe.wait_ge(*at("s0_T", 2 * j + 2))
                mm(B[4][:, 256:256 + P], pvT[:, j * P:(j + 1) * P], xc[:, 10 + g, P:NP])
                for b in range(NB):
                    q = mm(B[4][:, 384 + NL * b:384 + NL * (b + 1)], s0T[:, b, :],
                           xc[:, 10 + g, NP + NL * b:NP + NL * (b + 1)])
                q.then_inc(S("yo_mm"), 1)
                pe.wait_ge(*at("masked_b", g + 1))
                for i in range(2):
                    q = mm(B[6 + i][:, :], xds[0:NS, j * P:(j + 1) * P],
                           bm[:, 4 * i:4 * i + 4, :].rearrange("p b n -> p (b n)"))
                q.then_inc(S("upd_mm"), 1)

            def gate_sums():
                for g in range(2):
                    pe.wait_ge(*at("gate_sq", g + 1))
                    if g == 0:
                        pe.wait_ge(*at("seg", 48))
                    mm(B[2 + g][:, 0:T], ones[:, :], (ssq if g == 0 else sqt)[:, :]).then_inc(S("gate_mm"), 1)

            def hook_kv(y):
                if y == TOKENS_AT:
                    token_columns()
                if TOKENS_AT + 2 <= y < TOKENS_AT + 5:
                    token_rows(y - TOKENS_AT - 2)
                if y in (STATES_AT, STATES_AT + 1):
                    chunk_state(y - STATES_AT)
                if y == STATES_AT + 2:
                    final_state()
                if y == CB_AT:
                    c_b()
                if y in K_TURN_AT:
                    k_turn(K_TURN_AT.index(y))
                j = ssd_at(y, SSD_AT)
                if j is not None:
                    if j == 0:
                        pe.wait_ge(*at("xds", 3))
                    ssd_a(j)
                j = ssd_at(y, SSD_AT + SSD_HALF)
                if j is not None:
                    ssd_b(j)
                if y == GATE_AT:
                    gate_sums()
            for g in range(8):
                kv_group(g, hook_kv)

            def split_mm(out, wslot, wo, xh, xl, first, last):
                pe.matmul(out, lhsT=whi[:, wslot, wo:wo + P], rhs=xh, start=first, stop=False)
                pe.matmul(out, lhsT=whi[:, wslot, wo:wo + P], rhs=xl, start=False, stop=False)
                return pe.matmul(out, lhsT=wlo[:, wslot, wo:wo + P], rhs=xh, start=False, stop=last)

            def split_group(g, bank0, bank_free, ready, width=GW, between=None):
                for s in range(8):
                    pe.wait_ge(*at("w_lo", 8 * g + (s + 1)))
                    for m in range(width // P):
                        if s == 0:
                            bank_free(m)
                        for kk in range(2):
                            if m == 0:
                                ready(2 * s + kk)
                            k = 2 * s + kk
                            q = split_mm(B[bank0 + m][:, 0:T], s % 2, kk * width + m * P, hhi[:, k, :], hlo[:, k, :],
                                         s == 0 and kk == 0, s == 7 and kk == 1)
                        if s == 7:
                            q.then_inc(S("b_acc"), 1)
                    if s < 7:
                        q.then_inc(S("b_slab"), 1)
                    if between:
                        between(s)

            def never(_):
                pass

            def four_groups(g0, before, read, ready, between=None):
                split_group(g0, 0, before, ready, between=between)
                with pe.Fori(1, 3) as i:
                    split_group(g0 + i, 0, lambda m: pe.wait_ge(*at(read, 4 * i + (m - 3))), never)
                split_group(g0 + 3, 4, never, never)

            def mean_square(n):
                def after(s):
                    if s == 4:
                        pe.wait_ge(*at("ssq_done", n))
                        mm(B[4][:, 0:T], ones[:, :], ssq[:, :]).then_inc(S("sum_mm"), 1)
                return after

            def ready_cat(k):
                name, n = ("cat_a", k + 1) if k < 4 else ("cat_b", k - 3) if k < 8 else ("cat_c", k - 7)
                pe.wait_ge(*at(name, n))

            def before_out(m):
                pe.wait_ge(*at("kv_read", 16))
                pe.wait_ge(*at("gate_read", 2))
            four_groups(G_OUT, before_out, "x_out", ready_cat)
            four_groups(G_Q, lambda m: pe.wait_ge(*at("x_out", 9 + m)), "q_read",
                        lambda k: pe.wait_ge(*at("hxa", k + 1)), mean_square(1))

            pe.wait_ge(*at("q_read", 16))
            def scores(n):
                h, l = divmod(n, 2)
                if n >= 2:
                    pe.wait_ge(*at("p_exp", n - 1))
                for d in range(4):
                    q = mm(B[n % 2][:, 0:NM], qT[:, 4 * h + d, l * P:(l + 1) * P], kT[:, 4 * h + d, :],
                           d == 0, d == 3)
                q.then_inc(S("scores"), 1)

            def p_turn(n):
                pe.wait_ge(*at("p_norm", n + 1))
                if n >= 2:
                    pe.wait_ge(*at("pT", n - 1))
                for t in range(MT):
                    q = pe.transpose(B[2 + n % 2][:, t * P:(t + 1) * P], pr[:, n % 2, t * P:(t + 1) * P], ident[:, :])
                q.then_inc(S("p_t"), 1)

            def p_values(n):
                h, l = divmod(n, 2)
                pe.wait_ge(*at("pT", n + 1))
                if n >= 2:
                    pe.wait_ge(*at("o_lo", n - 1))
                for d in range(4):
                    for t in range(MT):
                        c0 = (4 * h + d) * P
                        q = mm(B[4 + n % 2][:, d * P:(d + 1) * P], vtok[:, t, c0:c0 + P], pT[:, n % 2, t, :],
                               t == 0, t == MT - 1)
                q.then_inc(S("pv"), 1)

            def turn_k(u):
                b, h = divmod(u, XH)
                if h == 0:
                    pe.wait_ge(*at(f"kv_loaded{b % 2}", 32 * (b // 2 + 1)))
                if u >= 2:
                    pe.wait_ge(*at("kc_lo", 2 * (u - 1)))
                for i in range(2):
                    for d in range(2):
                        for t in range(MT):
                            c0 = (4 * h + 2 * i + d) * P
                            q = pe.transpose(B[4 + 2 * (u % 2) + i][:, d * NM + t * P:d * NM + (t + 1) * P],
                                             kv[:, b % 2, t, c0:c0 + P], ident[:, :])
                    q.then_inc(S("kc_t"), 1)

            def sample_scores(u):
                b, h = divmod(u, XH)
                pe.wait_ge(*at("kc_lo", 2 * u + 2))
                if h == 0 and b >= 2:
                    pe.wait_ge(*at("s_kept", b - 1))
                for d in range(4):
                    k = 4 * h + d
                    q = padded_mm(B[b % 2][:, 0:NM], (qs_hi[:, k, :, :], qs_lo[:, k, :, :]),
                                  (kc_hi[:, u % 2, d, :], kc_lo[:, u % 2, d, :]), k == 0, k == KT - 1)
                q.then_inc(S("s_scores"), 1)

            def padded_mm(out, left, right, first, last):
                left = [x.rearrange("p h t -> p (h t)") for x in left]
                pe.matmul(out, lhsT=left[0], rhs=right[0], start=first, stop=False)
                pe.matmul(out, lhsT=left[0], rhs=right[1], start=False, stop=False)
                return pe.matmul(out, lhsT=left[1], rhs=right[0], start=False, stop=last)

            scores(0)
            for n in range(8 + 1):
                if n < 7:
                    scores(n + 1)
                if n >= 1:
                    p_values(n - 1)
                if n < 8:
                    p_turn(n)
            pe.wait_ge(*at("p_exp", 8))
            pe.wait_ge(*at("o_lo", 8))
            pe.wait_ge(*at("qs_lo", 4))
            for u in range(NB * XH + 1):
                if u < NB * XH:
                    turn_k(u)
                if u > 0:
                    sample_scores(u - 1)
            pe.wait_ge(*at("ps_norm", 1))
            pe.wait_ge(*at("pT", 8))
            for t in range(MT):
                q = pe.transpose(B[4][:, t * P:(t + 1) * P], prs[:, t * P:(t + 1) * P], ident[:, :])
            q.then_inc(S("ps_t"), 1)
            pe.wait_ge(*at("pTs_lo", 4))
            for b in range(NB):
                for h in range(XH):
                    n = XH * b + h
                    pe.wait_ge(*at("v_lo", n + 1))
                    if h == 0 and b >= 2:
                        pe.wait_ge(*at("o_kept", b - 1))
                    for t in range(MT):
                        q = padded_mm(B[2 + b % 2][:, 0:XD], (pTs_hi[:, t, h, :, :], pTs_lo[:, t, h, :, :]),
                                      [x[:, t, :] for x in v_slot(n)],
                                      h == 0 and t == 0, h == XH - 1 and t == MT - 1)
                    q.then_inc(S("pv_sample"), 1)
            pe.wait_ge(*at("o_kept", NB))
            for d in range(4):
                q = pe.transpose(B[4][:, d * P:(d + 1) * P], osum[:, d * P:(d + 1) * P], ident[:, :])
            q.then_inc(S("os_t"), 1)

            def ready_o(k):
                pe.wait_ge(*at("os_lo", 1))
            def ff_columns(s):
                if s != 4:
                    return
                pe.wait_ge(*at("ff_rows", 16 * 4))
                for i in range(2):
                    q = pe.transpose(B[5][:, i * 86:(i + 1) * 86], frow[:, i, :], ident[0:86, 0:86])
                q.then_inc(S("ff_t"), 1)
                for r in range(2):
                    lo, hi_ = (0, 32) if r == 0 else (32, FT)
                    for t in range(lo, hi_):
                        q = pe.transpose(B[6 + r][:, (t - lo) * 16:(t - lo + 1) * 16], fhrow[:, t * P:(t + 1) * P],
                                         ident[0:16, 0:16])
                    q.then_inc(S("ff_t"), 1)
            four_groups(G_O, never, "x_o", lambda k: ready_o(k) if k == 0 else None, ff_columns)

            def before_up(m):
                pe.wait_ge(*at("ff_cols", 3))
                pe.wait_ge(*at("norm_v", 3))
            split_group(G_FF, 0, lambda m: pe.wait_ge(*at("x_o", 9 + m)), lambda k: pe.wait_ge(*at("hffn", k + 1)),
                        between=mean_square(2))
            split_group(G_FF + 1, 4, before_up, never)
            with pe.Fori(1, FPAIRS) as i:
                split_group(G_FF + 2 * i, 0, lambda m: pe.wait_ge(*at("g_read", 4 * i + (m - 3))), never)
                split_group(G_FF + 1 + 2 * i, 4, lambda m: pe.wait_ge(*at("act", 4 * i + (m - 3))), never)
            split_group(G_FF + 2 * FPAIRS, 0, lambda m: pe.wait_ge(*at("g_read", 4 * FPAIRS + m - 3)), never, FTAIL * P)
            split_group(G_FF + 1 + 2 * FPAIRS, 4, lambda m: pe.wait_ge(*at("act", 4 * FPAIRS + m - 3)), never, FTAIL * P)

            pe.wait_ge(*at("act", FT))
            for r in range(11):
                if r >= 8:
                    pe.wait_ge(*at("fx_read", r - 7))
                for t in range(4 * r, min(4 * r + 4, FT)):
                    q = pe.transpose(B[r % 8][0:18, (t % 4) * P:(t % 4 + 1) * P], gcol[:, t, :], ident[:, :])
                q.then_inc(S("fx_t"), 1)

            pe.wait_ge(*at("fx_read", 11))
            for half in range(2):
                base = half * FT

                def down(f, j, first, last):
                    pe.wait_ge(*at("w_lo", NB_DOWN + base + f + 1))
                    pe.wait_ge(*at("a_lo", base + f + 1))
                    slot = (NB_DOWN + base + j) % 2
                    for m in range(DG):
                        if first and half == 1:
                            pe.wait_ge(*at("x_down", m + 1))
                        q = split_mm(B[m][:, 0:T], slot, m * P, ahi[:, slot, :], alo[:, slot, :], first, last)
                    q.then_inc(S("d_slab"), 1)

                for j in range(4):
                    down(j, j, j == 0, False)
                with pe.Fori(1, FT // 4) as i:
                    for j in range(4):
                        down(4 * i + j, j, False, False)
                for j in range(FT % 4):
                    f = FT - FT % 4 + j
                    down(f, j, False, f == FT - 1)

            pe.wait_ge(*at("ssq_done", 3))
            pe.wait_ge(*at("x_down", DG + 1))
            mm(B[0][:, 0:T], ones[:, :], ssq[:, :], True, False)
            for k in range(DG, KT):
                pe.wait_ge(*at("fin_sq", k - DG + 1))
                q = mm(B[0][:, 0:T], ones[:, :], act[:, SQ_AT + k - DG, :], False, k == KT - 1)
            q.then_inc(S("sum_mm"), 1)
            pe.wait_ge(*at("x_down", KT))
            for k in range(KT):
                if k < DG:
                    pe.wait_ge(*at("xw", k + 1))
                else:
                    pe.wait_ge(*at("hfin", k - DG + 1))
                set_ = (k // 4) % 2
                if k % 4 == 0 and k >= 8:
                    pe.wait_ge(*at("y_read_a", 2 * (k // 4 - 1)))
                    pe.wait_ge(*at("y_read_d", k // 4 - 1))
                for t in range(3):
                    w = P if t < 2 else NS
                    q = pe.transpose(B[1 + 3 * set_ + t][0:w, (k % 4) * P:(k % 4 + 1) * P],
                                     (xT if k < DG else fT)[:, k, t * P:t * P + w], ident[:, :])
                    if k % 4 == 3 and t == 2:
                        q.then_inc(S("y_t"), 1)
                if k == 3:
                    pe.wait_ge(*at("norm_v", 4))
                    for t in range(3):
                        w = P if t < 2 else NS
                        q = mm(B[7][0:w, t:t + 1], rstd[:, t * P:t * P + w], ident[:, 0:1])
                    q.then_inc(S("col_t"), 1)

        @block.scalar
        def _(sc_):
            a = sc_.activation
            me = Own(sc_, S("act_step"))

            def row_load(dst, src):
                sc_.dma_start(dst, src).then_inc(S("rows_loaded"), 16)

            def tiles(ap):
                return ap.rearrange("(k p) -> k p", p=P)
            sc_.dma_start(rows[0:16, 0, :], tiles(I["norm_mix_w"][0])).then_inc(S("mix_loaded"), 16)
            sc_.wait_ge(*at("x_loaded", 48))
            for t in range(3):
                w = P if t < 2 else NS
                a(hT[:, :, :].rearrange("p a b -> p (a b)")[0:w, 0:D], xtok[0:w, t, :], ACT.Square,
                  accum_out=xsum[0:w, 0, t:t + 1]).then_inc(S("x_sq"), 1)
                sc_.wait_ge(*at("x_sq", t + 1))
            sc_.wait_ge(*at("norm_v", 1))
            a(xsum[:, 0, 0:2], xsum[:, 0, 0:2], ACT.Sqrt)
            a(xsum[0:NS, 0, 2:3], xsum[0:NS, 0, 2:3], ACT.Sqrt).then_inc(S("norm_s"), 1)
            for i, name in enumerate(("norm_xa_w", "norm_mem_w", "norm_ffn_w"), 1):
                row_load(rows[16 * i:16 * i + 16, 0, :], tiles(I[name][0]))
            row_load(rows[64:80, 0, :], tiles(I["final_norm_w"]))
            for i, name in enumerate(("conv_a_b", "ln_a_w", "ln_a_b", "s5_d", "s5_glu_b")):
                row_load(rows[80 + 4 * i:84 + 4 * i, 0, :], tiles(I[name][0]))
            row_load(rows[100:108, 0, :], tiles(I["ssd_norm_w"][0]))
            row_load(rows[108:120, 0, :], tiles(I["conv_c_b"][0]))
            row_load(rows[0:16, 1, :], I["s5_lam_re"][0].rearrange("(j a) p -> j (a p)", a=2))
            row_load(rows[16:32, 1, :], I["s5_lam_im"][0].rearrange("(j a) p -> j (a p)", a=2))
            row_load(pairs[32:48, :], I["s5_log_dt"][0].rearrange("(j a) -> j a", a=2))
            row_load(rows[48:96, 1, :], I["conv_c_w"][0].rearrange("w (t p) -> (w t) p", p=P))
            row_load(pairs[96:104, :], I["ssd_d"][0].rearrange("(j a) -> j a", a=2))
            row_load(rows[0:124, 2, :], I["conv_a_w"][0].rearrange("w (t p) -> (w t) p", p=P))
            sc_.dma_start(hcol[:, 0:1], I["ssd_a_log"][0].unsqueeze(1)).then_inc(S("hcol_loaded"), 16)
            sc_.dma_start(hcol[:, 1:2], I["ssd_dt_bias"][0].unsqueeze(1)).then_inc(S("hcol_loaded"), 16)

            sc_.wait_ge(*at("s0_turned", 17))
            a(sc[:, 0, :], prm[:, C_LDT:C_LDT + SJ], ACT.Exp).then_inc(S("s5_exp"), 1)
            sc_.wait_ge(*at("s5_arg", 1))
            a(sc[:, 14, :], sc[:, 1, :], ACT.Exp).then_inc(S("s5_exp"), 1)
            sc_.wait_ge(*at("s5_arg", 2))
            a(sc[:, 6, :], sc[:, 4, :], ACT.Sin, scale=0.5).then_inc(S("s5_sin"), 1)
            a(sc[:, 7, :], sc[:, 5, :], ACT.Sin).then_inc(S("s5_sin"), 1)
            sc_.wait_ge(*at("hcol_loaded", 32))
            a(hcol[:, 2:3], hcol[:, 0:1], ACT.Exp).then_inc(S("dt_act"), 1)
            sc_.wait_ge(*at("dt_dve", 1))
            a(R_EXP, R_EXP, ACT.Exp).then_inc(S("dt_act"), 1)
            sc_.wait_ge(*at("dt_dve", 2))
            a(R_LN, R_W, ACT.Ln).then_inc(S("dt_act"), 1)
            sc_.wait_ge(*at("dt_dve", 3))
            a(R_END, R_END, ACT.Exp).then_inc(S("dt_act"), 1)
            a(hcol[:, 3:4], R_CS[:, NP - 1:NP], ACT.Exp).then_inc(S("dt_act"), 1)

            def in_evac(g):
                for m in range(GM):
                    sc_.wait_ge(*at("in_acc", 4 * g + m + 1))
                    bk = B[m]
                    bs = vsplit(bk[:, NP:T], NB)
                    if g == 0:
                        q = a(uT[:, m, :], bk[:, 0:T], ACT.Copy)
                    elif g == 1:
                        q = a(va[:, m, :], bk[:, 0:T], ACT.Copy, scale=0.5)
                    elif g == 2:
                        q = a(th[:, m, :], bk[:, 0:T], ACT.Tanh, scale=0.5)
                    elif g < 6:
                        t = 4 * (g - 3) + m
                        a(xb(t)[:, HC:XP], bk[:, 0:NP], ACT.Copy)
                        q = a(xbr_sample(t)[:, :, HC:XS], bs, ACT.Copy)
                    else:
                        q = a(zs[:, 4 * (g - 6) + m, :], bk[:, 0:T], ACT.Silu)
                    q.then_inc(S("in_read"), 1)

            in_evac(0)
            for r in range(4):
                sc_.wait_ge(*at("s5_bus_mm", r + 1))
                a(hsr[:, :, :, :].rearrange("p i (a r) n -> p i a r n", r=4)[:, :, :, r, :],
                  B[4 + r][:, 0:8 * NS].rearrange("p (i a n) -> p i a n", i=2, a=4), ACT.Copy)\
                    .then_inc(S("s5_bus"), 1)
            in_evac(1)
            in_evac(2)
            in_evac(3)

            def first_tap(dst, dst_s, src, src_s, w, b, name):
                a(dst, src, ACT.Identity, scale=w, bias=b).then_inc(S(name), 1)
                a(dst_s, src_s, ACT.Identity, scale=w, bias=b).then_inc(S(name), 1)

            for t in range(4):
                sc_.wait_ge(*at("u_done", 2 * t + 2))
                first_tap(va[:, t, 0:NP], vsplit(va[:, t, NP:T], NB), up[:, t, 0:NP], up_sample(t)[:, :, 0:NL],
                          col(C_CAW + t), col(C_CAB + t), "tap_a")
            in_evac(4)
            for t in range(4):
                sc_.wait_ge(*at("s5_yd", t + 1))
                a(uT[:, t, :], uT[:, t, :], ACT.Gelu_apprx_tanh).then_inc(S("s5_gelu"), 1)
            sc_.wait_ge(*at("mem_loaded", 32))
            for t in range(MT):
                a(zs[:, :, :].rearrange("p a b -> p (a b)")[:, 0:D], mtok[:, t, :], ACT.Square,
                  accum_out=msum[:, t:t + 1]).then_inc(S("mem_sq"), 1)
                sc_.wait_ge(*at("mem_sq", t + 1))
            sc_.wait_ge(*at("mem_v", 1))
            a(msum[:, 2:4], msum[:, 2:4], ACT.Sqrt).then_inc(S("mem_s"), 1)
            sc_.wait_ge(*at("mem_v", 2))
            for t in range(MT):
                a(mtok[:, t, :], mtok[:, t, :], ACT.Copy, scale=msum[:, 4 + t:5 + t]).then_inc(S("memn"), 1)
            in_evac(5)
            for t in range(12):
                sc_.wait_ge(*at("in_read", 12 + t + 1))
                sc_.wait_ge(*at("s0_turned", 21))
                first_tap(xc[:, t, 0:NP], vsplit(xc[:, t, NP:T], NB), xb(t)[:, 0:NP], xbr_sample(t)[:, :, 0:NL],
                          col(C_CCW + t), col(C_CCB + t), "tap_c")
            for m in range(4):
                sc_.wait_ge(*at("glu_mm", m + 1))
                if m >= 2:
                    sc_.wait_ge(*at("cat_b", m - 1))
                a(hbuf[:, m % 2, :], B[4 + m % 2][:, 0:T], ACT.Tanh, scale=0.5, bias=gcol_b[:, m:m + 1])\
                    .then_inc(S("s5_gate"), 1)
                if m >= 1:
                    sc_.wait_ge(*at("gated_b", m))
                    a(hhi[:, 3 + m, :], hbuf[:, (m - 1) % 2, :], ACT.Copy, scale=0.5).then_inc(S("cat_b_hi"), 1)
            sc_.wait_ge(*at("gated_b", 4))
            a(hhi[:, 7, :], hbuf[:, 1, :], ACT.Copy, scale=0.5).then_inc(S("cat_b_hi"), 1)
            in_evac(6)
            sc_.wait_ge(*at("s5_h_used", SJ))
            sc_.wait_ge(*at("s5_fin", 2))
            a(new_a.rearrange("p (t b l) -> p t b l", t=4, b=NB),
              up[:, :, UP:UP + NB * US].rearrange("p t (b w) -> p t b w", w=US)[:, :, :, HA:US], ACT.Copy)\
                .then_inc(S("compact"), 1)
            for t0, room in ((0, xbr_a), (7, xbr_b)):
                n_t = 7 if t0 == 0 else 5
                a(new_c.rearrange("p (t b l) -> p t b l", t=12, b=NB)[:, t0:t0 + n_t],
                  room[:, :, XP:XP + NB * XS].rearrange("p t (b w) -> p t b w", w=XS)[:, :, :, XS - HC:XS],
                  ACT.Copy).then_inc(S("compact"), 1)
            for r in range(5):
                n_p, n_s = ((HA, NS), (HC, NB * HC), (HC, NB * HC), (HC, NB * HC), (SJ, P))[r]
                wide = 512 if r < 4 else 2 * P
                sc_.wait_ge(*at("ex_mm", r + 1))
                if r == 3:
                    sc_.wait_ge(*at("st_conv_a", 32))
                a(exa(r)[0:n_p, 0, 0:wide], B[4][0:n_p, 0:wide], ACT.Copy).then_inc(S("ex_read"), 1)
                a(exa(r)[0:n_s, 1, 0:wide], B[5][0:n_s, 0:wide], ACT.Copy).then_inc(S("ex_read"), 1)
                sc_.wait_ge(*at("ex_read", 2 * r + 2))
                if r == 0:
                    sc_.dma_start(O["p_conv_a"][0, 0], exa(r)[0:n_p, 0, :]).then_inc(S("st_conv_a"), 16)
                    sc_.dma_start(O["s_conv_a"][0][:, HA - NL:HA, :], exa(r)[0:n_s, 1, :])\
                       .then_inc(S("st_conv_a"), 16)
                elif r < 4:
                    cs = slice((r - 1) * 512, r * 512)
                    sc_.dma_start(O["p_conv_c"][0, 0][:, cs], exa(r)[0:n_p, 0, :]).then_inc(S("st_conv_c"), 16)
                    sc_.dma_start(O["s_conv_c"][0][:, :, cs], exa(r)[0:n_s, 1, :]).then_inc(S("st_conv_c"), 16)
                else:
                    for i, n_ in enumerate(("re", "im")):
                        sc_.dma_start(O[f"p_s5_{n_}"][0, 0].rearrange("(j a) p -> j (a p)", a=2),
                                      exa(r)[0:SJ, 0, i * P:(i + 1) * P]).then_inc(S("st_s5"), 16)
                        sc_.dma_start(O[f"s_s5_{n_}"][0].rearrange("b (j a) p -> (b j) (a p)", a=2),
                                      exa(r)[:, 1, i * P:(i + 1) * P]).then_inc(S("st_s5"), 16)
            for t in range(4):
                sc_.wait_ge(*at("centred", t + 1))
                a(th[:, t, :], va[:, t, :], ACT.Square).then_inc(S("conf_sq"), 1)
            in_evac(7)
            for k in range(KT):
                sc_.wait_ge(*at("mem_t", k // 2 + 1))
                a(memT[:, k, :], B[(6, 7, 2, 3)[(k // 2) % 4]][:, (k % 2) * NM:(k % 2 + 1) * NM], ACT.Copy,
                  scale=col(C_MEM + k)).then_inc(S("memT"), 1)
            sc_.wait_ge(*at("conf_read", 1))
            a(rstd[:, :], rstd[:, :], ACT.Sqrt).then_inc(S("conf_s"), 1)
            for t in range(4):
                sc_.wait_ge(*at("conf_scaled", t + 1))
                a(va[:, t, :], va[:, t, :], ACT.Silu, bias=col(C_LNB + t)).then_inc(S("conf_silu"), 1)
            for t in range(4):
                sc_.wait_ge(*at("conf_silu", t + 1))
                a(hhi[:, t, :], va[:, t, :], ACT.Copy).then_inc(S("cat_a_hi"), 1)

            for t in range(12):
                sc_.wait_ge(*at("conv_c_taps", t + 1))
                a(xc[:, t, :], xc[:, t, :], ACT.Silu).then_inc(S("conv_c"), 1)

            s0_src = I["state_ssd"][0].rearrange("b (j r) p n -> j (r p) b n", r=2)
            s0_dst = O["s_ssd"][0].rearrange("b (j r) p n -> j (r p) b n", r=2)
            sc_.wait_ge(*at("cat_a", 4))
            sc_.wait_ge(*at("cat_b", 4))
            sc_.wait_ge(*at("st_s5", 64))
            sc_.wait_ge(*at("st_conv_a", 32))
            sc_.wait_ge(*at("st_conv_c", 96))
            for j in range(2):
                sc_.dma_start(s0[:, j, :, :], s0_src[j]).then_inc(S(f"s0_loaded{j}"), 16)
            def split(g, s, width=GW):
                slot = s % 2
                wait_raw(sc_, NS_B // 4 + 2 * g + s // 4, s % 4)
                wait_used_B(sc_, g, s - 2)
                a(whi[:, slot, 0:2 * width], raw[:, s % 4, 0:2 * width], ACT.Copy).then_inc(S("w_hi"), 1)

            def kv_out(g):
                if g == 4:
                    sc_.wait_ge(*at("st_kv", 16 * 8))
                if g >= 4:
                    sc_.wait_ge(*at("k_t", 2 * (g - 4) + 2))
                for t in range(MT):
                    sc_.wait_ge(*at("kv_acc", 2 * g + t + 1))
                    a(vtok[:, t, (g % 4) * GW:(g % 4 + 1) * GW], B[t][:, :], ACT.Copy).then_inc(S("kv_read"), 1)
                for t in range(MT):
                    sc_.wait_ge(*at("kv_read", 2 * g + t + 1))
                    sc_.dma_start((O["p_mem_k"] if g < 4 else O["p_mem_v"])[0, 0][t * P:(t + 1) * P, g % 4, :],
                                  vtok[:, t, (g % 4) * GW:(g % 4 + 1) * GW]).then_inc(S("st_kv"), 16)

            def k_turned(g):
                for i in range(2):
                    sc_.wait_ge(*at("k_t", 2 * g + i + 1))
                    a(kT[:, 4 * g + 2 * i:4 * g + 2 * i + 2, :], v3(B[6 + i][:, :], NM), ACT.Copy)\
                        .then_inc(S("kT_read"), 1)

            def ssd_a(j):
                if 0 < j < YT - 1:
                    sc_.wait_ge(*at(f"st_ssd{(j - 1) % 2}", 16 * ((j - 1) // 2 + 1)))
                    sc_.dma_start(s0[:, (j - 1) % 2, :, :], s0_src[j + 1]).then_inc(S(f"s0_loaded{(j - 1) % 2}"), 16)
                for h in range(2):
                    sc_.wait_ge(*at("seg", 6 * j + 3 * h + 2))
                    a(dec[:, h, :], dec[:, h, :], ACT.Exp).then_inc(S("decay"), 1)
                    sc_.wait_ge(*at("seg", 6 * j + 3 * h + 3))
                    a(decs[:, h, :], decs[:, h, :], ACT.Exp).then_inc(S("decay"), 1)
                sc_.wait_ge(*at("ebc", j + 1))
                if j > 0:
                    sc_.wait_ge(*at("yo_read", j))
                    sc_.wait_ge(*at("s0_decayed", j))
                a(eb[:, :], B[4][:, 0:P + NS], ACT.Exp).then_inc(S("eb_ready"), 1)
                if j == 0:
                    sc_.wait_ge(*at("st_ssd_p", 16))
                for i in range(2):
                    sc_.wait_ge(*at("s0_t_mm", 2 * j + i + 1))
                    if j > 0:
                        sc_.wait_ge(*at("yo_mm", j))
                    a(s0T[:, 4 * i:4 * i + 4, :], v3(B[6 + i][:, :], P), ACT.Copy).then_inc(S("s0_T"), 1)

            def ssd_b(j):
                sc_.wait_ge(*at("upd_read", 2 * j + 2))
                sc_.dma_start(s0_dst[j], s0[:, j % 2, :, :]).then_inc(S(f"st_ssd{j % 2}"), 16)

            for y in range(NKV):
                if y % 8 == 7:
                    kv_out(y // 8)
                if y == STATES_AT + 2:
                    sc_.wait_ge(*at("st_out", 1))
                    sc_.dma_start(O["p_ssd"][0, 0].rearrange("(j r) p n -> (r p) j n", r=2), s0T[:, :, :])\
                       .then_inc(S("st_ssd_p"), 16)
                if y in K_TURN_AT:
                    k_turned(K_TURN_AT.index(y))
                j = ssd_at(y, SSD_AT)
                if j is not None:
                    ssd_a(j)
                j = ssd_at(y, SSD_AT + SSD_HALF)
                if j is not None:
                    ssd_b(j)
                if y == GATE_AT:
                    for g in range(2):
                        sc_.wait_ge(*at("gate_read", g + 1))
                        buf = rstd[:, :] if g == 0 else hbuf[:, 0, :]
                        a(buf, buf, ACT.Sqrt).then_inc(S("gate_s"), 1)
                if y == NKV - 1:
                    split(G_OUT, 0)
                    split(G_OUT, 1)
                if y == NKV - 1:
                    for j in range(YT):
                        sc_.wait_ge(*at("gate_scaled", j + 1))
                        a(hhi[:, 8 + j, :], zs[:, j, :], ACT.Copy).then_inc(S("cat_c_hi"), 1)
                    for i in range(2):
                        sc_.wait_ge(*at(f"st_ssd{i}", 16 * 4))

            def root(n):
                sc_.wait_ge(*at("norm_v", n + 1))
                a(rstd[:, :], rstd[:, :], ACT.Sqrt).then_inc(S("norm_s"), 1)

            def groups_1_to_3(g0, after_slab):
                with sc_.Fori(1, 3) as i:
                    for s in range(8):
                        split(g0 + i, s)
                for s in range(8):
                    split(g0 + 3, s)
                    after_slab(s)

            def h_hi(w_col, x_name, k):
                sc_.wait_ge(*at(x_name, k + 1))
                a(hhi[:, k, :], xT[:, k, :], ACT.Copy, scale=col(w_col + k)).then_inc(S("h_hi"), 1)

            def h_hi_early(w_col, x_name):
                def after_slab(s):
                    if s >= 2:
                        for k in (2 * s - 4, 2 * s - 3):
                            h_hi(w_col, x_name, k)
                return after_slab

            def first_group_after_norm(n, g, w_col, x_name):
                split(g, 0)
                split(g, 1)
                for k in range(12, KT):
                    h_hi(w_col, x_name, k)
                for s in range(2, 8):
                    split(g, s)
                root(n)

            for s in range(2, 8):
                split(G_OUT, s)
            groups_1_to_3(G_OUT, h_hi_early(C_XA, "x_out"))
            first_group_after_norm(1, G_Q, C_XA, "x_out")
            groups_1_to_3(G_Q, lambda s: None)
            SCALE = 1.0 / math.sqrt(XD)
            for n in range(8 + 1):
                if n < 8:
                    sc_.wait_ge(*at("p_max", n + 1))
                    if n >= 2:
                        sc_.wait_ge(*at("p_t", n - 1))
                    a(pr[:, n % 2, :], B[n % 2][:, 0:NM], ACT.Exp, scale=SCALE, bias=sm[:, n, 1:2],
                      accum_out=sm[:, n, 2:3]).then_inc(S("p_exp"), 1)
                if n >= 1:
                    o = n - 1
                    h, l = divmod(o, 2)
                    sc_.wait_ge(*at("p_t", o + 1))
                    if o >= 2:
                        sc_.wait_ge(*at("pv", o - 1))
                    a(pT[:, o % 2, :, :], v3(B[2 + o % 2][:, 0:NM], P), ACT.Copy).then_inc(S("pT"), 1)
                    sc_.wait_ge(*at("pv", o + 1))
                    a(hhi[:, 4 * h:4 * h + 4, l * P:(l + 1) * P], v3(B[4 + o % 2][:, :], P), ACT.Copy)\
                        .then_inc(S("o_hi"), 1)
            sc_.wait_ge(*at("pads", 2))
            for h in range(XH):
                a(qs_hi[:, 4 * h:4 * h + 4, h, :], qT[:, 4 * h:4 * h + 4, NP:T], ACT.Copy).then_inc(S("qs_hi"), 1)
            for u in range(NB * XH):
                for i in range(2):
                    sc_.wait_ge(*at("kc_t", 2 * u + i + 1))
                    if u >= 2:
                        sc_.wait_ge(*at("s_scores", u - 1))
                    a(kc_hi[:, u % 2, 2 * i:2 * i + 2, :], v3(B[4 + 2 * (u % 2) + i][:, :], NM), ACT.Copy)\
                        .then_inc(S("kc_hi"), 1)
            sc_.wait_ge(*at("ps_max", 1))
            a(prs[:, :], prs[:, :], ACT.Exp, scale=SCALE, bias=sm[:, 8, 1:2],
              accum_out=sm[:, 8, 2:3]).then_inc(S("ps_exp"), 1)
            sc_.wait_ge(*at("ps_t", 1))
            sc_.wait_ge(*at("pads", 4))
            for h in range(XH):
                a(pTs_hi[:, :, h, h, :], v3(B[4][:, 0:NM], P)[:, :, NS * h:NS * (h + 1)], ACT.Copy)\
                    .then_inc(S("pTs_hi"), 1)
            for b in range(NB):
                sc_.wait_ge(*at(f"kv_loaded{b % 2}", 32 * ((NB + b) // 2 + 1)))
                for h in range(XH):
                    n = XH * b + h
                    if n >= 4:
                        sc_.wait_ge(*at("pv_sample", n - 3))
                    a(v_slot(n)[0], kv[:, b % 2, :, h * XD:(h + 1) * XD], ACT.Copy)\
                        .then_inc(S("v_hi"), 1)
            sc_.wait_ge(*at("pv_sample", NB * XH))
            split(G_O, 0)
            sc_.wait_ge(*at("os_t", 1))
            a(hhi[:, :, NP:T].rearrange("p (h d) t -> p h d t", d=4),
              B[4][:, :].rearrange("p (d h t) -> p h d t", d=4, h=XH), ACT.Copy).then_inc(S("os_hi"), 1)

            sc_.wait_ge(*at("os_lo", 1))
            cw = I["ffn_conv_w"][0].rearrange("w (t p) -> (w t) p", p=P)
            sc_.dma_start(frow[:, 0, :], cw[0:86, :]).then_inc(S("ff_rows"), 16)
            sc_.dma_start(frow[0:3 * FT - 86, 1, :], cw[86:3 * FT, :]).then_inc(S("ff_rows"), 16)
            sc_.dma_start(frow[3 * FT - 86:86, 1, :], tiles(I["ffn_conv_b"][0])).then_inc(S("ff_rows"), 16)
            sc_.dma_start(fhrow[:, :], I["state_ffn_conv"][0].rearrange("b r c -> (b r) c"))\
               .then_inc(S("ff_rows"), 16)
            for s in range(1, 8):
                split(G_O, s)
            groups_1_to_3(G_O, h_hi_early(C_FFN, "x_o"))

            def one(t, i):
                return t[:, i, :] if isinstance(i, int) else t[:, bass.ds(i, 1), :].rearrange("p a b -> p (a b)")

            def pcol(r, f):
                return fprm[:, r, f:f + 1] if isinstance(f, int) else fprm[:, r, bass.ds(f, 1)]

            def affine(i, m):
                f = 4 * i + m
                sc_.wait_ge(*at("g_read", f + 1))
                if not (isinstance(i, int) and i == 0):
                    sc_.wait_ge(*at("act", f - 3))
                a(cg[:, m, :], gs[:, m, :], ACT.Identity, scale=pcol(2, f), bias=pcol(3, f)).then_inc(S("aff"), 1)
                a(spad[:, m, :, 2:2 + NL], vsplit(gs[:, m, NP:T], NB), ACT.Copy).then_inc(S("aff"), 1)

            def silu(i, m):
                sc_.wait_ge(*at("taps", 4 * i + m + 1))
                a(cg[:, m, :], cg[:, m, :], ACT.Silu).then_inc(S("silu"), 1)

            def pair(i, mt=GM, width=GW):
                g = G_FF + 2 * i
                if isinstance(i, int) and i == 0:
                    first_group_after_norm(2, g, C_FFN, "x_o")
                    sc_.wait_ge(*at("ff_cols", 3))
                else:
                    for s in range(8):
                        split(g, s, width)
                split(g + 1, 0, width)
                split(g + 1, 1, width)
                for m in range(4):
                    if m < mt:
                        affine(i, m)
                    if 0 < m:
                        silu(i, m - 1) if m - 1 < mt else None
                    split(g + 1, 2 + m, width)
                if mt == 4:
                    silu(i, 3)
                split(g + 1, 6, width)
                split(g + 1, 7, width)
            loop(sc_, FPAIRS, pair)
            pair(FPAIRS, FTAIL, FTAIL * P)

            def gate_rows_out():
                for r in range(11):
                    w = P * (min(4 * r + 4, FT) - 4 * r)
                    sc_.wait_ge(*at("fx_t", r + 1))
                    a(fx(r)[:, 0:w], B[r % 8][0:18, 0:w], ACT.Copy).then_inc(S("fx_read"), 1)
                sc_.wait_ge(*at("fx_read", 11))
                for room, f0, nf in ((kT, 0, 4096), (vtok, 4096, FF - 4096)):
                    rows_ = room[:, :, :].rearrange("p a b -> p (a b)")
                    sc_.dma_start(O["p_ffn_conv"][0, 0][:, f0:f0 + nf], rows_[0:2, 0:nf]).then_inc(S("st_ffn"), 16)
                    sc_.dma_start(O["s_ffn_conv"][0].rearrange("b r n -> (b r) n")[:, f0:f0 + nf],
                                  rows_[2:18, 0:nf]).then_inc(S("st_ffn"), 16)

            for half in range(2):
                base = half * FT

                def down(f, j, turn):
                    n = NB_DOWN + base + j
                    slot = n % 2
                    wait_raw(sc_, (NS_B + n) // 4 + turn, n % 4)
                    if half == 0 and isinstance(f, int) and f < 2:
                        wait_used_B(sc_, NG_B - 1, 6 + f)
                    else:
                        sc_.wait_ge(*at("d_slab", base + f - 1))
                    a(whi[:, slot, :], raw[:, n % 4, :], ACT.Copy).then_inc(S("w_hi"), 1)
                    a(ahi[:, slot, :], one(act, f), ACT.Copy).then_inc(S("a_hi"), 1)

                for j in range(4):
                    down(j, j, 0)
                    if half == 0 and j == 1:
                        gate_rows_out()
                with sc_.Fori(1, FT // 4) as i:
                    for j in range(4):
                        down(4 * i + j, j, i)
                for j in range(FT % 4):
                    down(FT - FT % 4 + j, j, FT // 4)

            for k in range(DG, KT):
                sc_.wait_ge(*at("x_down", k + 1))
                a(act[:, SQ_AT + k - DG, :], xT[:, k, :], ACT.Square).then_inc(S("fin_sq"), 1)
            sc_.wait_ge(*at("col_t", 1))
            a(xsum[:, 0, 0:2], B[7][:, 0:2], ACT.Sqrt)
            a(xsum[0:NS, 0, 2:3], B[7][0:NS, 2:3], ACT.Sqrt).then_inc(S("norm_s"), 1)
            sc_.wait_ge(*at("norm_r", 4))
            for n in range(4):
                sc_.wait_ge(*at("y_t", n + 1))
                if n >= 2:
                    sc_.wait_ge(*at(f"st_y{n % 2}", 16 * 3))
                for t in (0, 2):
                    w = P if t < 2 else NS
                    slot = 3 * (n % 2) + t
                    a(yst[0:w, slot, :], B[1 + slot][0:w, :], ACT.Copy, scale=xsum[0:w, 1, t:t + 1])\
                        .then_inc(S("y_read_a"), 1)

        @block.vector
        def _(v):
            me = Own(v, S("dve_step"))

            def turned(n, *copies):
                v.wait_ge(*at("s0_t", n + 1))
                for i, (dst, src) in enumerate(copies):
                    q = v.tensor_copy(dst, src)
                q.then_inc(S("s0_turned"), 1)

            for k in range(KT):
                turned(k, (xT[:, k, :], B[4 + k % 3][:, 0:T]),
                       *([(prm[:, 0:KT], B[0][:, 0:KT])] if k == KT - 1 else []))
                if k == 11:
                    v.wait_ge(*at("x_sq", 3))
                    v.tensor_scalar(xsum[:, 0, 0:2], xsum[:, 0, 0:2], 1.0 / D, EPS, ALU.mult, ALU.add)
                    v.tensor_scalar(xsum[0:NS, 0, 2:3], xsum[0:NS, 0, 2:3], 1.0 / D, EPS, ALU.mult, ALU.add)\
                        .then_inc(S("norm_v"), 1)
                if k == 14:
                    v.wait_ge(*at("norm_s", 1))
                    v.reciprocal(xsum[:, 1, 0:2], xsum[:, 0, 0:2]).then_inc(S("norm_r"), 1)
                    v.reciprocal(xsum[0:NS, 1, 2:3], xsum[0:NS, 0, 2:3]).then_inc(S("norm_r"), 1)
            v.wait_ge(*at("sum_mm", 1))
            me.link(v.tensor_copy(rstd[:, :], B[7][:, 0:T]))
            for k in range(KT):
                v.scalar_tensor_tensor(out=hT[:, k, :], in0=xT[:, k, :], scalar=col(C_MIX + k), in1=rstd[:, :],
                                       op0=ALU.mult, op1=ALU.mult).then_inc(S("hmix"), 1)
            v.wait_ge(*at("rows_loaded", 16 * 17))
            for r in (slice(32, 48), slice(96, 104)):
                v.tensor_copy(rows[r, 1, :].rearrange("j (a p) -> j a p", a=2),
                              pairs[r, :].unsqueeze(2).to_broadcast([r.stop - r.start, 2, 64]))\
                    .then_inc(S("rows_spread"), 1)
            turned(16, (prm[:, KT:348], B[6][:, KT:348]))
            lr, li = prm[:, C_LR:C_LR + SJ], prm[:, C_LI:C_LI + SJ]
            c = lambda i: sc[:, i, :]
            tt, ts, stt = v.tensor_tensor, v.tensor_scalar, v.scalar_tensor_tensor
            v.wait_ge(*at("s5_exp", 1))
            tt(c(1), lr, c(0), ALU.mult).then_inc(S("s5_arg"), 1)
            me.link(tt(c(2), li, c(0), ALU.mult))
            me.link(ts(c(3), c(2), 1.0 / TWO_PI, MAGIC, ALU.mult, ALU.add))
            me.link(ts(c(3), c(3), MAGIC, None, ALU.subtract))
            me.link(stt(c(4), c(3), -PI_A, c(2), ALU.mult, ALU.add))
            me.link(stt(c(4), c(3), -PI_B, c(4), ALU.mult, ALU.add))
            me.link(stt(c(4), c(3), -PI_C, c(4), ALU.mult, ALU.add))
            me.link(stt(c(5), c(4), -1.0, c(4), ALU.mult, ALU.max))
            ts(c(5), c(5), -0.5, math.pi / 2, ALU.mult, ALU.add).then_inc(S("s5_arg"), 1)
            v.wait_ge(*at("s5_sin", 2))
            me.step(tt(c(8), c(6), c(6), ALU.mult))
            me.step(stt(c(9), c(6), 2.0, c(7), ALU.mult, ALU.mult))
            me.sync()
            me.link(ts(c(8), c(8), -2.0, 1.0, ALU.mult, ALU.add))
            me.step(v.tensor_copy(c(16), c(8)))
            me.step(v.tensor_copy(c(17), c(9)))
            me.step(v.memset(tabC[:, :, 0:1], 1.0))
            v.memset(tabS[:, :, 0:1], 0.0).then_inc(S("theta"), 1)
            v.wait_ge(*at("s5_exp", 2))
            me.step(tt(c(12), c(14), c(8), ALU.mult))
            me.step(tt(c(13), c(14), c(9), ALU.mult))
            me.step(tt(c(10), lr, lr, ALU.mult))
            me.step(tt(c(11), li, li, ALU.mult))
            me.sync()
            me.step(tt(c(10), c(10), c(11), ALU.add))
            me.step(ts(c(15), c(12), -1.0, None, ALU.add))
            me.sync()
            me.step(v.reciprocal(c(10), c(10)))
            me.step(tt(c(21), c(15), lr, ALU.mult))
            me.step(tt(c(22), c(13), li, ALU.mult))
            me.step(tt(c(23), c(13), lr, ALU.mult))
            me.step(tt(c(24), c(15), li, ALU.mult))
            me.sync()
            me.step(tt(c(21), c(21), c(22), ALU.add))
            me.step(tt(c(23), c(23), c(24), ALU.subtract))
            me.sync()
            me.step(tt(c(21), c(21), c(10), ALU.mult))
            me.step(tt(c(22), c(23), c(10), ALU.mult))
            me.sync()
            co_r = c(21).unsqueeze(2).to_broadcast([P, SJ, 16])
            co_i = c(22).unsqueeze(2).to_broadcast([P, SJ, 16])
            tmp = [v3(zs[:, i, 0:SJ * 16], 16) for i in range(4)]
            v.wait_ge(*at("hist_loaded", 16 * 9))
            me.step(tt(tmp[0], brow[:, 0, :, :], co_r, ALU.mult))
            me.step(tt(tmp[1], brow[:, 1, :, :], co_i, ALU.mult))
            me.step(tt(tmp[2], brow[:, 1, :, :], co_r, ALU.mult))
            me.step(tt(tmp[3], brow[:, 0, :, :], co_i, ALU.mult))
            me.sync()
            v.wait_ge(*at("consts", 1))
            for i, (x, y, op) in enumerate(((0, 1, ALU.subtract), (2, 3, ALU.add))):
                for g in range(2):
                    r = slice(64 * g, 64 * g + 64)
                    q = tt(bpad[r, i, :, 16 * g:16 * g + 16], tmp[x][r], tmp[y][r], op)
                    if g == 0:
                        me.step(q)
                q.then_inc(S("bc_padded"), 1)
            me.link(v.reduce_sum(gsel[:, 0:1], g4[:, :], axis=AX.X))
            me.link(ts(gsel[:, 1:2], gsel[:, 0:1], -1.0, 1.0, ALU.mult, ALU.add))
            me.link(ts(gneg[:, :], gsel[:, :], -1.0, None, ALU.mult))
            for i in range(2):
                m_ = gsel if i == 0 else gneg
                for g in range(2):
                    q = ts(cpad[:, i, :, g, :], crow[:, i, :, :], m_[:, g:g + 1], None, ALU.mult)
                    if g == 0:
                        me.step(q)
                q.then_inc(S("bc_padded"), 1)
            me.step(ts(gcol_b[:, :], prm[:, C_GLB:C_GLB + 4], 0.5, None, ALU.mult))

            turned(17, (s0s[:, :, :], v3(B[4][:, 0:256], P)))
            me.step(v.memset(up[:, :, 0:HA], 0.0))
            me.step(v.memset(xbr_a[:, :, 0:HC], 0.0))
            me.step(v.memset(xbr_b[:, :, 0:HC], 0.0))
            for half in range(2):
                dsts = []
                for t in range(4):
                    dsts.append((up_sample(t)[:, 4 * half:4 * half + 4, 0:HA],
                                 v3(B[5 + half][:, t * 120:(t + 1) * 120], HA)))
                turned(18 + half, *dsts)

            v.wait_ge(*at("dt_mm", 1))
            v.wait_ge(*at("dt_act", 1))
            ts(R_RAW, B[7][0:NH, 0:T], hcol[:, 1:2], None, ALU.add).then_inc(S("dt_read"), 1)
            v.wait_ge(*at("dt_read", 1))
            me.link(ts(R_DT, R_RAW, 0.0, None, ALU.max))
            stt(R_EXP, R_DT, -2.0, R_RAW, ALU.mult, ALU.add).then_inc(S("dt_dve"), 1)
            v.wait_ge(*at("dt_act", 2))
            ts(R_W, R_EXP, 1.0, None, ALU.add).then_inc(S("dt_dve"), 1)
            v.wait_ge(*at("dt_dve", 2))
            me.link(ts(R_T, R_W, -1.0, None, ALU.add))
            v.wait_ge(*at("dt_act", 3))
            me.link(ts(R_W, R_T, 0.0, None, ALU.is_equal))
            me.link(ts(R_T, R_T, 1e-30, None, ALU.max))
            me.link(v.reciprocal(R_T, R_T))
            v.wait_ge(*at("dt_act", 3))
            me.link(tt(R_T, R_T, R_LN, ALU.mult))
            me.link(tt(R_T, R_T, R_W, ALU.add))
            me.link(tt(R_T, R_T, R_EXP, ALU.mult))
            me.link(tt(R_DT, R_DT, R_T, ALU.add))
            me.link(ts(R_LN, R_DT, hcol[:, 2:3], -1.0, ALU.mult, ALU.mult))
            me.link(v.tensor_tensor_scan(R_CS, segmask[:, :], R_LN, 0.0, ALU.mult, ALU.add))
            for c0, n, w in ((0, 2, P), (NP, NB, NL)):
                seg_ = R_CS[:, c0:c0 + n * w].rearrange("p (a b) -> p a b", b=w)
                q = tt(R_END[:, c0:c0 + n * w].rearrange("p (a b) -> p a b", b=w),
                       seg_[:, :, w - 1:w].to_broadcast([NH, n, w]), seg_, ALU.subtract)
                if n == 2:
                    me.step(q)
            q.then_inc(S("dt_dve"), 1)
            v.wait_ge(*at("dt_act", 5))
            v.tensor_scalar(diag[:, :], ident[0:NH, 0:NH], hcol[:, 3:4], None, ALU.mult).then_inc(S("dt_rows"), 1)

            turned(20, *[(xbr_sample(t)[:, :, 0:HC], v3(B[4][:, t * 24:(t + 1) * 24], HC)) for t in range(12)])

            for i in range(4):
                turned(21 + i, ((bT if i < 2 else cT)[:, i % 2, :, :], v3(B[4 + i][:, :], P)))
            def s5_y(jt):
                v.wait_ge(*at("s5_y", jt + 1))
                stt(uT[:, jt, :], uT[:, jt, :], col(C_S5D + jt), B[6 + jt % 2][:, 0:T], ALU.mult, ALU.add)\
                    .then_inc(S("s5_yd"), 1)

            n = 1
            while n < NP:
                er, ei = sc[:, 16, :], sc[:, 17, :]
                step = min(n, 32)
                for o in range(0, n, step):
                    e_r = er.unsqueeze(2).to_broadcast([P, SJ, step])
                    e_i = ei.unsqueeze(2).to_broadcast([P, SJ, step])
                    c_in, s_in = tabC[:, :, o:o + step], tabS[:, :, o:o + step]
                    t1 = tAB[:, 0, :, :].rearrange("p a b -> p (a b)")[:, 0:SJ * step].rearrange(
                        "p (j t) -> p j t", j=SJ)
                    t2 = tAB[:, 1, :, :].rearrange("p a b -> p (a b)")[:, 0:SJ * step].rearrange(
                        "p (j t) -> p j t", j=SJ)
                    me.step(tt(t1, c_in, e_r, ALU.mult))
                    me.step(tt(t2, s_in, e_i, ALU.mult))
                    me.sync()
                    me.step(tt(tabC[:, :, n + o:n + o + step], t1, t2, ALU.subtract))
                    me.sync()
                    me.step(tt(t1, c_in, e_i, ALU.mult))
                    me.step(tt(t2, s_in, e_r, ALU.mult))
                    me.sync()
                    me.step(tt(tabS[:, :, n + o:n + o + step], t1, t2, ALU.add))
                    me.sync()
                n *= 2
                if n < NP:
                    a, b_, c_ = sc[:, 18, :], sc[:, 19, :], sc[:, 20, :]
                    me.step(tt(a, er, er, ALU.mult))
                    me.step(tt(b_, ei, ei, ALU.mult))
                    me.step(tt(c_, er, ei, ALU.mult))
                    me.sync()
                    me.step(tt(er, a, b_, ALU.subtract))
                    me.step(tt(ei, c_, c_, ALU.add))
                    me.sync()

            v.wait_ge(*at("s5_bus", 4))
            v.wait_ge(*at("s0_turned", 18))
            hr = hsr[:, 0, :, :].rearrange("p j (b l) -> p j b l", l=NL)
            hi = hsr[:, 1, :, :].rearrange("p j (b l) -> p j b l", l=NL)
            a_r = sc[:, 12, :].unsqueeze(2).to_broadcast([P, SJ, NB])
            a_i = sc[:, 13, :].unsqueeze(2).to_broadcast([P, SJ, NB])
            ta = hAB[:, 0, 0, 0:P].rearrange("p (j b) -> p j b", b=NB)
            tb = hAB[:, 0, 1, 0:P].rearrange("p (j b) -> p j b", b=NB)
            tc_ = hAB[:, 1, 0, 0:P].rearrange("p (j b) -> p j b", b=NB)
            td = hAB[:, 1, 1, 0:P].rearrange("p (j b) -> p j b", b=NB)
            for l in range(NL):
                p_r = s0s[:, 0, :].rearrange("p (b j) -> p j b", j=SJ) if l == 0 else hr[:, :, :, l - 1]
                p_i = s0s[:, 1, :].rearrange("p (b j) -> p j b", j=SJ) if l == 0 else hi[:, :, :, l - 1]
                me.step(tt(ta, a_r, p_r, ALU.mult))
                me.step(tt(tb, a_i, p_i, ALU.mult))
                me.step(tt(tc_, a_r, p_i, ALU.mult))
                me.step(tt(td, a_i, p_r, ALU.mult))
                me.sync()
                me.step(tt(ta, ta, tb, ALU.subtract))
                me.step(tt(tc_, tc_, td, ALU.add))
                me.sync()
                me.step(tt(hr[:, :, :, l], hr[:, :, :, l], ta, ALU.add))
                q = tt(hi[:, :, :, l], hi[:, :, :, l], tc_, ALU.add)
                if l < NL - 1:
                    me.step(q)
                    me.sync()
                else:
                    q.then_inc(S("s5_hs"), 1)
                    me.sync()
                    v.wait_ge(*at("s5_hs", 1))

            def s5_turn_back(j):
                v.wait_ge(*at("s5_prod", 2 * j + 2))
                if j >= 2:
                    v.wait_ge(*at("s5_h_used", j - 1))
                if j >= 1:
                    last_state(j - 1)
                tt(hri[:, j % 2, 0, :], hAB[:, 0, 0, :], hAB[:, 1, 1, :], ALU.subtract).then_inc(S("s5_h"), 1)
                tt(hri[:, j % 2, 1, :], hAB[:, 0, 1, :], hAB[:, 1, 0, :], ALU.add).then_inc(S("s5_h"), 1)

            def last_state(j):
                v.wait_ge(*at("s5_h", 2 * j + 2))
                for i in range(2):
                    me.step(v.tensor_copy(fin[:, i, j:j + 1], hri[:, j % 2, i, NP - 1:NP]))

            for j in range(SJ):
                v.wait_ge(*at("s5_in", j + 1))
                ps = v3(B[4 + j % 2][:, :], NP)
                tt(tAB[:, 0, :, :], ps, tabC[:, j, :].unsqueeze(1).to_broadcast([P, 2, NP]), ALU.mult)\
                    .then_inc(S("s5_turned"), 1)
                tt(tAB[:, 1, :, :], ps, tabS[:, j, :].unsqueeze(1).to_broadcast([P, 2, NP]), ALU.mult)\
                    .then_inc(S("s5_turned"), 1)
                v.wait_ge(*at("s5_turned", 2 * j + 2))
                g_ = gri[:, j % 2, :, :]
                if j >= 2:
                    v.wait_ge(*at("s5_prod", 2 * (j - 1)))
                me.step(tt(g_[:, 0, :], tAB[:, 0, 0, :], tAB[:, 1, 1, :], ALU.add))
                me.step(tt(g_[:, 1, :], tAB[:, 0, 1, :], tAB[:, 1, 0, :], ALU.subtract))
                me.sync()
                mag = sc[:, 14, j:j + 1].to_broadcast([P, NP])
                me.step(v.tensor_tensor_scan(g_[:, 0, :], mag, g_[:, 0, :], 0.0, ALU.mult, ALU.add))
                v.tensor_tensor_scan(g_[:, 1, :], mag, g_[:, 1, :], 0.0, ALU.mult, ALU.add)\
                    .then_inc(S("s5_scanned"), 1)
                if j >= 1:
                    s5_turn_back(j - 1)
                if j == 8:
                    s5_y(0)
                if j == 12:
                    s5_y(1)
            s5_turn_back(SJ - 1)
            last_state(SJ - 1)
            me.sync()
            for t in range(4):
                v.wait_ge(*at("in_read", 8 + t + 1))
                stt(up[:, t, HA:UP], th[:, t, 0:NP], 1.0, va[:, t, 0:NP], ALU.add, ALU.mult)\
                    .then_inc(S("u_done"), 1)
                stt(up_sample(t)[:, :, HA:US], vsplit(th[:, t, NP:T], NB), 1.0, vsplit(va[:, t, NP:T], NB),
                    ALU.add, ALU.mult).then_inc(S("u_done"), 1)
            def gate_lo(m):
                v.wait_ge(*at("cat_b_hi", m + 1))
                stt(hlo[:, 4 + m, :], hbuf[:, m % 2, :], 0.5, hhi[:, 4 + m, :].bitcast(F32), ALU.mult, ALU.subtract)\
                    .then_inc(S("cat_b"), 1)

            def s5_gated():
                for m in range(4):
                    v.wait_ge(*at("s5_gate", m + 1))
                    stt(hbuf[:, m % 2, :], hbuf[:, m % 2, :], 1.0, uT[:, m, :], ALU.add, ALU.mult)\
                        .then_inc(S("gated_b"), 1)
                    if m >= 1:
                        gate_lo(m - 1)
                gate_lo(3)

            for t in range(4):
                v.wait_ge(*at("tap_a", 2 * t + 2))
                for w in range(1, WA):
                    wc = col(C_CAW + 4 * w + t)
                    me.step(stt(va[:, t, 0:NP], up[:, t, w:w + NP], wc, va[:, t, 0:NP], ALU.mult, ALU.add))
                    vs = vsplit(va[:, t, NP:T], NB)
                    q = stt(vs, up_sample(t)[:, :, w:w + NL], wc, vs, ALU.mult, ALU.add)
                    if w < WA - 1:
                        me.link(q)
                    else:
                        q.then_inc(S("conv_a"), 1)
                if t == 0:
                    s5_y(2)
                    s5_y(3)
                if t == 1:
                    v.wait_ge(*at("mem_sq", 2))
                    ts(msum[:, 2:4], msum[:, 0:2], 1.0 / D, EPS, ALU.mult, ALU.add).then_inc(S("mem_v"), 1)
                    v.wait_ge(*at("mem_s", 1))
                    v.reciprocal(msum[:, 4:6], msum[:, 2:4]).then_inc(S("mem_v"), 1)
                if t == 2:
                    s5_gated()
            def conv_c(t):
                v.wait_ge(*at("tap_c", 2 * t + 2))
                for w in range(1, WC):
                    wc = col(C_CCW + 12 * w + t)
                    me.step(stt(xc[:, t, 0:NP], xb(t)[:, w:w + NP], wc, xc[:, t, 0:NP], ALU.mult, ALU.add))
                    vs = vsplit(xc[:, t, NP:T], NB)
                    q = stt(vs, xbr_sample(t)[:, :, w:w + NL], wc, vs, ALU.mult, ALU.add)
                    if w < WC - 1:
                        me.link(q)
                    else:
                        q.then_inc(S("conv_c_taps"), 1)

            for t in range(8):
                conv_c(t)
            v.wait_ge(*at("conf_mm", 1))
            for t in range(4):
                stt(va[:, t, :], B[6][:, 0:T], -1.0 / 512, va[:, t, :], ALU.mult, ALU.add).then_inc(S("centred"), 1)
            for t in range(8, 10):
                conv_c(t)
            v.wait_ge(*at("centred", 4))
            v.wait_ge(*at("conf_mm", 2))
            ts(rstd[:, :], B[7][:, 0:T], 1.0 / 512, EPS, ALU.mult, ALU.add).then_inc(S("conf_read"), 1)
            v.wait_ge(*at("conf_s", 1))
            me.link(v.reciprocal(rstd[:, :], rstd[:, :]))
            for t in range(4):
                stt(va[:, t, :], va[:, t, :], col(C_LNW + t), rstd[:, :], ALU.mult, ALU.mult)\
                    .then_inc(S("conf_scaled"), 1)
            for t in range(10, 12):
                conv_c(t)
            for t in range(4):
                v.wait_ge(*at("cat_a_hi", t + 1))
                tt(hlo[:, t, :], va[:, t, :], hhi[:, t, :].bitcast(F32), ALU.subtract).then_inc(S("cat_a"), 1)
            v.wait_ge(*at("cat_a", 4))


            v.wait_ge(*at("st_s5", 64))
            v.wait_ge(*at("st_conv_a", 32))
            v.wait_ge(*at("st_conv_c", 96))
            v.wait_ge(*at("tok_mm", 1))
            src = B[4][:, 0:9 * NH].rearrange("p (q c h) -> p q c h", q=3, c=3)
            dst = tokT[:, :, :].rearrange("p (q c) h -> p q c h", q=3)
            v.tensor_copy(dst[:, :, 0:2, :], src[:, :, 0:2, :]).then_inc(S("tok_read"), 1)
            v.tensor_copy(dst[0:NS, :, 2, :], src[0:NS, :, 2, :]).then_inc(S("tok_read"), 1)
            v.tensor_copy(ecl[:, :], B[4][:, 256:256 + NH]).then_inc(S("tok_read"), 1)
            v.wait_ge(*at("tok_read", 3))

            def per_head(q, c, w, h0=0, n=NH):
                return tokT[0:w, 3 * q + c, h0:h0 + n].unsqueeze(2).to_broadcast([w, n, HP])
            for c in range(3):
                w = P if c < 2 else NS
                for hf in range(2):
                    v.wait_ge(*at("x_t", 2 * c + hf + 1))
                    tt(v3(xdt[0:w, c, hf * 512:(hf + 1) * 512], HP), v3(B[2 + hf][0:w, :], HP),
                       per_head(0, c, w, 8 * hf, 8), ALU.mult).then_inc(S("xdt"), 1)
                v.wait_ge(*at("b_t", c + 1))
                v.tensor_copy(btok[0:w, c, :, :], v3(B[5][0:w, 0:2 * P], P)).then_inc(S("btok"), 1)
            v.wait_ge(*at("xdt", 6))
            tt(v3(xds[:, :], HP), v3(xdt[:, 0, :], HP), per_head(2, 0, P), ALU.mult).then_inc(S("xds"), 1)
            v.wait_ge(*at("st_mm", 1))
            for g in range(2):
                v.tensor_copy(pvT[:, g * 512:(g + 1) * 512], B[2 + g][:, :]).then_inc(S("st_read"), 1)
            tt(v3(xds[:, :], HP), v3(xdt[:, 1, :], HP), per_head(2, 1, P), ALU.mult).then_inc(S("xds"), 1)
            v.wait_ge(*at("st_mm", 2))
            v.wait_ge(*at("st_read", 2))
            me.link(tt(v3(xds[:, :], HP), v3(pvT[:, :], HP), ecl[:, :].unsqueeze(2).to_broadcast([P, NH, HP]),
                       ALU.mult))
            for g in range(2):
                part = xds[:, g * 512:(g + 1) * 512]
                tt(part, B[2 + g][:, :], part, ALU.add).then_inc(S("st_read"), 1)
            v.wait_ge(*at("st_mm", 3))
            me.step(v.tensor_copy(s0T[:, 0:4, :], v3(B[2][:, :], P)))
            v.tensor_copy(s0T[:, 4:8, :], v3(B[3][:, :], P)).then_inc(S("st_out"), 1)
            v.wait_ge(*at("cb_mm", 1))
            v.tensor_copy(cb[:, :, :, :], B[6][:, :].rearrange("p (c g n) -> p c g n", c=2, g=2))\
                .then_inc(S("cb_read"), 1)
            v.tensor_copy(cbs[:, :, :], v3(B[7][0:NS, 0:2 * NS], NS)).then_inc(S("cb_read"), 1)
            v.wait_ge(*at("btok", 3))

            def masked_b(g):
                tt(bm[:, :, :], btok[0:NS, 2, g, :].unsqueeze(1).to_broadcast([NS, NB, NST]),
                   bmask[0:NS, :].unsqueeze(2).to_broadcast([NS, NB, NST]), ALU.mult).then_inc(S("masked_b"), 1)
            masked_b(0)
            tt(v3(xds[0:NS, :], HP), v3(xdt[0:NS, 2, :], HP), per_head(2, 2, NS), ALU.mult).then_inc(S("xds"), 1)

            for j in range(YT):
                for h in range(2):
                    hd = 2 * j + h
                    v.wait_ge(*at("abc", hd + 1))
                    if j > 0:
                        v.wait_ge(*at("y_mm", 2 * (j - 1) + h + 1))
                    for c in range(2):
                        stt(dec[:, h, c * P:(c + 1) * P], B[2 + h][:, c * P:(c + 1) * P],
                            tokT[:, 3 + c, hd:hd + 1], negmask[:, :], ALU.subtract, ALU.add).then_inc(S("seg"), 1)
                    stt(decs[:, h, :], B[2 + h][0:NS, NP:T], tokT[0:NS, 5, hd:hd + 1], negs[:, :],
                        ALU.subtract, ALU.add).then_inc(S("seg"), 1)
                v.wait_ge(*at("yo_mm", j + 1))
                tt(yo[:, :], B[4][:, 256:256 + P + NS], eb[:, :], ALU.mult).then_inc(S("yo_read"), 1)
                me.link(stt(hbuf[:, 0, :], xc[:, j, :], col(C_SSDD + j), B[5][:, 0:T], ALU.mult, ALU.add))
                v.wait_ge(*at("yo_read", j + 1))
                me.link(tt(hbuf[:, 0, P:T], hbuf[:, 0, P:T], yo[:, :], ALU.add))
                tt(zs[:, j, :], zs[:, j, :], hbuf[:, 0, :], ALU.mult).then_inc(S("gated"), 1)
                v.wait_ge(*at("upd_mm", j + 1))
                v.wait_ge(*at("s0_decayed", j + 1))
                for i in range(2):
                    part = s0[:, j % 2, 4 * i:4 * i + 4, :]
                    tt(part, v3(B[6 + i][:, :], NST), part, ALU.add).then_inc(S("upd_read"), 1)
                if j == 3:
                    masked_b(1)
            def split(g, s, width=GW):
                v.wait_ge(*at("w_hi", 8 * g + (s + 1)))
                wsl = slice(0, 2 * width)
                tt(wlo[:, s % 2, wsl], raw[:, s % 4, wsl], whi[:, s % 2, wsl].bitcast(F32), ALU.subtract)\
                    .then_inc(S("w_lo"), 1)

            def one(t, i):
                return t[:, i, :] if isinstance(i, int) else t[:, bass.ds(i, 1), :].rearrange("p a b -> p (a b)")

            def bank_of(i, m):
                return B[m] if not isinstance(i, int) or i < 3 else B[4 + m]

            def x_add(g0, name, i, m):
                v.wait_ge(*at("b_acc", 4 * (g0 + i) + (m + 1)))
                x_ = one(xT, 4 * i + m)
                tt(x_, bank_of(i, m)[:, 0:T], x_, ALU.add).then_inc(S(name), 1)

            def q_scale(i, m):
                v.wait_ge(*at("b_acc", 4 * (G_Q + i) + (m + 1)))
                tt(one(qT, 4 * i + m), bank_of(i, m)[:, 0:T], rstd[:, :], ALU.mult).then_inc(S("q_read"), 1)

            def h_lo(n, w_col, name, k):
                v.wait_ge(*at("h_hi", KT * (n - 1) + k + 1))
                stt(hlo[:, k, :], xT[:, k, :], col(w_col + k), hhi[:, k, :].bitcast(F32), ALU.mult, ALU.subtract)\
                    .then_inc(S(name), 1)

            def groups_1_to_3(g0, evac, after_slab):
                with v.Fori(1, 3) as i:
                    split(g0 + i, 0)
                    for m in range(GM):
                        evac(i - 1, m)
                    for s in range(1, 8):
                        split(g0 + i, s)
                split(g0 + 3, 0)
                for m in range(GM):
                    evac(2, m)
                for s in range(1, 8):
                    split(g0 + 3, s)
                    after_slab(s)

            def h_lo_early(n, w_col, name):
                def after_slab(s):
                    if s >= 2:
                        for k in (2 * s - 4, 2 * s - 3):
                            h_lo(n, w_col, name, k)
                return after_slab

            def first_group_after_norm(n, g, w_col, name, evac):
                split(g, 0)
                split(g, 1)
                for m in range(GM):
                    evac(3, m)
                for m in range(GM):
                    h_lo(n, w_col, name, 12 + m)
                for s in range(2, 7):
                    split(g, s)
                v.wait_ge(*at("sum_mm", n + 1))
                v.tensor_scalar(rstd[:, :], B[4][:, 0:T], 1.0 / D, EPS, ALU.mult, ALU.add)\
                    .then_inc(S("norm_v"), 1)
                split(g, 7)
                v.wait_ge(*at("norm_s", n + 1))
                me.link(v.reciprocal(rstd[:, :], rstd[:, :]))

            for g in range(2):
                v.wait_ge(*at("gate_mm", g + 1))
                if g == 0:
                    v.wait_ge(*at("gated", YT))
                ts(rstd[:, :] if g == 0 else hbuf[:, 0, :], B[2 + g][:, 0:T], 1.0 / 512, EPS, ALU.mult, ALU.add)\
                    .then_inc(S("gate_read"), 1)
            for g in range(2):
                v.wait_ge(*at("gate_s", g + 1))
                buf = rstd[:, :] if g == 0 else hbuf[:, 0, :]
                me.link(v.reciprocal(buf, buf))
            for j in range(YT):
                stt(zs[:, j, :], zs[:, j, :], col(C_SNW + j), rstd[:, :] if j < 4 else hbuf[:, 0, :],
                    ALU.mult, ALU.mult).then_inc(S("gate_scaled"), 1)
            split(G_OUT, 0)
            split(G_OUT, 1)
            for j in range(YT):
                v.wait_ge(*at("cat_c_hi", j + 1))
                q = tt(hlo[:, 8 + j, :], zs[:, j, :], hhi[:, 8 + j, :].bitcast(F32), ALU.subtract)
                q.then_inc(S("cat_c"), 1)
            v.wait_ge(*at("cat_c", 8))
            for s in range(2, 8):
                split(G_OUT, s)

            add_out = lambda i, m: x_add(G_OUT, "x_out", i, m)
            groups_1_to_3(G_OUT, add_out, h_lo_early(1, C_XA, "hxa"))
            first_group_after_norm(1, G_Q, C_XA, "hxa", add_out)
            groups_1_to_3(G_Q, q_scale, lambda s: None)
            for m in range(GM):
                q_scale(3, m)
            SCALE = 1.0 / math.sqrt(XD)

            def row_max(src, n, name):
                me.link(v.reduce_max(sm[:, n, 0:1], src, axis=AX.X))
                ts(sm[:, n, 1:2], sm[:, n, 0:1], -SCALE, None, ALU.mult).then_inc(S(name), 1)

            def normalise(buf, n, name):
                me.link(v.reciprocal(sm[:, n, 3:4], sm[:, n, 2:3]))
                ts(buf, buf, sm[:, n, 3:4], None, ALU.mult).then_inc(S(name), 1)
            for n in range(8 + 1):
                if n < 8:
                    v.wait_ge(*at("scores", n + 1))
                    row_max(B[n % 2][:, 0:NM], n, "p_max")
                    v.wait_ge(*at("p_exp", n + 1))
                    normalise(pr[:, n % 2, :], n, "p_norm")
                if n >= 1:
                    o = n - 1
                    h, l = divmod(o, 2)
                    v.wait_ge(*at("o_hi", o + 1))
                    tt(hlo[:, 4 * h:4 * h + 4, l * P:(l + 1) * P], v3(B[4 + o % 2][:, :], P),
                       hhi[:, 4 * h:4 * h + 4, l * P:(l + 1) * P].bitcast(F32), ALU.subtract).then_inc(S("o_lo"), 1)
            for h in range(XH):
                v.wait_ge(*at("qs_hi", h + 1))
                tt(qs_lo[:, 4 * h:4 * h + 4, h, :], qT[:, 4 * h:4 * h + 4, NP:T],
                   qs_hi[:, 4 * h:4 * h + 4, h, :].bitcast(F32), ALU.subtract).then_inc(S("qs_lo"), 1)

            def keep(b, name, acc, bank, n):
                if b == 0:
                    q = ts(acc, bank[:, 0:n], bmask[:, 0:1], None, ALU.mult)
                else:
                    v.wait_ge(*at(name, b))
                    q = stt(acc, bank[:, 0:n], bmask[:, b:b + 1], acc, ALU.mult, ALU.add)
                q.then_inc(S(name), 1)

            def keep_scores(b):
                v.wait_ge(*at("s_scores", XH * (b + 1)))
                keep(b, "s_kept", prs[:, :], B[b % 2], NM)

            def keep_values(b):
                v.wait_ge(*at("pv_sample", XH * (b + 1)))
                keep(b, "o_kept", osum[:, :], B[2 + b % 2], XD)

            for u in range(NB * XH):
                for i in range(2):
                    v.wait_ge(*at("kc_hi", 2 * u + i + 1))
                    half = slice(2 * i, 2 * i + 2)
                    tt(kc_lo[:, u % 2, half, :], v3(B[4 + 2 * (u % 2) + i][:, :], NM),
                       kc_hi[:, u % 2, half, :].bitcast(F32), ALU.subtract).then_inc(S("kc_lo"), 1)
                if u % XH == 1 and u > 1:
                    keep_scores(u // XH - 1)
            keep_scores(NB - 1)
            v.wait_ge(*at("s_kept", NB))
            row_max(prs[:, :], 8, "ps_max")
            v.wait_ge(*at("ps_exp", 1))
            normalise(prs[:, :], 8, "ps_norm")
            for h in range(XH):
                v.wait_ge(*at("pTs_hi", 4))
                tt(pTs_lo[:, :, h, h, :], v3(B[4][:, 0:NM], P)[:, :, NS * h:NS * (h + 1)],
                   pTs_hi[:, :, h, h, :].bitcast(F32), ALU.subtract).then_inc(S("pTs_lo"), 1)
            for n in range(NB * XH):
                b, h = divmod(n, XH)
                v.wait_ge(*at("v_hi", n + 1))
                v_hi, v_lo = v_slot(n)
                tt(v_lo, kv[:, b % 2, :, h * XD:(h + 1) * XD], v_hi.bitcast(F32), ALU.subtract).then_inc(S("v_lo"), 1)
                if h == 3 and b > 0:
                    keep_values(b - 1)
            keep_values(NB - 1)
            split(G_O, 0)
            v.wait_ge(*at("os_hi", 1))
            tt(hlo[:, :, NP:T].rearrange("p (h d) t -> p h d t", d=4),
               B[4][:, :].rearrange("p (d h t) -> p h d t", d=4, h=XH),
               hhi[:, :, NP:T].bitcast(F32).rearrange("p (h d) t -> p h d t", d=4), ALU.subtract)\
                .then_inc(S("os_lo"), 1)
            for s in range(1, 7):
                split(G_O, s)

            def ffn_columns():
                v.wait_ge(*at("ff_t", 1))
                v.tensor_copy(fprm[:, :, :], v3(B[5][:, 0:4 * FT], FT)).then_inc(S("ff_cols"), 1)
                for r in range(2):
                    lo_, hi_ = (0, 32) if r == 0 else (32, FT)
                    v.wait_ge(*at("ff_t", r + 2))
                    v.tensor_copy(fh[:, lo_:hi_, :, :],
                                  B[6 + r][:, 0:16 * (hi_ - lo_)].rearrange("p (t b r) -> p t b r", b=NB, r=2))\
                        .then_inc(S("ff_cols"), 1)
                v.wait_ge(*at("ff_cols", 3))
            ffn_columns()
            split(G_O, 7)
            add_o = lambda i, m: x_add(G_O, "x_o", i, m)
            groups_1_to_3(G_O, add_o, h_lo_early(2, C_FFN, "hffn"))

            def gate_scale(i, m):
                f = 4 * i + m
                v.wait_ge(*at("b_acc", 4 * G_FF + 8 * i + m + 1))
                tt(gs[:, m, :], B[m][:, 0:T], rstd[:, :], ALU.mult).then_inc(S("g_read"), 1)

            def taps(i, m):
                f = 4 * i + m
                w0, w1 = [fprm[:, r, f:f + 1] if isinstance(f, int) else fprm[:, r, bass.ds(f, 1)] for r in range(2)]
                v.wait_ge(*at("aff", 2 * f + 2))
                hist = fh[:, f, :, :] if isinstance(f, int) \
                    else fh[:, bass.ds(f, 1), :, :].rearrange("p a b r -> p (a b) r")
                v.tensor_copy(spad[:, m, :, 0:2], hist).then_inc(S("tap_step"), 1)
                stt(cg[:, m, 1:NP], gs[:, m, 0:NP - 1], w1, cg[:, m, 1:NP], ALU.mult, ALU.add)\
                    .then_inc(S("tap_step"), 1)
                v.wait_ge(*at("tap_step", 4 * f + 1))
                cs = vsplit(cg[:, m, NP:T], NB)
                stt(cs, spad[:, m, :, 1:1 + NL], w1, cs, ALU.mult, ALU.add).then_inc(S("tap_step"), 1)
                v.wait_ge(*at("tap_step", 4 * f + 2))
                stt(cg[:, m, 2:NP], gs[:, m, 0:NP - 2], w0, cg[:, m, 2:NP], ALU.mult, ALU.add)\
                    .then_inc(S("tap_step"), 1)
                v.wait_ge(*at("tap_step", 4 * f + 3))
                stt(cs, spad[:, m, :, 0:NL], w0, cs, ALU.mult, ALU.add)
                gc = one(gcol, f)
                v.tensor_copy(gc[:, 0:2], gs[:, m, NP - 2:NP])
                v.tensor_copy(v3(gc[:, 2:18], 2), spad[:, m, :, NL:NL + 2]).then_inc(S("taps"), 1)

            def times_up(i, m, tail=False):
                f = 4 * i + m
                v.wait_ge(*at("gate_n", f + 1))
                v.wait_ge(S("b_acc"), 4 * (G_FF + 2 * FPAIRS) + FTAIL + m + 1 if tail
                          else 4 * (G_FF + 1) + 8 * i + (m + 1))
                tt(one(act, f), B[4 + m][:, 0:T], cg[:, m, :], ALU.mult).then_inc(S("act"), 1)

            def pair(i, mt=GM, width=GW):
                g = G_FF + 2 * i
                if isinstance(i, int) and i == 0:
                    first_group_after_norm(2, g, C_FFN, "hffn", add_o)
                else:
                    split(g, 0, width)
                    for m in range(GM):
                        times_up(i - 1, m)
                    for s in range(1, 8):
                        split(g, s, width)
                split(g + 1, 0, width)
                gate_scale(i, 0)
                gate_scale(i, 1)
                split(g + 1, 1, width)
                for m in range(2, mt):
                    gate_scale(i, m)
                for m in range(4):
                    if m < mt:
                        taps(i, m)
                    split(g + 1, 2 + m, width)
                split(g + 1, 6, width)
                split(g + 1, 7, width)
            loop(v, FPAIRS, pair)
            pair(FPAIRS, FTAIL, FTAIL * P)
            for m in range(FTAIL):
                times_up(FPAIRS, m, True)

            def add_half(hf):
                v.wait_ge(*at("d_slab", (hf + 1) * FT))
                for m in range(DG):
                    x_ = xT[:, DG * hf + m, :]
                    tt(x_, B[m][:, 0:T], x_, ALU.add).then_inc(S("x_down"), 1)

            for half in range(2):
                base = half * FT

                def down(f, j):
                    slot = (NB_DOWN + base + j) % 2
                    v.wait_ge(*at("w_hi", NB_DOWN + base + f + 1))
                    tt(wlo[:, slot, :], raw[:, (NB_DOWN + base + j) % 4, :], whi[:, slot, :].bitcast(F32),
                       ALU.subtract).then_inc(S("w_lo"), 1)
                    v.wait_ge(*at("a_hi", base + f + 1))
                    tt(alo[:, slot, :], one(act, f), ahi[:, slot, :].bitcast(F32), ALU.subtract)\
                        .then_inc(S("a_lo"), 1)

                down(0, 0)
                if half == 1:
                    add_half(0)
                for j in range(1, 4):
                    down(j, j)
                with v.Fori(1, FT // 4) as i:
                    for j in range(4):
                        down(4 * i + j, j)
                for j in range(FT % 4):
                    down(FT - FT % 4 + j, j)

            add_half(1)
            v.wait_ge(*at("x_down", KT))
            for k in range(DG, KT):
                ts(fT[:, k, :], xT[:, k, :], col(C_FIN + k), None, ALU.mult).then_inc(S("hfin"), 1)
                if k == DG + 3:
                    v.wait_ge(*at("sum_mm", 4))
                    ts(rstd[:, :], B[0][:, 0:T], 1.0 / D, EPS, ALU.mult, ALU.add).then_inc(S("norm_v"), 1)
            v.wait_ge(*at("norm_s", 4))
            v.reciprocal(xsum[:, 1, 0:2], xsum[:, 0, 0:2]).then_inc(S("norm_r"), 1)
            v.reciprocal(xsum[0:NS, 1, 2:3], xsum[0:NS, 0, 2:3]).then_inc(S("norm_r"), 1)
            v.wait_ge(*at("norm_r", 4))
            for n in range(4):
                slot = 3 * (n % 2) + 1
                v.wait_ge(*at("y_t", n + 1))
                if n >= 2:
                    v.wait_ge(*at(f"st_y{n % 2}", 16 * 3))
                ts(yst[:, slot, :], B[1 + slot][:, :], xsum[:, 1, 1:2], None, ALU.mult).then_inc(S("y_read_d"), 1)


OUTPUTS = [
    ("y_prompt", (1, NP, D)), ("y_sample", (NB, NL, D)),
    ("p_conv_a", (1, 1, HA, 512)), ("p_s5_re", (1, 1, SG, SP_)), ("p_s5_im", (1, 1, SG, SP_)),
    ("p_conv_c", (1, 1, HC, 1536)), ("p_ssd", (1, 1, NH, HP, NST)), ("p_ffn_conv", (1, 1, 2, FF)),
    ("p_mem_k", (1, 1, NM, XH, XD)), ("p_mem_v", (1, 1, NM, XH, XD)),
    ("s_conv_a", (1, NB, HA, 512)), ("s_s5_re", (1, NB, SG, SP_)), ("s_s5_im", (1, NB, SG, SP_)),
    ("s_conv_c", (1, NB, HC, 1536)), ("s_ssd", (1, NB, NH, HP, NST)), ("s_ffn_conv", (1, NB, 2, FF)),
]


def kernel(**inputs):
    import numpy as np
    import concourse.bacc as bacc
    from concourse.bass_utils import run_bass_kernel_spmd as run

    nc = bacc.Bacc("TRN2", target_bir_lowering=False, num_devices=1)
    arrays, ins, outs = {}, {}, {}
    for name, value in inputs.items():
        value = np.ascontiguousarray(value)
        arrays[f"in_{name}"] = value
        ins[name] = nc.dram_tensor(f"in_{name}", value.shape, mybir.dt.from_np(value.dtype),
                                   kind="ExternalInput").ap()
    for name, shape in OUTPUTS:
        outs[name] = nc.dram_tensor(f"out_{name}", shape, F32, kind="ExternalOutput").ap()
    hymba_step(nc, ins, outs)
    r = run(nc, [arrays], core_ids=[0]).results[0]
    return tuple(r[f"out_{name}"] for name, _ in OUTPUTS)
```
